# Optimizing a Trainium2 kernel written in Bass

```python
import math
import jax
import jax.numpy as jnp
from jax import lax
import numpy as np

D_MODEL = 1024
BATCH = 1
SEQ = 256
DEPTH = 2
DEC_BATCH = 8
DEC_SEQ = 4
PAST_LEN = 256
PAGE_SIZE = 128

POOL_WIDTH = D_MODEL // 4
POOL_WINDOWS = (2, 4, 8, 16)
POOL_GROUPS = len(POOL_WINDOWS)
POOL_GROUP_WIDTH = POOL_WIDTH // POOL_GROUPS
POOL_BUF = max(POOL_WINDOWS) - 1

CONV_WIDTH = D_MODEL // 4
CONV_K = 31
CONV_BUF = CONV_K - 1

ATT_HEADS = 4
ATT_HEAD_DIM = D_MODEL // 8
ATT_WIDTH = ATT_HEADS * ATT_HEAD_DIM
ROT_DIM = ATT_HEAD_DIM // 4
ROPE_THETA = 500000.0
MOBA_BLOCK = 256
MOBA_TOPK = 3
MOBA_QUERY_ROWS = 128

MIX_WIDTH = POOL_WIDTH + CONV_WIDTH + ATT_WIDTH
IN_WIDTH = POOL_WIDTH + 2 * CONV_WIDTH + 3 * ATT_WIDTH

N_MEM = 256
MEM_HEADS = 4
MEM_HEAD_DIM = D_MODEL // MEM_HEADS

D_FF = ((8 * D_MODEL // 3 + 127) // 128) * 128
EPS = 1e-6

kernel_name = 'hybrid_pool_conv_moba_decoder_step'

def rms_norm(x, g):
    xf = x.astype(jnp.float32)
    y = xf * lax.rsqrt(jnp.mean(xf * xf, axis=-1, keepdims=True) + EPS)
    return (y * g.astype(jnp.float32)).astype(x.dtype)

def layer_norm(x, g, b):
    xf = x.astype(jnp.float32)
    xc = xf - jnp.mean(xf, axis=-1, keepdims=True)
    y = xc * lax.rsqrt(jnp.mean(xc * xc, axis=-1, keepdims=True) + EPS)
    return (y * g.astype(jnp.float32) + b.astype(jnp.float32)).astype(x.dtype)

def swiglu_ffn(x, w_in, w_out):
    gate, up = jnp.split(x @ w_in, 2, axis=-1)
    return (jax.nn.silu(gate) * up) @ w_out

def partial_rope(x, pos):
    half = ROT_DIM // 2
    inv_freq = jnp.power(jnp.float32(ROPE_THETA), -jnp.arange(half, dtype=jnp.float32) / half)
    ang = pos.astype(jnp.float32)[:, None] * inv_freq[None, :]
    cos = jnp.cos(ang)[None, :, None, :]
    sin = jnp.sin(ang)[None, :, None, :]
    xf = x.astype(jnp.float32)
    x1 = xf[..., :half]
    x2 = xf[..., half:ROT_DIM]
    out = jnp.concatenate([x1 * cos - x2 * sin, x2 * cos + x1 * sin, xf[..., ROT_DIM:]], axis=-1)
    return out.astype(x.dtype)

def pool_mix(u, buf, pos0, w, scale):
    bsz, t, _ = u.shape
    ext = jnp.concatenate([buf, u], axis=1).astype(jnp.float32)
    csum = jnp.concatenate([jnp.zeros_like(ext[:, :1]), jnp.cumsum(ext, axis=1)], axis=1)
    upto = csum[:, POOL_BUF + 1:]
    pos = pos0 + jnp.arange(t, dtype=jnp.int32)
    diffs = []
    for g, win in enumerate(POOL_WINDOWS):
        ch = slice(g * POOL_GROUP_WIDTH, (g + 1) * POOL_GROUP_WIDTH)
        before = csum[:, POOL_BUF + 1 - win:POOL_BUF + 1 - win + t, ch]
        count = jnp.minimum(pos + 1, win).astype(jnp.float32)[None, :, None]
        diffs.append((upto[..., ch] - before) / count - ext[:, POOL_BUF:, ch])
    d = jnp.stack(diffs, axis=2)
    y = jnp.einsum('btgc,gcd->btgd', d, w.astype(jnp.float32)).reshape(bsz, t, POOL_WIDTH)
    y = y * scale.astype(jnp.float32)
    return y.astype(u.dtype), ext[:, -POOL_BUF:].astype(u.dtype)

def conv_mix(a, gate, buf, dw_w, dw_b, ln_g, ln_b, pw_w, pw_b):
    h = a * jax.nn.sigmoid(gate)
    ext = jnp.concatenate([buf, h], axis=1)
    y = lax.conv_general_dilated(ext, dw_w[:, None, :], window_strides=(1,), padding='VALID',
                                 dimension_numbers=('NWC', 'WIO', 'NWC'),
                                 feature_group_count=CONV_WIDTH) + dw_b
    y = jax.nn.silu(layer_norm(y, ln_g, ln_b))
    return y @ pw_w + pw_b, ext[:, -CONV_BUF:]

def moba_attend(q, k_all, v_all, q_pos0):
    bsz, tq, nh, dh = q.shape
    klen = k_all.shape[1]
    nb = -(-klen // MOBA_BLOCK)
    pad = nb * MOBA_BLOCK - klen
    kb = jnp.pad(k_all, ((0, 0), (0, pad), (0, 0), (0, 0))).reshape(bsz, nb, MOBA_BLOCK, nh, dh).transpose(0, 3, 1, 2, 4)
    vb = jnp.pad(v_all, ((0, 0), (0, pad), (0, 0), (0, 0))).reshape(bsz, nb, MOBA_BLOCK, nh, dh).transpose(0, 3, 1, 2, 4)
    kmean = jnp.mean(kb.astype(jnp.float32), axis=3)
    topk = min(MOBA_TOPK, nb)
    cap = max(1, MOBA_QUERY_ROWS // bsz)
    qc = max(c for c in range(1, min(cap, tq) + 1) if tq % c == 0)
    nchunk = tq // qc
    qh = q.transpose(0, 2, 1, 3).reshape(bsz, nh, nchunk, qc, dh).transpose(2, 0, 1, 3, 4)
    qpos = (q_pos0 + jnp.arange(tq, dtype=jnp.int32)).reshape(nchunk, qc)
    blk_ids = jnp.arange(nb, dtype=jnp.int32)
    key_off = jnp.arange(MOBA_BLOCK, dtype=jnp.int32)
    b_idx = jnp.arange(bsz)[:, None, None, None]
    h_idx = jnp.arange(nh)[None, :, None, None]
    scale = dh ** -0.5

    def one_chunk(args):
        qx, p = args
        own = p // MOBA_BLOCK
        qf = qx.astype(jnp.float32)
        gate = jnp.einsum('bhqd,bhnd->bhqn', qf, kmean)
        gate = jnp.where(blk_ids[None, :] < own[:, None], gate, -jnp.inf)
        _, top = lax.top_k(gate, topk)
        top_ok = top < own[:, None]
        sel = jnp.concatenate([top, jnp.broadcast_to(own[:, None], (bsz, nh, qc, 1))], axis=-1)
        ok = jnp.concatenate([top_ok, jnp.ones((bsz, nh, qc, 1), dtype=bool)], axis=-1)
        kg = kb[b_idx, h_idx, sel]
        vg = vb[b_idx, h_idx, sel]
        s = jnp.einsum('bhqd,bhqsjd->bhqsj', qf, kg.astype(jnp.float32)) * scale
        kpos = sel[..., None] * MOBA_BLOCK + key_off
        mask = ok[..., None] & (kpos <= p[:, None, None])
        s = jnp.where(mask, s, -jnp.inf)
        pr = jax.nn.softmax(s.reshape(bsz, nh, qc, -1), axis=-1).reshape(s.shape)
        o = jnp.einsum('bhqsj,bhqsjd->bhqd', pr, vg.astype(jnp.float32))
        return o.astype(q.dtype)

    out = lax.map(one_chunk, (qh, qpos))
    return out.transpose(1, 0, 3, 2, 4).reshape(bsz, tq, nh, dh)

def mixer_groups(h, pos0, pool_buf, conv_buf, past_k, past_v, p):
    bsz, t, _ = h.shape
    z = h @ p['w_in']
    c1 = POOL_WIDTH
    c2 = c1 + CONV_WIDTH
    c3 = c2 + CONV_WIDTH
    c4 = c3 + ATT_WIDTH
    c5 = c4 + ATT_WIDTH
    y_pool, new_pool = pool_mix(z[..., :c1], pool_buf, pos0, p['pool_w'], p['pool_scale'])
    y_conv, new_conv = conv_mix(z[..., c1:c2], z[..., c2:c3], conv_buf, p['conv_dw_w'], p['conv_dw_b'],
                                p['conv_ln_g'], p['conv_ln_b'], p['conv_pw_w'], p['conv_pw_b'])
    pos = pos0 + jnp.arange(t, dtype=jnp.int32)
    q = partial_rope(rms_norm(z[..., c3:c4].reshape(bsz, t, ATT_HEADS, ATT_HEAD_DIM), p['att_q_norm']), pos)
    k = partial_rope(rms_norm(z[..., c4:c5].reshape(bsz, t, ATT_HEADS, ATT_HEAD_DIM), p['att_k_norm']), pos)
    v = z[..., c5:].reshape(bsz, t, ATT_HEADS, ATT_HEAD_DIM)
    if past_k is None:
        k_all, v_all = k, v
    else:
        k_all = jnp.concatenate([past_k, k], axis=1)
        v_all = jnp.concatenate([past_v, v], axis=1)
    y_att = moba_attend(q, k_all, v_all, pos0).reshape(bsz, t, ATT_WIDTH)
    y = jnp.concatenate([y_pool, y_conv, y_att], axis=-1) @ p['w_out']
    return y, new_pool, new_conv, k, v

def memory_kv(mem, p):
    bsz = mem.shape[0]
    kv = rms_norm(mem, p['ln_mem']) @ p['w_ckv']
    mk, mv = jnp.split(kv, 2, axis=-1)
    mk = rms_norm(mk.reshape(bsz, N_MEM, MEM_HEADS, MEM_HEAD_DIM), p['ck_norm'])
    mv = mv.reshape(bsz, N_MEM, MEM_HEADS, MEM_HEAD_DIM)
    return mk, mv

def memory_attend(h, mk, mv, p):
    bsz, t, _ = h.shape
    q = rms_norm((h @ p['w_cq']).reshape(bsz, t, MEM_HEADS, MEM_HEAD_DIM), p['cq_norm'])
    s = jnp.einsum('bthd,bmhd->bhtm', q.astype(jnp.float32), mk.astype(jnp.float32)) * (MEM_HEAD_DIM ** -0.5)
    pr = jax.nn.softmax(s, axis=-1)
    o = jnp.einsum('bhtm,bmhd->bthd', pr, mv.astype(jnp.float32)).astype(h.dtype)
    return o.reshape(bsz, t, D_MODEL) @ p['w_co']

def decoder_layer(x, pos0, pool_buf, conv_buf, past_k, past_v, mk, mv, p):
    x = x + 0.5 * swiglu_ffn(rms_norm(x, p['ln_ffn1']), p['w_ffn1_in'], p['w_ffn1_out'])
    y, new_pool, new_conv, k, v = mixer_groups(rms_norm(x, p['ln_mix']), pos0, pool_buf, conv_buf, past_k, past_v, p)
    x = x + y
    x = x + memory_attend(rms_norm(x, p['ln_cross']), mk, mv, p)
    x = x + 0.5 * swiglu_ffn(rms_norm(x, p['ln_ffn2']), p['w_ffn2_in'], p['w_ffn2_out'])
    return x, new_pool, new_conv, k, v

def setup_inputs(seed: int = 0) -> dict:
    key = jax.random.key(seed)
    ks = iter(jax.random.split(key, 64))
    f32 = jnp.float32
    L = DEPTH

    def nrm(shape, scale=1.0):
        return jax.random.normal(next(ks), shape, f32) * scale

    def gain(shape):
        return 1.0 + 0.05 * jax.random.normal(next(ks), shape, f32)

    n_pages = PAST_LEN // PAGE_SIZE
    n_phys = (DEC_BATCH * n_pages * 5) // 4
    inp = {}
    inp['x_prompt'] = nrm((BATCH, SEQ, D_MODEL))
    inp['x_sample'] = nrm((DEC_BATCH, DEC_SEQ, D_MODEL))
    inp['cache_att_k'] = nrm((L, n_phys, PAGE_SIZE, ATT_HEADS, ATT_HEAD_DIM))
    inp['cache_att_v'] = nrm((L, n_phys, PAGE_SIZE, ATT_HEADS, ATT_HEAD_DIM))
    inp['cache_mem_k'] = nrm((L, DEC_BATCH, N_MEM, MEM_HEADS, MEM_HEAD_DIM))
    inp['cache_mem_v'] = nrm((L, DEC_BATCH, N_MEM, MEM_HEADS, MEM_HEAD_DIM))
    inp['state_pool'] = nrm((L, DEC_BATCH, POOL_BUF, POOL_WIDTH))
    inp['state_conv'] = nrm((L, DEC_BATCH, CONV_BUF, CONV_WIDTH), 0.5)
    perm = jax.random.permutation(next(ks), n_phys)
    inp['page_table'] = perm[:DEC_BATCH * n_pages].reshape(DEC_BATCH, n_pages).astype(jnp.int32)
    inp['mem_prompt'] = nrm((BATCH, N_MEM, D_MODEL))
    inp['ln_ffn1'] = gain((L, D_MODEL))
    inp['w_ffn1_in'] = nrm((L, D_MODEL, 2 * D_FF), D_MODEL ** -0.5)
    inp['w_ffn1_out'] = nrm((L, D_FF, D_MODEL), D_FF ** -0.5)
    inp['ln_mix'] = gain((L, D_MODEL))
    inp['w_in'] = nrm((L, D_MODEL, IN_WIDTH), D_MODEL ** -0.5)
    inp['pool_w'] = nrm((L, POOL_GROUPS, POOL_GROUP_WIDTH, POOL_GROUP_WIDTH), POOL_GROUP_WIDTH ** -0.5)
    inp['pool_scale'] = 1.0 + 0.1 * nrm((L, POOL_WIDTH))
    inp['conv_dw_w'] = nrm((L, CONV_K, CONV_WIDTH), CONV_K ** -0.5)
    inp['conv_dw_b'] = nrm((L, CONV_WIDTH), 0.02)
    inp['conv_ln_g'] = gain((L, CONV_WIDTH))
    inp['conv_ln_b'] = nrm((L, CONV_WIDTH), 0.02)
    inp['conv_pw_w'] = nrm((L, CONV_WIDTH, CONV_WIDTH), CONV_WIDTH ** -0.5)
    inp['conv_pw_b'] = nrm((L, CONV_WIDTH), 0.02)
    inp['att_q_norm'] = gain((L, ATT_HEAD_DIM))
    inp['att_k_norm'] = gain((L, ATT_HEAD_DIM))
    inp['w_out'] = nrm((L, MIX_WIDTH, D_MODEL), MIX_WIDTH ** -0.5)
    inp['ln_cross'] = gain((L, D_MODEL))
    inp['ln_mem'] = gain((L, D_MODEL))
    inp['w_cq'] = nrm((L, D_MODEL, D_MODEL), D_MODEL ** -0.5)
    inp['w_ckv'] = nrm((L, D_MODEL, 2 * D_MODEL), D_MODEL ** -0.5)
    inp['cq_norm'] = gain((L, MEM_HEAD_DIM))
    inp['ck_norm'] = gain((L, MEM_HEAD_DIM))
    inp['w_co'] = nrm((L, D_MODEL, D_MODEL), D_MODEL ** -0.5)
    inp['ln_ffn2'] = gain((L, D_MODEL))
    inp['w_ffn2_in'] = nrm((L, D_MODEL, 2 * D_FF), D_MODEL ** -0.5)
    inp['w_ffn2_out'] = nrm((L, D_FF, D_MODEL), D_FF ** -0.5)
    return inp

def reference(x_prompt, x_sample, cache_att_k, cache_att_v, cache_mem_k, cache_mem_v, state_pool, state_conv,
              page_table, mem_prompt, ln_ffn1, w_ffn1_in, w_ffn1_out, ln_mix, w_in, pool_w, pool_scale,
              conv_dw_w, conv_dw_b, conv_ln_g, conv_ln_b, conv_pw_w, conv_pw_b, att_q_norm, att_k_norm, w_out,
              ln_cross, ln_mem, w_cq, w_ckv, cq_norm, ck_norm, w_co, ln_ffn2, w_ffn2_in, w_ffn2_out):
    weights = dict(ln_ffn1=ln_ffn1, w_ffn1_in=w_ffn1_in, w_ffn1_out=w_ffn1_out, ln_mix=ln_mix, w_in=w_in,
                   pool_w=pool_w, pool_scale=pool_scale, conv_dw_w=conv_dw_w, conv_dw_b=conv_dw_b,
                   conv_ln_g=conv_ln_g, conv_ln_b=conv_ln_b, conv_pw_w=conv_pw_w, conv_pw_b=conv_pw_b,
                   att_q_norm=att_q_norm, att_k_norm=att_k_norm, w_out=w_out, ln_cross=ln_cross, ln_mem=ln_mem,
                   w_cq=w_cq, w_ckv=w_ckv, cq_norm=cq_norm, ck_norm=ck_norm, w_co=w_co, ln_ffn2=ln_ffn2,
                   w_ffn2_in=w_ffn2_in, w_ffn2_out=w_ffn2_out)
    bsz = x_prompt.shape[0]
    dbsz = x_sample.shape[0]
    n_pages = page_table.shape[1]
    past_len = n_pages * PAGE_SIZE
    hp = x_prompt
    hs = x_sample
    p_k, p_v, p_mk, p_mv, p_pool, p_conv = [], [], [], [], [], []
    s_k, s_v, s_pool, s_conv = [], [], [], []
    for l in range(DEPTH):
        p = {name: w[l] for name, w in weights.items()}
        mk, mv = memory_kv(mem_prompt, p)
        zero_pool = jnp.zeros((bsz, POOL_BUF, POOL_WIDTH), hp.dtype)
        zero_conv = jnp.zeros((bsz, CONV_BUF, CONV_WIDTH), hp.dtype)
        hp, np_pool, np_conv, nk, nv = decoder_layer(hp, 0, zero_pool, zero_conv, None, None, mk, mv, p)
        p_k.append(nk)
        p_v.append(nv)
        p_mk.append(mk)
        p_mv.append(mv)
        p_pool.append(np_pool)
        p_conv.append(np_conv)
        past_k = cache_att_k[l][page_table].reshape(dbsz, past_len, ATT_HEADS, ATT_HEAD_DIM)
        past_v = cache_att_v[l][page_table].reshape(dbsz, past_len, ATT_HEADS, ATT_HEAD_DIM)
        hs, ns_pool, ns_conv, sk, sv = decoder_layer(hs, past_len, state_pool[l], state_conv[l], past_k, past_v,
                                                     cache_mem_k[l], cache_mem_v[l], p)
        s_k.append(sk)
        s_v.append(sv)
        s_pool.append(ns_pool)
        s_conv.append(ns_conv)
    return (hp, hs, jnp.stack(p_k), jnp.stack(p_v), jnp.stack(p_mk), jnp.stack(p_mv), jnp.stack(p_pool),
            jnp.stack(p_conv), jnp.stack(s_k), jnp.stack(s_v), jnp.stack(s_pool), jnp.stack(s_conv))


_drawn_inputs = setup_inputs


def setup_inputs(seed=0):
    import zlib

    import numpy as np

    out = dict(_drawn_inputs(seed))
    spreads = {}
    factors = {'conv_dw_b': 3.611,
     'conv_ln_g': 2.697,
     'conv_ln_b': 8.0,
     'conv_pw_b': 4.974,
     'att_q_norm': 7.201,
     'ln_cross': 8.0,
     'cq_norm': 8.0}
    for name, (base, spread) in spreads.items():
        noise = np.random.default_rng([zlib.crc32(name.encode()), seed]).standard_normal(out[name].shape)
        drawn = base * np.exp(spread * noise) if base else spread * noise
        out[name] = jnp.asarray(drawn.astype(out[name].dtype))
    for name, factor in factors.items():
        out[name] = (out[name] * factor).astype(out[name].dtype)
    return out
```

```python
from contextlib import ExitStack

import numpy as np

import concourse.bass as bass
from concourse import mybir

F32 = mybir.dt.float32
F32R = mybir.dt.float32r
I32 = mybir.dt.int32
ACT = mybir.ActivationFunctionType
ALU = mybir.AluOpType
AX = mybir.AxisListType

P = 128
D_MODEL, SEQ, DEPTH, SAMPLES, NEW, PAST, PAGE = 1024, 256, 2, 8, 4, 256, 128
TS = SAMPLES * NEW
T = SEQ + TS
KD = D_MODEL // P
D_FF = ((8 * D_MODEL // 3 + 127) // 128) * 128
KF = D_FF // P
POOL_W, CONV_W, HEADS, DH = 256, 256, 4, 128
ATT_W = HEADS * DH
WINDOWS = (2, 4, 8, 16)
PBUF, CONV_K = max(WINDOWS) - 1, 31
CBUF = CONV_K - 1
N_MEM, MDH = 256, 256
PAGES = PAST // PAGE
ROPE_DIM, THETA = DH // 4, 500000.0
EPS = 1e-6
MASKED = -1e30
PX = PBUF + SEQ + SAMPLES * (PBUF + NEW)
CX = CBUF + SEQ + SAMPLES * (CBUF + NEW)
ROWS = SAMPLES * HEADS * NEW

COLS = {}
_at = 0
for _name, _n in (("ident", P), ("causal", P), ("own", TS), ("inv_count", 2 * PX), ("cos", T), ("sin", T), ("swap", ROPE_DIM)):
    COLS[_name] = (_at, _at + _n)
    _at += _n
N_CONST = _at

PROWS = {}
_at = 0
for _name, _n in (("ln_ffn1", 8), ("ln_mix", 8), ("ln_cross", 8), ("ln_mem", 8), ("ln_ffn2", 8), ("pool_scale", 2),
                  ("conv_dw_b", 2), ("conv_ln_g", 2), ("conv_ln_b", 2), ("conv_pw_b", 2), ("att_q_norm", 1),
                  ("att_k_norm", 1), ("cq_norm", 2), ("conv_dw_w", 2 * CONV_K)):
    PROWS[_name] = (_at, _n)
    _at += _n
N_PROWS = _at

UNITS, TURNS = {}, {}
_u = _t = 0
for _name, _nu, _nt in (("f1in", KF, KF), ("f1out", 12, 4), ("state_in", 0, 1), ("win", 9, 9), ("qk_stat", 0, 4),
                        ("rope", 0, 4), ("pool", 0, 1), ("state_out", 0, 1), ("tok", 0, 3), ("att_k", 0, SAMPLES),
                        ("att_s", 0, 2), ("att_pt", 0, 2), ("att_o", 0, 2), ("pw", 0, 1), ("wout", 4, 4),
                        ("cq", 4, 4), ("ckv", 8, 8), ("cq_stat", 0, 2), ("mkt", 0, 2), ("mem_k", 0, 2 * SAMPLES),
                        ("cx_s", 0, 2), ("cx_pt", 0, 2), ("cx_o", 0, 2), ("co", 4, 4), ("f2in", KF, KF),
                        ("f2out", 12, 4)):
    UNITS[_name], TURNS[_name] = _u, _t
    _u += _nu
    _t += _nt
N_UNITS = _u
RING_UNITS = N_UNITS + N_UNITS % 2
N_TURNS = _t
assert N_TURNS % 2 == 0
UNIT = 2048
OUT_PARTS = (8, 8, KF - 16)


def shape_constants():
    c = np.zeros((P, N_CONST), np.float32)

    def put(name, a):
        c[:a.shape[0], COLS[name][0]:COLS[name][0] + a.shape[1]] = a

    put("ident", np.eye(P, dtype=np.float32))
    put("causal", np.where(np.arange(P)[None, :] <= np.arange(P)[:, None], 0.0, MASKED).astype(np.float32))
    rb, rt = np.arange(ROWS) // (HEADS * NEW), np.arange(ROWS) % NEW
    cb, ct = np.arange(TS) // NEW, np.arange(TS) % NEW
    ok = (rb[:, None] == cb[None, :]) & (ct[None, :] <= rt[:, None])
    put("own", np.where(ok, 0.0, MASKED).astype(np.float32))
    inv = np.zeros((P, 2, PX), np.float32)
    for g, win in enumerate(WINDOWS):
        rows = slice(64 * (g % 2), 64 * (g % 2) + 64)
        inv[rows, g // 2, :] = 1.0 / win
        inv[rows, g // 2, PBUF:PBUF + SEQ] = 1.0 / np.minimum(np.arange(SEQ) + 1, win)
    put("inv_count", inv.reshape(P, -1))
    half = ROPE_DIM // 2
    freq = np.power(np.float32(THETA), -np.arange(half, dtype=np.float32) / np.float32(half)).astype(np.float32)
    pos = np.concatenate([np.arange(SEQ), PAST + np.arange(TS) % NEW]).astype(np.float32)
    ang = (pos[None, :] * freq[:, None]).astype(np.float32)
    put("cos", np.concatenate([np.cos(ang), np.cos(ang)]).astype(np.float32))
    put("sin", np.concatenate([-np.sin(ang), np.sin(ang)]).astype(np.float32))
    put("swap", np.roll(np.eye(ROPE_DIM, dtype=np.float32), half, axis=0))
    return c


def trunk_kernel(nc, a, o):
    with ExitStack() as ctx:
        cursor = [nc.sbuf_base + (-nc.sbuf_base) % 64]

        def at(name, shape, dt, offset):
            return nc.alloc_sbuf_tensor_at(name, [P, *shape], dt, offset=offset)

        def region(n_elems):
            start = cursor[0]
            cursor[0] += 4 * n_elems
            cursor[0] += (-cursor[0]) % 32
            return start

        def sb(name, shape, dt=F32):
            return at(name, shape, dt, region(int(np.prod(shape))))

        raw = sb("raw_weights", [2, UNIT])
        w_hi = sb("w_hi", [2, UNIT], F32R)
        w_lo = sb("w_lo", [2, UNIT], F32R)
        x = sb("x_residual", [KD, T])
        const = sb("shape_consts", [N_CONST])
        prm_all = sb("params_all", [DEPTH, N_PROWS])
        prm = sb("params", [N_PROWS])
        ck_gain = sb("ck_gain", [MDH])
        pool_w = sb("pool_w_blocks", [2, P])
        pw_w = sb("conv_pw_w", [2, CONV_W])
        mem_t = sb("mem_normed", [KD, N_MEM])
        q_diag = sb("q_diag", [2, SAMPLES * HEADS, 32])
        ones = sb("ones", [P])
        small = sb("small", [96])
        pages = nc.alloc_sbuf_tensor_at("pages", [1, SAMPLES * PAGES], I32, offset=region(SAMPLES * PAGES))
        h_at = region(2 * KD * T)
        h_hi = at("h_hi", [KD, T], F32R, h_at)
        h_lo = at("h_lo", [KD, T], F32R, h_at + 4 * KD * T)
        hh0, hl0 = h_at, h_at + 4 * KD * T
        squares = at("squares", [KD, T], F32, hl0)
        rq = at("qk_rms", [2, 2, T], F32, hh0)
        conv_sq = at("conv_sq", [2, T], F32, hh0 + 16 * T)
        rope_tmp = at("rope_tmp", [2, T], F32, hh0 + 16 * T)
        conv_act = at("conv_act", [2, T], F32, hh0 + 24 * T)
        probs = at("att_probs", [HEADS, 384], F32, hl0)
        sprobs = at("att_sample_probs", [PAST + TS], F32, hl0 + 6144)
        sprobs_t = at("att_sample_probs_t", [384], F32, hl0 + 6144 + 4 * T)
        cx_probs = at("cx_probs", [HEADS, 512], F32, hl0)
        cx_sprobs = at("cx_sample_probs", [N_MEM], F32, hh0)
        cx_sprobs_t = at("cx_sample_probs_t", [N_MEM], F32, hh0 + 4 * N_MEM)
        y_at = region(2 * KD * T)
        y_hi = at("y_hi", [KD, T], F32R, y_at)
        y_lo = at("y_lo", [KD, T], F32R, y_at + 4 * KD * T)
        norm_tmp = at("norm_tmp", [KD, T], F32, y_at + 4 * KD * T)
        mix_tmp_at = region(2 * T)
        silu = at("silu", [2, T], F32, mix_tmp_at)
        mix_tmp = at("mix_tmp", [2, T], F32, mix_tmp_at)
        norm_r = sb("norm_r", [T])
        kv_at = region(2 * 2048)
        mem_kv = at("mem_kv", [2, 2, D_MODEL], F32, kv_at)
        att_kv = at("att_kv", [2, PAGES, ATT_W], F32, kv_at)
        rows_in = at("rows_in", [2, 2, D_MODEL], F32, kv_at)
        conv_a = at("conv_a", [2, T], F32, kv_at + 8192)
        conv_gate = at("conv_gate", [2, T], F32, kv_at + 8192 + 8 * T)
        conv_acc = at("conv_acc", [2, T], F32, kv_at + 8192 + 16 * T)
        kt_at = region(2 * 2048)
        mem_kt = at("mem_kt", [2, KD, N_MEM], F32, kt_at)
        att_kt = at("att_kt", [2, HEADS, PAST], F32, kt_at)
        win_a = at("win_a", [PX], F32, kt_at + 8192)
        win_b = at("win_b", [PX], F32, kt_at + 8192 + 1696)
        win_c = at("win_c", [PX], F32, kt_at + 8192 + 2 * 1696)
        pool_rows = at("pool_rows", [POOL_W], F32, kt_at + 8192 + 3 * 1696)
        conv_rows = at("conv_rows", [2, CONV_W], F32, kt_at + 8192 + 3 * 1696 + 1024)
        param_rows = at("param_rows", [DEPTH, P], F32, kt_at)
        arena = region(2 * KF * T)
        g_hi = at("g_hi", [KF, T], F32R, arena)
        g_lo = at("g_lo", [KF, T], F32R, arena + 4 * KF * T)
        zpos = [arena]

        def az(name, shape):
            start = zpos[0]
            zpos[0] += (4 * int(np.prod(shape)) + 31) // 32 * 32
            assert zpos[0] <= arena + 8 * KF * T, name
            return at(name, shape, F32, start)

        z = az("z_qk", [KD, T])
        after_z = zpos[0]
        v_t = az("v_t", [HEADS, T])
        k_tok = az("k_tok", [3, ATT_W])
        v_tok = az("v_tok", [3, ATT_W])
        pxt = az("pool_ext", [2, PX])
        cxt = az("conv_ext", [2, CX])
        pool_d = az("pool_diff", [2, PX])
        fresh = az("fresh", [4, TS])
        probs_t = az("att_probs_t", [HEADS, 384])
        sstate = az("sample_state", [2 * POOL_W])
        pstate = az("prompt_state", [2, POOL_W])
        zpos[0] = after_z
        mk = az("mk", [2, D_MODEL])
        mv = az("mv", [2, D_MODEL])
        mkt = az("mk_t", [KD, N_MEM])
        cx_probs_t = az("cx_probs_t", [HEADS, 512])
        zpos[0] = arena
        y_rows = az("y_rows", [3, D_MODEL])
        assert cursor[0] <= nc.sbuf_usable_end, (cursor[0], nc.sbuf_usable_end)

        G = ctx.enter_context(nc.psum_tensor("pairs", [P, 2, 2, 512], F32))
        M = ctx.enter_context(nc.psum_tensor("fixed", [P, 4, 512], F32))
        SCORES, STAT, TP, NEWS = 0, 1, 2, 3

        def sem(name):
            return ctx.enter_context(nc.semaphore(name))

        raw_landed = [sem(f"raw_landed{i}") for i in range(2)]
        hi_ready, lo_ready, unit_used = sem("hi_ready"), sem("lo_ready"), sem("unit_used")
        acc_ready, acc_free = sem("acc_ready"), sem("acc_free")
        const_landed, rows_landed, pages_landed = sem("const_landed"), sem("rows_landed"), sem("pages_landed")
        mem_landed, x_landed = sem("mem_landed"), sem("x_landed")
        fills_done, start_turned, start_taken = sem("fills_done"), sem("start_turned"), sem("start_taken")
        mem_sq, mem_norm = sem("mem_squared"), sem("mem_normed_s")
        sq_ready, stat_ready, root_ready, h_ready = (sem(n) for n in ("sq_ready", "stat_ready", "root_ready", "h_ready"))
        silu_ready, g_ready = sem("silu_ready"), sem("g_ready")
        gate_ready, zsq_ready, rq_ready, z_normed, z_done = (
            sem(n) for n in ("gate_ready", "zsq_ready", "rq_ready", "z_normed", "z_done"))
        mixer_idle, mixer_params, states_in = sem("mixer_idle"), sem("mixer_params"), sem("states_in")
        tiles_free, out_landed, carry_landed = sem("tiles_free"), sem("out_landed"), sem("carry_landed")
        pooled, fresh_ready = sem("pooled"), sem("fresh_ready")
        kv_landed = [sem(f"kv_landed{i}") for i in range(2)]
        v_used, kt_half, score_done = sem("v_used"), sem("kt_half"), sem("score_done")
        q_diag_ready, news_done, s_bias, s_exp, s_probs, s_turned, s_probs_t = (
            sem(n) for n in ("q_diag_ready", "news_done", "s_bias", "s_exp", "s_probs", "s_turned", "s_probs_t"))
        p_bias, p_exp, p_probs = sem("p_bias"), sem("p_exp"), sem("p_probs")
        conv_done, ln_sum, ln_centred, ln_sq, ln_var, ln_root, ln_out, conv_silu = (
            sem(n) for n in ("conv_done", "ln_sum", "ln_centred", "ln_sq", "ln_var", "ln_root", "ln_out", "conv_silu"))
        y_ready, m_ready, mk_sq, mk_root, mk_ready = (
            sem(n) for n in ("y_ready", "m_ready", "mk_sq", "mk_root", "mk_ready"))
        rows_ready, final_landed = sem("rows_ready"), sem("final_landed")
        cx_bias = sem("cx_bias")
        sp_passed, pool_passed = sem("sp_passed"), sem("pool_passed")
        x_sample_rows = mem_kt[0:TS, 1, 0:4, :].rearrange("p k c -> p (k c)")

        def cc(name, parts=P):
            return const[0:parts, COLS[name][0]:COLS[name][1]]

        ident = cc("ident")

        def par(name, k=0):
            r = PROWS[name][0] + k
            return prm[:, r:r + 1]

        def ap(t, offset, dims, parts=P, part0=0):
            full = t[part0:part0 + parts]
            return bass.AP(tensor=full.tensor, offset=full.offset + offset, ap=[[full.ap[0][0], parts], *dims])

        sm = lambda i, n=1: small[:, i:i + n]
        eps = sm(0)

        def pool_diff(c):
            return pool_d[:, c, :]

        def spread_q(dve, att):
            for d in range(1 if att else 2):
                for odd in range(2):
                    dst = ap(q_diag, d * SAMPLES * HEADS * 32 + odd * (HEADS * 32 + 16), [[256, 4], [36, HEADS], [1, NEW]])
                    src = ap(z, (0 if att else d * T) + SEQ + odd * NEW, [[2 * NEW, 4], [T if att else 2 * T, HEADS], [1, NEW]])
                    last = dve.tensor_copy(dst, src)
            last.then_inc(q_diag_ready, 1)

        def normalise_probs(dve, L, exp_sem, exp_value, tile, parts, done):
            dve.wait_ge(exp_sem, exp_value)
            dve.reciprocal(sm(48, 8), sm(24, 8))
            dve.drain()
            for h in range(HEADS):
                for c, s in enumerate(parts):
                    dve.tensor_scalar(tile[:, h, s], tile[:, h, s], sm(48 + 2 * h + c), None, ALU.mult).then_inc(done, 1)

        def raw_value(L, i, u):
            per_layer = RING_UNITS // 2 - (u % 2) * (RING_UNITS - N_UNITS)
            return 32 * (L * per_layer + i + u // 2 + 1)

        def half_value(L, i, u, half):
            return L * (2 * RING_UNITS) + i * 4 + (2 * u + half + 1)

        def half_inc(u, half):
            return 1 + (2 * (RING_UNITS - N_UNITS) if (u == N_UNITS - 1 and half) else 0)

        def turn_value(L, i, t):
            return L * N_TURNS + i * 2 + (t + 1)

        def passed(L, i, t):
            return turn_value(L, i, t) + 2

        def release(u):
            prev = u - 2
            if prev < 0:
                return "turn", -1
            for name in UNITS:
                nu = {"f1out": 12, "f2out": 12}.get(name)
                if nu and UNITS[name] <= prev < UNITS[name] + nu:
                    m, q = divmod(prev - UNITS[name], 3)
                    if q < 2:
                        return "unit", 2 * m + q + (8 if name == "f2out" else 0)
                    return "turn", TURNS[name] + m
            name = [n for n in UNITS if UNITS[n] <= prev and (n.startswith("f") or n in ("win", "wout", "cq", "ckv", "co"))][-1]
            return "turn", TURNS[name] + prev - UNITS[name]

        def chunks_of(u):
            for f in ("f1out", "f2out"):
                if UNITS[f] <= u < UNITS[f] + 12:
                    return OUT_PARTS[(u - UNITS[f]) % 3]
            return 8

        block = ctx.enter_context(nc.Block())

        @block.sync
        def _(sp):
            sp.dma_start(const[:, :], a["shape_constants"]).then_inc(const_landed, 16)
            sp.dma_start(pages[:, :], a["page_table"].rearrange("(o b) c -> o (b c)", o=1)).then_inc(pages_landed, 16)
            sp.dma_start(rows_in[:, 0, :, :], a["mem_prompt"].rearrange("o (c p) d -> p (o c) d", p=P)).then_inc(mem_landed, 16)
            sp.dma_start(rows_in[:, 1, :, :], a["x_prompt"].rearrange("o (c p) d -> p (o c) d", p=P)).then_inc(x_landed, 16)
            sp.dma_start(x_sample_rows, a["x_sample"].rearrange("b t d -> (b t) d")).then_inc(x_landed, 16)

            def load(L, i, u, src, nk=8, gates=False):
                sp.wait_ge(lo_ready, half_value(L, i, u, 1))
                sp.sem_inc(sp_passed, 1)
                dst = raw[:, u % 2, 0:nk * 256]
                if gates:
                    dst = dst.rearrange("p (k g c) -> p k g c", g=2, c=P)
                    for g in range(2):
                        sp.dma_start(dst[:, :, g, :], src[:, :, g, :]).then_inc(raw_landed[u % 2], 16)
                else:
                    sp.dma_start(dst.rearrange("p (k c) -> p k c", c=256), src).then_inc(raw_landed[u % 2], 32)

            def ffn_in(L, name, w):
                v = w.rearrange("l (k p) (g m c) -> l m p k g c", p=P, g=2, c=P)
                with sp.Fori(0, KF // 2) as i:
                    for j in range(2):
                        load(L, i, UNITS[name] + j, v[L, i * 2 + j], gates=True)

            def ffn_out(L, name, w):
                v = w.rearrange("l (k p) (m c) -> l m p k c", p=P, c=256)
                for m in range(4):
                    for n, nk in enumerate(OUT_PARTS):
                        load(L, 0, UNITS[name] + 3 * m + n, v[L, m, :, 8 * n:8 * n + nk, :], nk)

            def square(L, name, w, order):
                v = w.rearrange("l (k p) (m c) -> l m p k c", p=P, c=256)
                for n, m in enumerate(order):
                    load(L, 0, UNITS[name] + n, v[L, m])

            with sp.Fori(0, DEPTH) as L:
                ffn_in(L, "f1in", a["w_ffn1_in"])
                ffn_out(L, "f1out", a["w_ffn1_out"])
                square(L, "win", a["w_in"], (1, 2, 0, 3, 4, 5, 6, 7, 8))
                square(L, "wout", a["w_out"], range(4))
                square(L, "cq", a["w_cq"], range(4))
                square(L, "ckv", a["w_ckv"], range(8))
                square(L, "co", a["w_co"], range(4))
                ffn_in(L, "f2in", a["w_ffn2_in"])
                ffn_out(L, "f2out", a["w_ffn2_out"])
            sp.wait_ge(rows_ready, 3)
            sp.dma_start(o["y_prompt"].rearrange("o (c p) d -> p (o c) d", p=P), y_rows[:, 0:2, :]).then_inc(final_landed, 16)
            sp.dma_start(o["y_sample"].rearrange("b t d -> (b t) d"), y_rows[0:TS, 2, :]).then_inc(final_landed, 16)
            sp.wait_ge(final_landed, 32)

        @block.gpsimd
        def _(pool):
            pool.memset(ones[:, :], 1.0).then_inc(fills_done, 1)
            pool.memset(eps, EPS).then_inc(fills_done, 1)
            pool.memset(q_diag[:, :, :, :], 0.0).then_inc(fills_done, 1)
            pool.memset(pool_w[:, :, :], 0.0).then_inc(fills_done, 1)
            for name, (r, n) in PROWS.items():
                src = a[name]
                if name == "conv_dw_w":
                    src = src.rearrange("l j (c p) -> (j c) l p", p=P)
                else:
                    src = src.rearrange("l (c p) -> c l p", p=P)
                pool.dma_start(param_rows[r:r + n, :, :], src).then_inc(rows_landed, 16)
            pool.dma_start(o["s_pool"][:, :, 0:PBUF - NEW, :], a["state_pool"][:, :, NEW:PBUF, :]).then_inc(carry_landed, 16)
            pool.dma_start(o["s_conv"][:, :, 0:CBUF - NEW, :], a["state_conv"][:, :, NEW:CBUF, :]).then_inc(carry_landed, 16)
            pool.wait_ge(pages_landed, 16)
            pool.wait_ge(fills_done, 4)
            pool.wait_ge(start_taken, 10)

            def page(L, n, cache):
                if n >= SAMPLES + 2:
                    pool.wait_ge(v_used, L * (2 * SAMPLES) + n - SAMPLES - 1)
                elif n >= 2:
                    pool.wait_ge(acc_ready, passed(L, 0, TURNS["att_k"] + n - 2))
                pool.sem_inc(pool_passed, 1)
                for c in range(PAGES):
                    i = (n % SAMPLES) * PAGES + c
                    which = pool.value_load(pages[0:1, i:i + 1], min_val=0, max_val=cache.shape[1] - 1)
                    pool.dma_start(att_kv[:, n % 2, c, :], cache[L, bass.ds(which, 1), :, :, :].rearrange("o p h d -> p (o h d)")
                                   ).then_inc(kv_landed[n % 2], 16)

            with pool.Fori(0, DEPTH) as L:
                pool.wait_ge(mixer_idle, L + 1)
                for g in range(4):
                    s = slice(64 * (g % 2), 64 * (g % 2) + 64)
                    pool.dma_start(pool_w[s, g // 2, s], a["pool_w"][L, g]).then_inc(mixer_params, 16)
                pool.dma_start(pw_w[:, :, :], a["conv_pw_w"][L].rearrange("(k p) c -> p k c", p=P)).then_inc(mixer_params, 16)
                pool.dma_start(ck_gain[:, :], a["ck_norm"][L].partition_broadcast(P)).then_inc(mixer_params, 16)
                pool.dma_start(pool_rows[0:120, :], a["state_pool"][L].rearrange("b r c -> (b r) c")).then_inc(states_in, 16)
                pool.dma_start(conv_rows[0:120, :, :], a["state_conv"][L].rearrange("(n b) r c -> (b r) n c", n=2)).then_inc(states_in, 16)
                for n in range(SAMPLES):
                    page(L, n, a["cache_att_k"])
                for n in range(SAMPLES, 2 * SAMPLES):
                    page(L, n, a["cache_att_v"])
                pool.wait_ge(acc_free, passed(L, 0, TURNS["tok"] + 2))
                for name, tile in (("att_k", k_tok), ("att_v", v_tok)):
                    pool.dma_start(o["p_" + name][L].rearrange("o (c p) h d -> p (o c) (h d)", p=P), tile[:, 0:2, :]).then_inc(out_landed, 16)
                    pool.dma_start(o["s_" + name][L].rearrange("b t h d -> (b t) (h d)"), tile[0:TS, 2, :]).then_inc(out_landed, 16)
                pool.dma_start(o["s_pool"][L][:, PBUF - NEW:PBUF, :], sstate[0:TS, 0:POOL_W]).then_inc(out_landed, 16)
                pool.dma_start(o["s_conv"][L][:, CBUF - NEW:CBUF, :], sstate[0:TS, POOL_W:]).then_inc(out_landed, 16)
                pool.dma_start(o["p_pool"][L, 0], pstate[0:PBUF, 0, :]).then_inc(out_landed, 16)
                pool.dma_start(o["p_conv"][L, 0], pstate[0:CBUF, 1, :]).then_inc(out_landed, 16)
                pool.wait_ge(out_landed, L * 160 + 128)
                pool.sem_inc(tiles_free, 1)
                pool.wait_ge(conv_silu, L + 1)
                for n in range(2 * SAMPLES):
                    cache = a["cache_mem_k"] if n < SAMPLES else a["cache_mem_v"]
                    if 2 <= n < SAMPLES + 2:
                        pool.wait_ge(acc_ready, passed(L, 0, TURNS["mem_k"] + 2 * (n - 2) + 1))
                    else:
                        before = SAMPLES - 1 if n < 2 else n - 2
                        pool.wait_ge(v_used, L * (2 * SAMPLES) + before + 1)
                    pool.sem_inc(pool_passed, 1)
                    pool.dma_start(mem_kv[:, n % 2, :, :], cache[L, n % SAMPLES].rearrange("(c p) h d -> p c (h d)", p=P)
                                   ).then_inc(kv_landed[n % 2], 16)
                pool.wait_ge(mk_ready, L * 8 + 8)
                pool.wait_ge(acc_free, passed(L, 0, TURNS["ckv"] + 7))
                pool.dma_start(o["p_mem_k"][L, 0].rearrange("(c p) h d -> p c (h d)", p=P), mk[:, :, :]).then_inc(out_landed, 16)
                pool.dma_start(o["p_mem_v"][L, 0].rearrange("(c p) h d -> p c (h d)", p=P), mv[:, :, :]).then_inc(out_landed, 16)
                pool.wait_ge(out_landed, L * 160 + 160)
                pool.sem_inc(tiles_free, 1)
            pool.wait_ge(carry_landed, 32)

        def kv_value(L, n):
            per_layer = 16 * (SAMPLES * PAGES + SAMPLES)
            done = n // 2 + 1
            att = min(done, SAMPLES)
            return L * per_layer + 16 * (att * PAGES + (done - att))

        @block.scalar
        def _(act):
            def copy(out, in_):
                return act.activation(out, in_, ACT.Copy)

            def split(L, i, u, base=0):
                n = chunks_of(u) * 128
                act.wait_ge(raw_landed[u % 2], raw_value(L, i, u))
                kind, n_before = release(u)
                if kind == "turn":
                    act.wait_ge(acc_ready, passed(L, i, n_before))
                else:
                    act.wait_ge(unit_used, L * 16 + n_before + 1)
                for half in range(2):
                    s = slice(half * n, half * n + n)
                    copy(w_hi[:, u % 2, s], raw[:, u % 2, s]).then_inc(hi_ready, half_inc(u, half))

            def norm(L, n):
                for k in range(KD):
                    if n == 0:
                        act.wait_ge(acc_free, passed(L, 0, -1))
                    else:
                        act.wait_ge(acc_free, passed(L, 0, TURNS[("", "f1out", "wout", "co")[n]] + k // 2))
                    act.activation(squares[:, k, :], x[:, k, :], ACT.Square).then_inc(sq_ready, 1)
                act.wait_ge(stat_ready, L * 4 + n + 1)
                act.activation(norm_r[:, :], M[:, STAT, 0:T], ACT.Sqrt, bias=eps, scale=1.0 / D_MODEL).then_inc(root_ready, 1)

            def ffn(L, first, fin, fout):
                n0 = 0 if fin == "f1in" else KF
                u0, t0 = UNITS[fin], TURNS[fin]
                with act.Fori(0, KF // 2) as i:
                    for j in range(2):
                        split(L, i, u0 + j + 1)
                        act.wait_ge(acc_ready, passed(L, i, t0 + j))
                        act.activation(silu[:, (t0 + j) % 2, :], G[:, (t0 + j) % 2, 0, 0:T], ACT.Silu).then_inc(silu_ready, 1)
                u0 = UNITS[fout]
                for n in range(1, 12):
                    split(L, 0, u0 + n)
                if fout == "f1out":
                    split(L, 0, u0 + 12)

            act.wait_ge(fills_done, 4)
            act.wait_ge(mem_landed, 16)
            for c in range(2):
                act.activation(norm_tmp[:, 4 * c:4 * c + 4, 0:256], rows_in[:, 0, c, :], ACT.Square, accum_out=sm(1 + c))
            act.drain()
            act.activation(sm(3, 2), sm(1, 2), ACT.Sqrt, bias=eps, scale=1.0 / D_MODEL).then_inc(mem_sq, 1)

            act.wait_ge(start_taken, 10)
            with act.Fori(0, DEPTH) as L:
                split(L, 0, 0)
                norm(L, 0)
                ffn(L, 0, "f1in", "f1out")
                norm(L, 1)
                for n in range(9):
                    split(L, 0, UNITS["win"] + n + 1)
                    if n == 1:
                        act.wait_ge(acc_ready, passed(L, 0, TURNS["win"] + 1))
                        act.activation(conv_gate[:, :, :], G[:, (TURNS["win"] + 1) % 2, :, 0:T], ACT.Sigmoid).then_inc(gate_ready, 1)
                act.wait_ge(acc_ready, passed(L, 0, TURNS["win"] + 8))
                for j in range(4):
                    act.wait_ge(acc_free, passed(L, 0, TURNS["win"] + 3 + j))
                    act.activation(squares[:, 2 * j:2 * j + 2, :], z[:, 2 * j:2 * j + 2, :], ACT.Square).then_inc(zsq_ready, 1)
                for j in range(4):
                    t = TURNS["qk_stat"] + j
                    act.wait_ge(acc_ready, passed(L, 0, t))
                    if j >= 2:
                        act.wait_ge(z_normed, L * 4 + j - 1)
                    act.activation(rq[:, j % 2, :, :], G[:, t % 2, :, 0:T], ACT.Sqrt, bias=eps, scale=1.0 / DH).then_inc(rq_ready, 1)

                def key_half(L, t, n, out):
                    act.wait_ge(acc_ready, passed(L, 0, t))
                    copy(out, G[:, t % 2, 0, :]).then_inc(kt_half, 1)

                for b in range(SAMPLES):
                    if b >= 2:
                        act.wait_ge(score_done, L * 16 + b - 1)
                    key_half(L, TURNS["att_k"] + b, b, att_kt[:, b % 2, 0:2, :].rearrange("p h c -> p (h c)"))
                for h in range(HEADS):
                    act.wait_ge(p_bias, L * 2 + 1)
                    for c, s in ((0, slice(0, 128)), (1, slice(128, 384))):
                        act.activation(probs[:, h, s], probs[:, h, s], ACT.Exp, bias=sm(16 + 2 * h + c), scale=DH ** -0.5,
                                       accum_out=sm(24 + 2 * h + c)).then_inc(p_exp, 1)
                act.wait_ge(s_bias, L * 2 + 1)
                act.activation(sprobs[:, :], sprobs[:, :], ACT.Exp, bias=sm(5), scale=DH ** -0.5, accum_out=sm(6)).then_inc(s_exp, 1)
                act.wait_ge(ln_centred, L + 1)
                act.activation(conv_sq[:, :, :], conv_acc[:, :, :], ACT.Square).then_inc(ln_sq, 1)
                act.wait_ge(ln_var, L + 1)
                act.activation(norm_r[:, :], M[:, STAT, 0:T], ACT.Sqrt, bias=eps, scale=1.0 / CONV_W).then_inc(ln_root, 1)
                act.wait_ge(ln_out, L + 1)
                act.activation(conv_act[:, :, :], conv_acc[:, :, :], ACT.Silu).then_inc(conv_silu, 1)
                for n in range(4):
                    split(L, 0, UNITS["wout"] + n + 1)
                norm(L, 2)
                for n in range(4):
                    split(L, 0, UNITS["cq"] + n + 1)
                for n in range(8):
                    t = TURNS["ckv"] + n
                    split(L, 0, UNITS["ckv"] + n + 1)
                    if n < HEADS:
                        for c in range(2):
                            act.wait_ge(acc_ready, passed(L, 0, t))
                            act.activation(G[:, t % 2, c, 256:512], G[:, t % 2, c, 0:MDH], ACT.Square,
                                           accum_out=sm(32 + 4 * c + n)).then_inc(mk_sq, 1)
                act.drain()
                act.activation(sm(40, 8), sm(32, 8), ACT.Sqrt, bias=eps, scale=1.0 / MDH).then_inc(mk_root, 1)
                for j in range(4):
                    act.wait_ge(acc_free, passed(L, 0, TURNS["cq"] + j))
                    act.activation(squares[:, 2 * j:2 * j + 2, :], z[:, 2 * j:2 * j + 2, :], ACT.Square).then_inc(zsq_ready, 1)
                for j in range(2):
                    t = TURNS["cq_stat"] + j
                    act.wait_ge(acc_ready, passed(L, 0, t))
                    act.activation(rq[:, j % 2, :, :], G[:, t % 2, :, 0:T], ACT.Sqrt, bias=eps, scale=1.0 / MDH).then_inc(rq_ready, 1)
                for b in range(SAMPLES):
                    for half in range(2):
                        if b >= 2 and half == 0:
                            act.wait_ge(score_done, L * 16 + SAMPLES + b - 1)
                        key_half(L, TURNS["mem_k"] + 2 * b + half, b,
                                 mem_kt[:, b % 2, 4 * half:4 * half + 2, :].rearrange("p h c -> p (h c)"))
                act.wait_ge(s_bias, L * 2 + 2)
                act.activation(cx_sprobs[:, :], M[:, SCORES, 0:N_MEM], ACT.Exp, bias=sm(5), scale=MDH ** -0.5, accum_out=sm(6)).then_inc(s_exp, 1)
                for j in range(2):
                    t = TURNS["cx_s"] + j
                    act.wait_ge(cx_bias, L * 2 + j + 1)
                    for e in range(2):
                        h = 2 * j + e
                        for c in range(2):
                            act.activation(cx_probs[:, h, 256 * c:256 * c + 256], G[:, t % 2, e, 256 * c:256 * c + 256], ACT.Exp,
                                           bias=sm(16 + 2 * h + c), scale=MDH ** -0.5, accum_out=sm(24 + 2 * h + c)).then_inc(p_exp, 1)
                for n in range(4):
                    split(L, 0, UNITS["co"] + n + 1)
                norm(L, 3)
                ffn(L, 0, "f2in", "f2out")


        @block.vector
        def _(dve):
            def tt(out, in0, in1, op):
                return dve.tensor_tensor(out, in0, in1, op)

            def stt(out, in0, scalar, in1, op0, op1):
                return dve.scalar_tensor_tensor(out, in0, scalar, in1, op0, op1)

            def split(L, i, u):
                n = chunks_of(u) * 128
                for half in range(2):
                    s = slice(half * n, half * n + n)
                    dve.wait_ge(hi_ready, half_value(L, i, u, half))
                    tt(w_lo[:, u % 2, s], raw[:, u % 2, s], w_hi[:, u % 2, s].bitcast(F32), ALU.subtract
                       ).then_inc(lo_ready, half_inc(u, half))

            def hi_lo(items, done, first_step=None):
                n = len(items)
                for k in range(n + 2):
                    if k < n and items[k][0] is not None:
                        items[k][0]()
                    if 1 <= k <= n:
                        _, src, hi, lo = items[k - 1]
                        dve.tensor_copy(hi, src)
                    if k >= 2:
                        _, src, hi, lo = items[k - 2]
                        done(tt(lo, src, hi.bitcast(F32), ALU.subtract), k - 2)
                    if k < n + 1:
                        dve.drain()

            def norm(L, n, gain):
                dve.wait_ge(root_ready, L * 4 + n + 1)
                dve.reciprocal(norm_r[:, :], norm_r[:, :])
                dve.drain()

                def step(k):
                    return lambda: stt(norm_tmp[:, k, :], x[:, k, :], par(gain, k), norm_r[:, :], ALU.mult, ALU.mult)

                hi_lo([(step(k), norm_tmp[:, k, :], h_hi[:, k, :], h_lo[:, k, :]) for k in range(KD)],
                      lambda ins, k: ins.then_inc(h_ready, 1))

            def free(ins):
                return ins.then_inc(acc_free, 1)

            def acc(L, t, i=0):
                dve.wait_ge(acc_ready, passed(L, i, t))
                return G[:, t % 2, :, :]

            def residual(L, t, m, scale):
                pair = acc(L, t)
                free(stt(x[:, 2 * m:2 * m + 2, :], pair[:, :, 0:T], scale, x[:, 2 * m:2 * m + 2, :], ALU.mult, ALU.add))

            def ffn(L, which, fin, fout):
                u0, t0 = UNITS[fin], TURNS[fin]
                with dve.Fori(0, KF // 2) as i:
                    for j in range(2):
                        split(L, i, u0 + j + 1)
                        b = (t0 + j) % 2
                        dve.wait_ge(silu_ready, L * (2 * KF) + i * 2 + (which * KF + j + 1))
                        pair = acc(L, t0 + j, i)
                        free(tt(silu[:, b, :], silu[:, b, :], pair[:, 1, 0:T], ALU.mult))
                        dve.drain()
                        m = i * 2 + j
                        hi = g_hi[:, bass.ds(m, 1), :].rearrange("p o t -> p (o t)")
                        lo = g_lo[:, bass.ds(m, 1), :].rearrange("p o t -> p (o t)")
                        dve.tensor_copy(hi, silu[:, b, :])
                        dve.drain()
                        tt(lo, silu[:, b, :], hi.bitcast(F32), ALU.subtract).then_inc(g_ready, 1)
                for m in range(4):
                    for n in range(3 * m + 1, 3 * m + 4):
                        if n < 12 or fout == "f1out":
                            split(L, 0, UNITS[fout] + n)
                    residual(L, TURNS[fout] + m, m, 0.5)

            dve.sem_inc(acc_free, 2)
            dve.sem_inc(lo_ready, 4)
            dve.sem_inc(mixer_idle, 1)
            dve.wait_ge(mem_sq, 1)
            dve.reciprocal(sm(3, 2), sm(3, 2))
            dve.drain()
            for c in range(2):
                dve.tensor_scalar(rows_in[:, 0, c, :], rows_in[:, 0, c, :], sm(3 + c), None, ALU.mult).then_inc(mem_norm, 1)
            for n in range(10):
                dve.wait_ge(start_turned, n + 1)
                bank = M[:, n % 4, :]
                if n == 0:
                    ins = dve.tensor_copy(prm_all[:, :, :], bank[:, 0:2 * N_PROWS].rearrange("p (l r) -> p l r", l=2))
                elif n < 9:
                    k = 2 * ((n - 1) % 4)
                    dst = mem_t[:, k:k + 2, :] if n < 5 else x[:, k:k + 2, 0:SEQ]
                    ins = dve.tensor_copy(dst, bank.rearrange("p (k t) -> p k t", k=2))
                else:
                    ins = dve.tensor_copy(x[:, :, SEQ:T], bank[:, 0:KD * TS].rearrange("p (k t) -> p k t", k=KD))
                ins.then_inc(start_taken, 1)
            dve.drain()

            with dve.Fori(0, DEPTH) as L:
                dve.tensor_copy(prm[:, :], prm_all[:, bass.ds(L, 1), :].rearrange("p o r -> p (o r)"))
                split(L, 0, 0)
                dve.drain()
                norm(L, 0, "ln_ffn1")
                ffn(L, 0, "f1in", "f1out")

                dve.memset(pxt[:, :, 0:PBUF], 0.0)
                dve.memset(cxt[:, :, 0:CBUF], 0.0)
                norm(L, 1, "ln_mix")

                def pool_new(c):
                    return pxt[:, c, PBUF + SEQ:].rearrange("p (b r) -> p b r", b=SAMPLES)

                def conv_new(c):
                    return cxt[:, c, CBUF + SEQ:].rearrange("p (b r) -> p b r", b=SAMPLES)

                pair = acc(L, TURNS["state_in"])
                for c in range(2):
                    for half in range(2):
                        dve.tensor_copy(conv_new(c)[:, 4 * half:4 * half + 4, 0:CBUF],
                                        pair[:, 0, 240 * c + 120 * half:240 * c + 120 * half + 120].rearrange("p (b r) -> p b r", b=4))
                    last = dve.tensor_copy(pool_new(c)[:, :, 0:PBUF], pair[:, 1, 120 * c:120 * c + 120].rearrange("p (b r) -> p b r", b=SAMPLES))
                free(last)
                for n in range(9):
                    split(L, 0, UNITS["win"] + n + 1)
                    dve.drain()
                    pair = acc(L, TURNS["win"] + n)
                    both = pair[:, :, 0:T]
                    if n == 0:
                        free(dve.tensor_copy(conv_a[:, :, :], both))
                    elif n == 1:
                        dve.wait_ge(gate_ready, L + 1)
                        free(tt(cxt[:, :, CBUF:CBUF + SEQ], conv_a[:, :, 0:SEQ], conv_gate[:, :, 0:SEQ], ALU.mult))
                        tt(fresh[:, 2:4, :], conv_a[:, :, SEQ:T], conv_gate[:, :, SEQ:T], ALU.mult)
                        dve.drain()
                        for c in range(2):
                            dve.tensor_copy(conv_new(c)[:, :, CBUF:], fresh[:, 2 + c, :].rearrange("p (b t) -> p b t", b=SAMPLES))
                    elif n == 2:
                        dve.tensor_copy(pxt[:, :, PBUF:PBUF + SEQ], pair[:, :, 0:SEQ])
                        dve.tensor_copy(fresh[:, 0:2, :], pair[:, :, SEQ:T])
                        for c in range(2):
                            last = dve.tensor_copy(pool_new(c)[:, :, PBUF:], pair[:, c, SEQ:T].rearrange("p (b t) -> p b t", b=SAMPLES))
                        free(last)
                    elif n < 7:
                        free(dve.tensor_copy(z[:, 2 * n - 6:2 * n - 4, :], both))
                    else:
                        free(dve.tensor_copy(v_t[:, 2 * n - 14:2 * n - 12, :], both))
                dve.drain()

                for c in range(2):
                    e = pxt[:, c, :]
                    low, high = slice(0, 64), slice(64, P)
                    inv = cc("inv_count").rearrange("p (c t) -> p c t", c=2)[:, c, :]
                    tt(win_a[:, 1:], e[:, 1:], e[:, :-1], ALU.add)
                    dve.drain()
                    if c == 0:
                        sums = {0: win_a, 1: win_b}
                        tt(win_b[high, 3:], win_a[high, 3:], win_a[high, 1:-2], ALU.add)
                        dve.drain()
                    else:
                        tt(win_b[:, 3:], win_a[:, 3:], win_a[:, 1:-2], ALU.add)
                        dve.drain()
                        tt(win_c[:, 7:], win_b[:, 7:], win_b[:, 3:-4], ALU.add)
                        dve.drain()
                        tt(win_a[high, 15:], win_c[high, 15:], win_c[high, 7:-8], ALU.add)
                        sums = {0: win_c, 1: win_a}
                        dve.drain()
                    for g, s in enumerate((low, high)):
                        w = slice(PBUF, PX)
                        tt(sums[g][s, w], sums[g][s, w], inv[s, w], ALU.mult)
                    dve.drain()
                    for g, s in enumerate((low, high)):
                        w = slice(PBUF, PX)
                        last = tt(pool_diff(c)[s, w], sums[g][s, w], e[s, w], ALU.subtract)
                    dve.drain()
                last.then_inc(pooled, 1)
                dve.sem_inc(fresh_ready, 1)

                for j in range(4):
                    t = TURNS["qk_stat"] + j
                    dve.wait_ge(rq_ready, L * 6 + j + 1)
                    acc(L, t)
                    free(dve.reciprocal(rq[:, j % 2, :, :], rq[:, j % 2, :, :]))
                    dve.drain()
                    gain = par("att_q_norm" if j < 2 else "att_k_norm")
                    stt(z[:, 2 * j:2 * j + 2, :], z[:, 2 * j:2 * j + 2, :], gain, rq[:, j % 2, :, :], ALU.mult, ALU.mult
                        ).then_inc(z_normed, 1)
                dve.drain()
                for j in range(4):
                    pair = acc(L, TURNS["rope"] + j)
                    turned = z[0:ROPE_DIM, 2 * j:2 * j + 2, :]
                    cos2 = ap(const, COLS["cos"][0], [[0, 2], [1, T]], ROPE_DIM)
                    sin2 = ap(const, COLS["sin"][0], [[0, 2], [1, T]], ROPE_DIM)
                    free(tt(rope_tmp[0:ROPE_DIM, :, :], pair[0:ROPE_DIM, :, 0:T], sin2, ALU.mult))
                    tt(turned, turned, cos2, ALU.mult)
                    dve.drain()
                    tt(turned, turned, rope_tmp[0:ROPE_DIM, :, :], ALU.add).then_inc(z_done, 1)
                    dve.drain()
                spread_q(dve, att=True)
                pair = acc(L, TURNS["pool"])
                free(dve.tensor_copy(mix_tmp[:, :, :], pair[:, :, 0:T]))
                dve.drain()

                def scaled(c):
                    return lambda: dve.tensor_scalar(mix_tmp[:, c, :], mix_tmp[:, c, :], par("pool_scale", c), None, ALU.mult)

                hi_lo([(scaled(c), mix_tmp[:, c, :], y_hi[:, c, :], y_lo[:, c, :]) for c in range(2)],
                      lambda ins, k: ins.then_inc(y_ready, 1))
                pair = acc(L, TURNS["state_out"])
                dve.tensor_copy(sstate[0:TS, :], pair[0:TS, 0, :])
                dve.tensor_copy(pstate[0:PBUF, 0, :], pair[0:PBUF, 1, 0:256])
                free(dve.tensor_copy(pstate[0:CBUF, 1, :], pair[0:CBUF, 1, 256:512]))
                for c in range(3):
                    n = P if c < 2 else TS
                    pair = acc(L, TURNS["tok"] + c)
                    dve.tensor_copy(k_tok[0:n, c, :], pair[0:n, 0, :])
                    last = dve.tensor_copy(v_tok[0:n, c, :], pair[0:n, 1, :])
                    free(last)

                def taps(j0, j1):
                    for j in range(j0, j1):
                        w = PROWS["conv_dw_w"][0] + 2 * j
                        for c in range(2):
                            ins_outs = ((conv_acc[:, c, 0:SEQ], cxt[:, c, j:j + SEQ]),
                                        (conv_acc[:, c, SEQ:T].rearrange("p (b t) -> p b t", b=SAMPLES), conv_new(c)[:, :, j:j + NEW]))
                            for out, src in ins_outs:
                                if j == 0:
                                    dve.tensor_scalar(out, src, prm[:, w + c:w + c + 1], par("conv_dw_b", c), ALU.mult, ALU.add)
                                else:
                                    last = stt(out, src, prm[:, w + c:w + c + 1], out, ALU.mult, ALU.add)
                        dve.drain()
                    return last

                for b in range(SAMPLES):
                    pair = acc(L, TURNS["att_k"] + b)
                    if b >= 2:
                        dve.wait_ge(score_done, L * 16 + b - 1)
                    dve.wait_ge(kt_half, L * 24 + b + 1)
                    free(dve.tensor_copy(att_kt[:, b % 2, 2:4, :].rearrange("p h c -> p (h c)"), pair[:, 1, :]))
                    taps(4 * b, min(4 * b + 4, CONV_K))
                dve.sem_inc(conv_done, 1)

                for j in range(2):
                    pair = acc(L, TURNS["att_s"] + j)
                    blocks = pair.rearrange("p e (n c) -> p e n c", n=2)[:, :, :, 0:P]
                    causal4 = ap(const, COLS["causal"][0], [[0, 2], [0, 2], [1, P]])
                    out = ap(probs, 2 * j * 384, [[384, 2], [256, 2], [1, P]])
                    tt(out, blocks, causal4, ALU.add)
                    free(dve.tensor_copy(probs[:, 2 * j:2 * j + 2, P:2 * P], pair[:, :, P:2 * P]))
                dve.drain()
                peak = small[:, 72:80].rearrange("p (h c) -> p h c", c=2)
                dve.tensor_reduce(peak[:, :, 0], probs[:, :, 0:P], AX.X, ALU.max, negate=True)
                dve.tensor_reduce(peak[:, :, 1], probs[:, :, P:384], AX.X, ALU.max, negate=True)
                dve.drain()
                dve.tensor_scalar(sm(16, 8), sm(72, 8), DH ** -0.5, None, ALU.mult).then_inc(p_bias, 2)

                dve.wait_ge(news_done, L + 1)
                dve.tensor_copy(sprobs[:, 0:PAST], M[:, SCORES, 0:PAST])
                tt(sprobs[:, PAST:], M[:, NEWS, 0:TS], cc("own"), ALU.add)
                dve.drain()
                dve.tensor_reduce(sm(64), sprobs[:, :], AX.X, ALU.max, negate=True)
                dve.drain()
                dve.tensor_scalar(sm(5), sm(64), DH ** -0.5, None, ALU.mult).then_inc(s_bias, 1)
                dve.wait_ge(ln_sum, L + 1)
                for c in range(2):
                    last = stt(conv_acc[:, c, :], M[:, STAT, 0:T], -1.0 / CONV_W, conv_acc[:, c, :], ALU.mult, ALU.add)
                last.then_inc(ln_centred, 1)
                normalise_probs(dve, L, p_exp, L * 16 + 8, probs, (slice(0, P), slice(P, 384)), p_probs)
                for j in range(2):
                    pair = acc(L, TURNS["att_pt"] + j)
                    free(dve.tensor_copy(probs_t[:, 2 * j:2 * j + 2, :], pair[:, :, 0:384]))
                dve.wait_ge(s_exp, L * 2 + 1)
                dve.reciprocal(sm(7), sm(6))
                dve.drain()
                dve.tensor_scalar(sprobs[:, :], sprobs[:, :], sm(7), None, ALU.mult).then_inc(s_probs, 1)
                dve.wait_ge(s_turned, L * 2 + 1)
                dve.tensor_copy(sprobs_t[:, 0:PAST], M[:, TP, 0:PAST])
                dve.tensor_copy(sprobs_t[0:TS, PAST:384], M[0:TS, TP, PAST:384]).then_inc(s_probs_t, 1)
                dve.drain()
                for j in range(2):
                    pair = acc(L, TURNS["att_o"] + j)
                    s = slice(4 + 2 * j, 6 + 2 * j)
                    dve.tensor_copy(y_hi[:, s, 0:SEQ], pair[:, :, 0:SEQ])
                    dve.drain()
                    free(tt(y_lo[:, s, 0:SEQ], pair[:, :, 0:SEQ], y_hi[:, s, 0:SEQ].bitcast(F32), ALU.subtract))
                dve.wait_ge(ln_root, L + 1)
                dve.reciprocal(norm_r[:, :], norm_r[:, :])
                dve.drain()
                for c in range(2):
                    stt(conv_acc[:, c, :], conv_acc[:, c, :], par("conv_ln_g", c), norm_r[:, :], ALU.mult, ALU.mult)
                dve.drain()
                for c in range(2):
                    last = dve.tensor_scalar(conv_acc[:, c, :], conv_acc[:, c, :], par("conv_ln_b", c), None, ALU.add)
                last.then_inc(ln_out, 1)
                dve.wait_ge(v_used, L * 16 + 8)
                new = M[:, NEWS, 0:HEADS * TS].rearrange("p (h t) -> p h t", h=HEADS)
                dve.tensor_copy(y_hi[:, 4:8, SEQ:T], new)
                dve.drain()
                tt(y_lo[:, 4:8, SEQ:T], new, y_hi[:, 4:8, SEQ:T].bitcast(F32), ALU.subtract).then_inc(y_ready, 1)
                pair = acc(L, TURNS["pw"])
                for c in range(2):
                    last = dve.tensor_scalar(mix_tmp[:, c, :], pair[:, c, 0:T], par("conv_pw_b", c), None, ALU.add)
                free(last)
                dve.drain()
                hi_lo([(None, mix_tmp[:, c, :], y_hi[:, 2 + c, :], y_lo[:, 2 + c, :]) for c in range(2)],
                      lambda ins, k: ins.then_inc(y_ready, 1))
                for n in range(4):
                    split(L, 0, UNITS["wout"] + n + 1)
                    residual(L, TURNS["wout"] + n, n, 1.0)

                norm(L, 2, "ln_cross")
                dve.drain()

                def gained(k):
                    return lambda: dve.tensor_scalar(mix_mem(k), mem_t[:, k, :], par("ln_mem", k), None, ALU.mult)

                def mix_mem(k):
                    return mix_tmp[:, k % 2, 0:N_MEM]

                for n in range(4):
                    split(L, 0, UNITS["cq"] + n + 1)
                    pair = acc(L, TURNS["cq"] + n)
                    if n == 0:
                        dve.wait_ge(tiles_free, 2 * L + 1)
                    free(dve.tensor_copy(z[:, 2 * n:2 * n + 2, :], pair[:, :, 0:T]))
                    if n == 0:
                        for k in range(KD):
                            gained(k)()
                            dve.drain()
                            dve.tensor_copy(y_hi[:, k, 0:N_MEM], mix_mem(k))
                            dve.drain()
                            tt(y_lo[:, k, 0:N_MEM], mix_mem(k), y_hi[:, k, 0:N_MEM].bitcast(F32), ALU.subtract).then_inc(m_ready, 1)
                for n in range(8):
                    split(L, 0, UNITS["ckv"] + n + 1)
                    pair = acc(L, TURNS["ckv"] + n)
                    if n < HEADS:
                        dve.wait_ge(mk_sq, L * 8 + 2 * n + 2)
                        free(dve.tensor_copy(mk[:, :, n * MDH:(n + 1) * MDH], pair[:, :, 0:MDH]))
                    else:
                        last = dve.tensor_copy(mv[:, :, (n - HEADS) * MDH:(n - HEADS + 1) * MDH], pair[:, :, 0:MDH])
                        free(last)
                dve.wait_ge(mk_root, L + 1)
                dve.reciprocal(sm(56, 8), sm(40, 8))
                dve.drain()
                for c in range(2):
                    for h in range(HEADS):
                        s = slice(h * MDH, (h + 1) * MDH)
                        stt(mk[:, c, s], mk[:, c, s], sm(56 + 4 * c + h), ck_gain[:, :], ALU.mult, ALU.mult).then_inc(mk_ready, 1)
                for j in range(2):
                    dve.wait_ge(rq_ready, L * 6 + 4 + j + 1)
                    acc(L, TURNS["cq_stat"] + j)
                    free(dve.reciprocal(rq[:, j, :, :], rq[:, j, :, :]))
                    dve.drain()
                    for h in (2 * j, 2 * j + 1):
                        for d in range(2):
                            last = stt(z[:, 2 * h + d, :], z[:, 2 * h + d, :], par("cq_norm", d), rq[:, j, h % 2, :], ALU.mult, ALU.mult)
                last.then_inc(z_done, 1)
                dve.drain()
                spread_q(dve, att=False)
                for j in range(2):
                    pair = acc(L, TURNS["mkt"] + j)
                    free(dve.tensor_copy(mkt[:, 4 * j:4 * j + 4, :].rearrange("p (e k) t -> p e k t", e=2),
                                         pair.rearrange("p e (k t) -> p e k t", k=2)))
                for b in range(SAMPLES):
                    for half in range(2):
                        pair = acc(L, TURNS["mem_k"] + 2 * b + half)
                        if b >= 2 and half == 0:
                            dve.wait_ge(score_done, L * 16 + SAMPLES + b - 1)
                        dve.wait_ge(kt_half, L * 24 + SAMPLES + 2 * b + half + 1)
                        free(dve.tensor_copy(mem_kt[:, b % 2, 4 * half + 2:4 * half + 4, :].rearrange("p h c -> p (h c)"), pair[:, 1, :]))
                dve.wait_ge(score_done, L * 16 + 2 * SAMPLES)
                dve.tensor_reduce(sm(64), M[:, SCORES, 0:N_MEM], AX.X, ALU.max, negate=True)
                dve.drain()
                dve.tensor_scalar(sm(5), sm(64), MDH ** -0.5, None, ALU.mult).then_inc(s_bias, 1)
                for j in range(2):
                    pair = acc(L, TURNS["cx_s"] + j)
                    dve.tensor_reduce(small[:, 72 + 4 * j:76 + 4 * j].rearrange("p (e c) -> p e c", e=2),
                                      pair.rearrange("p e (c t) -> p e c t", c=2), AX.X, ALU.max, negate=True)
                    dve.drain()
                    dve.tensor_scalar(sm(16 + 4 * j, 4), sm(72 + 4 * j, 4), MDH ** -0.5, None, ALU.mult).then_inc(cx_bias, 1)
                for j in range(2):
                    dve.wait_ge(p_exp, L * 16 + 8 + 4 * j + 4)
                    free(dve.reciprocal(sm(48 + 4 * j, 4), sm(24 + 4 * j, 4)))
                dve.drain()
                for h in range(HEADS):
                    for c in range(2):
                        s = slice(256 * c, 256 * c + 256)
                        dve.tensor_scalar(cx_probs[:, h, s], cx_probs[:, h, s], sm(48 + 2 * h + c), None, ALU.mult).then_inc(p_probs, 1)
                for j in range(2):
                    pair = acc(L, TURNS["cx_pt"] + j)
                    free(dve.tensor_copy(cx_probs_t[:, 2 * j:2 * j + 2, :], pair))
                dve.wait_ge(s_exp, L * 2 + 2)
                dve.reciprocal(sm(7), sm(6))
                dve.drain()
                dve.tensor_scalar(cx_sprobs[:, :], cx_sprobs[:, :], sm(7), None, ALU.mult).then_inc(s_probs, 1)
                dve.wait_ge(s_turned, L * 2 + 2)
                dve.tensor_copy(cx_sprobs_t[:, :], M[:, TP, 0:N_MEM]).then_inc(s_probs_t, 1)
                for j in range(2):
                    pair = acc(L, TURNS["cx_o"] + j).rearrange("p e (k t) -> p e k t", k=2)
                    hi = y_hi[:, 4 * j:4 * j + 4, 0:SEQ].rearrange("p (e k) t -> p e k t", e=2)
                    lo = y_lo[:, 4 * j:4 * j + 4, 0:SEQ].rearrange("p (e k) t -> p e k t", e=2)
                    dve.tensor_copy(hi, pair)
                    dve.drain()
                    free(tt(lo, pair, hi.bitcast(F32), ALU.subtract))
                dve.wait_ge(v_used, L * 16 + 16)
                new = M[:, NEWS, 0:KD * TS].rearrange("p (k t) -> p k t", k=KD)
                dve.tensor_copy(y_hi[:, :, SEQ:T], new)
                dve.drain()
                tt(y_lo[:, :, SEQ:T], new, y_hi[:, :, SEQ:T].bitcast(F32), ALU.subtract).then_inc(y_ready, 1)
                for n in range(4):
                    split(L, 0, UNITS["co"] + n + 1)
                    residual(L, TURNS["co"] + n, n, 1.0)
                dve.sem_inc(mixer_idle, 1)
                dve.wait_ge(tiles_free, 2 * L + 2)
                norm(L, 3, "ln_ffn2")
                ffn(L, 1, "f2in", "f2out")

            for c in range(3):
                n = P if c < 2 else TS
                dve.wait_ge(start_turned, 10 + c + 1)
                dve.tensor_copy(y_rows[0:n, c, :].rearrange("p (b d) -> p b d", b=2), M[0:n, 2 * (c % 2):2 * (c % 2) + 2, :]
                                ).then_inc(rows_ready, 1)

        @block.tensor
        def _(pe):
            def mm(out, lhsT, rhs, start=True, stop=True, **kw):
                return pe.matmul(out, lhsT, rhs, start=start, stop=stop, **kw)

            def take(L, t, i=0):
                pe.wait_ge(acc_free, turn_value(L, i, t))
                return G[:, t % 2, :, :]

            def unit(L, i, u, pair, rhs, first=True, last=True, nk=8, k0=0, tokens=T, wait=None):
                for k in range(nk):
                    if k % (nk // 2) == 0:
                        pe.wait_ge(lo_ready, half_value(L, i, u, k // (nk // 2)) + 4)
                    if wait is not None:
                        wait(k0 + k)
                    r_hi, r_lo = rhs(k0 + k)
                    for m in range(2):
                        s = slice((2 * k + m) * P, (2 * k + m + 1) * P)
                        out = pair[:, m, 0:tokens]
                        mm(out, w_hi[:, u % 2, s], r_hi, first and k == 0, False)
                        mm(out, w_hi[:, u % 2, s], r_lo, False, False)
                        ins = mm(out, w_lo[:, u % 2, s], r_hi, False, last and k == nk - 1)
                return ins.then_inc(acc_ready if last else unit_used, 1)

            def norm(L, n):
                for k in range(KD):
                    pe.wait_ge(sq_ready, L * 32 + 8 * n + k + 1)
                    ins = mm(M[:, STAT, 0:T], ones[:, :], squares[:, k, :], k == 0, k == KD - 1)
                ins.then_inc(stat_ready, 1)

            def h(k):
                return h_hi[:, k, :], h_lo[:, k, :]

            def h_wait(L, n):
                return lambda k: pe.wait_ge(h_ready, L * 32 + 8 * n + k + 1)

            def ffn(L, which, n, fin, fout):
                norm(L, n)
                with pe.Fori(0, KF // 2) as i:
                    for j in range(2):
                        pair = take(L, TURNS[fin] + j, i)
                        unit(L, i, UNITS[fin] + j, pair, h, wait=h_wait(L, n))
                for m in range(4):
                    pair = take(L, TURNS[fout] + m)
                    for q, nk in enumerate(OUT_PARTS):
                        unit(L, 0, UNITS[fout] + 3 * m + q, pair, lambda k: (g_hi[:, k, :], g_lo[:, k, :]),
                                   q == 0, q == 2, nk, 8 * q,
                                   wait=(lambda k: pe.wait_ge(g_ready, L * (2 * KF) + which * KF + k + 1)) if m == 0 else None)

            def turn(out, in_, n=P):
                return pe.transpose(out, in_, ident[0:n, 0:n])

            pe.sem_inc(acc_ready, 2)
            pe.wait_ge(const_landed, 16)
            pe.wait_ge(fills_done, 4)
            pe.wait_ge(rows_landed, 16 * len(PROWS))
            for layer in range(DEPTH):
                ins = turn(M[:, 0, layer * N_PROWS:(layer + 1) * N_PROWS], param_rows[0:N_PROWS, layer, :], N_PROWS)
            ins.then_inc(start_turned, 1)
            for n in range(1, 9):
                src = 0 if n < 5 else 1
                pe.wait_ge(mem_norm, 2) if n < 5 else pe.wait_ge(x_landed, 32)
                if n >= 4:
                    pe.wait_ge(start_taken, n - 3)
                for e in range(2):
                    k = 2 * ((n - 1) % 4) + e
                    for c in range(2):
                        ins = turn(M[:, n % 4, 256 * e + P * c:256 * e + P * c + P], rows_in[:, src, c, k * P:(k + 1) * P])
                ins.then_inc(start_turned, 1)
            pe.wait_ge(start_taken, 6)
            for k in range(KD):
                ins = turn(M[:, 1, k * TS:(k + 1) * TS], x_sample_rows[:, k * P:(k + 1) * P], TS)
            ins.then_inc(start_turned, 1)
            pe.wait_ge(start_taken, 10)

            with pe.Fori(0, DEPTH) as L:
                ffn(L, 0, 0, "f1in", "f1out")
                norm(L, 1)
                pair = take(L, TURNS["state_in"])
                pe.wait_ge(states_in, L * 32 + 32)
                for c in range(2):
                    for half in range(2):
                        turn(pair[:, 0, 240 * c + 120 * half:240 * c + 120 * half + 120], conv_rows[0:120, half, c * P:(c + 1) * P], 120)
                    ins = turn(pair[:, 1, 120 * c:120 * c + 120], pool_rows[0:120, c * P:(c + 1) * P], 120)
                ins.then_inc(acc_ready, 1)
                for n in range(9):
                    pair = take(L, TURNS["win"] + n)
                    unit(L, 0, UNITS["win"] + n, pair, h, wait=h_wait(L, 1))
                for j in range(4):
                    pair = take(L, TURNS["qk_stat"] + j)
                    pe.wait_ge(zsq_ready, L * 8 + j + 1)
                    for e in range(2):
                        ins = mm(pair[:, e, 0:T], ones[:, :], squares[:, 2 * j + e, :])
                    ins.then_inc(acc_ready, 1)
                for j in range(4):
                    pair = take(L, TURNS["rope"] + j)
                    pe.wait_ge(z_normed, L * 4 + j + 1)
                    for e in range(2):
                        ins = mm(pair[0:ROPE_DIM, e, 0:T], cc("swap"), z[:, 2 * j + e, :])
                    ins.then_inc(acc_ready, 1)
                pair = take(L, TURNS["pool"])
                pe.wait_ge(pooled, L + 1)
                pe.wait_ge(mixer_params, L * 96 + 96)
                for c in range(2):
                    d = pool_diff(c)
                    mm(pair[:, c, 0:SEQ], pool_w[:, c, :], d[:, PBUF:PBUF + SEQ])
                    new = d[:, PBUF + SEQ:].rearrange("p (b r) -> p b r", b=SAMPLES)[:, :, PBUF:]
                    ins = mm(pair[:, c, SEQ:T].rearrange("p (b t) -> p b t", b=SAMPLES), pool_w[:, c, :], new)
                ins.then_inc(acc_ready, 1)
                pair = take(L, TURNS["state_out"])
                pe.wait_ge(fresh_ready, L + 1)
                for k in range(4):
                    turn(pair[0:TS, 0, k * P:(k + 1) * P], fresh[:, k, :])
                for c in range(2):
                    turn(pair[0:PBUF, 1, c * P:(c + 1) * P], pxt[:, c, SEQ:SEQ + PBUF])
                    ins = turn(pair[0:CBUF, 1, 256 + c * P:256 + (c + 1) * P], cxt[:, c, SEQ:SEQ + CBUF])
                ins.then_inc(acc_ready, 1)
                pe.wait_ge(z_done, L * 5 + 4)
                for c in range(3):
                    pair = take(L, TURNS["tok"] + c)
                    n = P if c < 2 else TS
                    for hd in range(HEADS):
                        turn(pair[0:n, 0, hd * P:(hd + 1) * P], z[:, HEADS + hd, c * P:c * P + n])
                        ins = turn(pair[0:n, 1, hd * P:(hd + 1) * P], v_t[:, hd, c * P:c * P + n])
                    ins.then_inc(acc_ready, 1)

                def rows32(b):
                    return slice(32 * (b // 2), 32 * (b // 2) + 32)

                def att_scores(b):
                    pe.wait_ge(acc_free, passed(L, 0, TURNS["att_k"] + b))
                    for hd in range(HEADS):
                        ins = mm(M[rows32(b), SCORES, 0:PAST], q_diag[:, 0, b * HEADS + hd, :], att_kt[:, b % 2, hd, :],
                                 b % 2 == 0 and hd == 0, b % 2 == 1 and hd == HEADS - 1, skip_group_check=True)
                    ins.then_inc(score_done, 1)

                for b in range(SAMPLES):
                    pair = take(L, TURNS["att_k"] + b)
                    pe.wait_ge(kv_landed[b % 2], kv_value(L, b))
                    for hd in range(HEADS):
                        for c in range(PAGES):
                            col = 256 * (hd % 2) + P * c
                            ins = turn(pair[:, hd // 2, col:col + P], att_kv[:, b % 2, c, hd * P:(hd + 1) * P])
                    ins.then_inc(acc_ready, 1)
                    if b == 0:
                        pe.wait_ge(q_diag_ready, L * 2 + 1)
                    else:
                        att_scores(b - 1)
                att_scores(SAMPLES - 1)
                for b in range(SAMPLES):
                    for hd in range(HEADS):
                        ins = mm(M[rows32(b), NEWS, 0:TS], q_diag[:, 0, b * HEADS + hd, :], z[:, HEADS + hd, SEQ:T],
                                 b % 2 == 0 and hd == 0, b % 2 == 1 and hd == HEADS - 1, skip_group_check=True)
                ins.then_inc(news_done, 1)
                for j in range(2):
                    pair = take(L, TURNS["att_s"] + j)
                    for e in range(2):
                        hd = 2 * j + e
                        mm(pair[:, e, 0:P], z[:, hd, 0:P], z[:, HEADS + hd, 0:P])
                        ins = mm(pair[:, e, P:384], z[:, hd, P:SEQ], z[:, HEADS + hd, 0:SEQ])
                    ins.then_inc(acc_ready, 1)
                pe.wait_ge(conv_done, L + 1)
                for c in range(2):
                    ins = mm(M[:, STAT, 0:T], ones[:, :], conv_acc[:, c, :], c == 0, c == 1)
                ins.then_inc(ln_sum, 1)
                pe.wait_ge(ln_sq, L + 1)
                for c in range(2):
                    ins = mm(M[:, STAT, 0:T], ones[:, :], conv_sq[:, c, :], c == 0, c == 1)
                ins.then_inc(ln_var, 1)
                for j in range(2):
                    pair = take(L, TURNS["att_pt"] + j)
                    pe.wait_ge(p_probs, L * 16 + 4 * j + 4)
                    for e in range(2):
                        hd = 2 * j + e
                        turn(pair[:, e, 0:P], probs[:, hd, 0:P])
                        turn(pair[:, e, P:2 * P], probs[:, hd, P:2 * P])
                        ins = turn(pair[:, e, 2 * P:3 * P], probs[:, hd, 2 * P:3 * P])
                    ins.then_inc(acc_ready, 1)
                pe.wait_ge(s_probs, L * 2 + 1)
                for c in range(2):
                    turn(M[:, TP, c * P:(c + 1) * P], sprobs[:, c * P:(c + 1) * P])
                turn(M[0:TS, TP, 2 * P:3 * P], sprobs[:, 2 * P:]).then_inc(s_turned, 1)
                for j in range(2):
                    pair = take(L, TURNS["att_o"] + j)
                    pe.wait_ge(acc_free, passed(L, 0, TURNS["att_pt"] + j))
                    for e in range(2):
                        hd = 2 * j + e
                        s = slice(hd * P, (hd + 1) * P)
                        mm(pair[:, e, 0:P], v_tok[:, 0, s], probs_t[:, hd, 0:P])
                        mm(pair[:, e, P:SEQ], v_tok[:, 0, s], probs_t[:, hd, P:SEQ], True, False)
                        ins = mm(pair[:, e, P:SEQ], v_tok[:, 1, s], probs_t[:, hd, SEQ:384], False, True)
                    ins.then_inc(acc_ready, 1)
                pe.wait_ge(s_probs_t, L * 2 + 1)
                for hd in range(HEADS):
                    mm(M[:, NEWS, hd * TS:(hd + 1) * TS].rearrange("p (b t) -> p b t", b=SAMPLES), v_tok[0:TS, 2, hd * P:(hd + 1) * P],
                       sprobs_t[0:TS, PAST:384].rearrange("p (b h t) -> p b h t", b=SAMPLES, h=HEADS)[:, :, hd, :],
                       hd == 0, False, skip_group_check=True)
                for b in range(SAMPLES):
                    n = SAMPLES + b
                    pe.wait_ge(kv_landed[n % 2], kv_value(L, n))
                    for hd in range(HEADS):
                        for c in range(PAGES):
                            col = c * P + (b * HEADS + hd) * NEW
                            ins = mm(M[:, NEWS, hd * TS + b * NEW:hd * TS + (b + 1) * NEW], att_kv[:, n % 2, c, hd * P:(hd + 1) * P],
                                     sprobs_t[:, col:col + NEW], False, c == PAGES - 1, skip_group_check=True)
                    ins.then_inc(v_used, 1)
                pair = take(L, TURNS["pw"])
                pe.wait_ge(conv_silu, L + 1)
                for m in range(2):
                    for k in range(2):
                        ins = mm(pair[:, m, 0:T], pw_w[:, k, m * P:(m + 1) * P], conv_act[:, k, :], k == 0, k == 1)
                ins.then_inc(acc_ready, 1)

                def y(k):
                    return y_hi[:, k, :], y_lo[:, k, :]

                pe.wait_ge(y_ready, L * 6 + 5)
                pe.wait_ge(acc_free, passed(L, 0, TURNS["att_o"] + 1))
                for n in range(4):
                    pair = take(L, TURNS["wout"] + n)
                    unit(L, 0, UNITS["wout"] + n, pair, y)
                norm(L, 2)
                for n in range(4):
                    pair = take(L, TURNS["cq"] + n)
                    unit(L, 0, UNITS["cq"] + n, pair, h, wait=h_wait(L, 2))
                pe.wait_ge(m_ready, L * 8 + 8)
                for n in range(8):
                    u = UNITS["ckv"] + n
                    pair = take(L, TURNS["ckv"] + n)
                    for k in range(KD):
                        if k % 4 == 0:
                            pe.wait_ge(lo_ready, half_value(L, 0, u, k // 4) + 4)
                        s = slice(k * 256, (k + 1) * 256)
                        for c in range(2):
                            tok = slice(c * P, (c + 1) * P)
                            out = pair[:, c, 0:256]
                            mm(out, y_hi[:, k, tok], w_hi[:, u % 2, s], k == 0, False)
                            mm(out, y_hi[:, k, tok], w_lo[:, u % 2, s], False, False)
                            ins = mm(out, y_lo[:, k, tok], w_hi[:, u % 2, s], False, k == KD - 1)
                    ins.then_inc(acc_ready, 1)
                for j in range(2):
                    pair = take(L, TURNS["cq_stat"] + j)
                    pe.wait_ge(zsq_ready, L * 8 + 4 + 2 * j + 2)
                    for e in range(2):
                        for d in range(2):
                            ins = mm(pair[:, e, 0:T], ones[:, :], squares[:, 4 * j + 2 * e + d, :], d == 0, d == 1)
                    ins.then_inc(acc_ready, 1)
                pe.wait_ge(mk_ready, L * 8 + 8)
                for j in range(2):
                    pair = take(L, TURNS["mkt"] + j)
                    for q in range(4):
                        for c in range(2):
                            hd = 4 * j + q
                            col = 256 * (q % 2) + P * c
                            ins = turn(pair[:, q // 2, col:col + P], mk[:, c, hd * P:(hd + 1) * P])
                    ins.then_inc(acc_ready, 1)

                def mem_scores(b):
                    pe.wait_ge(acc_free, passed(L, 0, TURNS["mem_k"] + 2 * b + 1))
                    for hd in range(KD):
                        ins = mm(M[rows32(b), SCORES, 0:N_MEM], q_diag[:, hd % 2, b * HEADS + hd // 2, :], mem_kt[:, b % 2, hd, :],
                                 b % 2 == 0 and hd == 0, b % 2 == 1 and hd == KD - 1, skip_group_check=True)
                    ins.then_inc(score_done, 1)

                for b in range(SAMPLES):
                    pe.wait_ge(kv_landed[b % 2], kv_value(L, 2 * SAMPLES + b))
                    for half in range(2):
                        pair = take(L, TURNS["mem_k"] + 2 * b + half)
                        for q in range(4):
                            for c in range(2):
                                hd = 4 * half + q
                                col = 256 * (q % 2) + P * c
                                ins = turn(pair[:, q // 2, col:col + P], mem_kv[:, b % 2, c, hd * P:(hd + 1) * P])
                        ins.then_inc(acc_ready, 1)
                    if b == 0:
                        pe.wait_ge(q_diag_ready, L * 2 + 2)
                    else:
                        mem_scores(b - 1)
                mem_scores(SAMPLES - 1)
                pe.wait_ge(acc_free, passed(L, 0, TURNS["mkt"] + 1))
                pe.wait_ge(z_done, L * 5 + 5)
                for j in range(2):
                    pair = take(L, TURNS["cx_s"] + j)
                    for e in range(2):
                        for c in range(2):
                            for d in range(2):
                                hd = 2 * (2 * j + e) + d
                                ins = mm(pair[:, e, 256 * c:256 * c + 256], z[:, hd, c * P:(c + 1) * P], mkt[:, hd, :], d == 0, d == 1)
                    ins.then_inc(acc_ready, 1)
                for j in range(2):
                    pair = take(L, TURNS["cx_pt"] + j)
                    pe.wait_ge(p_probs, L * 16 + 8 + 4 * j + 4)
                    for e in range(2):
                        for c in range(2):
                            for m in range(2):
                                ins = turn(pair[:, e, 256 * m + P * c:256 * m + P * c + P],
                                           cx_probs[:, 2 * j + e, 256 * c + P * m:256 * c + P * m + P])
                    ins.then_inc(acc_ready, 1)
                pe.wait_ge(s_probs, L * 2 + 2)
                for c in range(2):
                    ins = turn(M[:, TP, c * P:(c + 1) * P], cx_sprobs[:, c * P:(c + 1) * P])
                ins.then_inc(s_turned, 1)
                for j in range(2):
                    pair = take(L, TURNS["cx_o"] + j)
                    pe.wait_ge(acc_free, passed(L, 0, TURNS["cx_pt"] + j))
                    for e in range(2):
                        hh = 2 * j + e
                        for d in range(2):
                            s = slice((2 * hh + d) * P, (2 * hh + d + 1) * P)
                            for m in range(2):
                                ins = mm(pair[:, e, 256 * d:256 * d + 256], mv[:, m, s], cx_probs_t[:, hh, 256 * m:256 * m + 256], m == 0, m == 1)
                    ins.then_inc(acc_ready, 1)
                pe.wait_ge(s_probs_t, L * 2 + 2)
                for b in range(SAMPLES):
                    n = 3 * SAMPLES + b
                    pe.wait_ge(kv_landed[n % 2], kv_value(L, n))
                    for hd in range(KD):
                        for c in range(2):
                            col = c * P + (b * HEADS + hd // 2) * NEW
                            ins = mm(M[:, NEWS, hd * TS + b * NEW:hd * TS + (b + 1) * NEW], mem_kv[:, n % 2, c, hd * P:(hd + 1) * P],
                                     cx_sprobs_t[:, col:col + NEW], b == 0 and hd == 0 and c == 0, c == 1, skip_group_check=True)
                    ins.then_inc(v_used, 1)
                pe.wait_ge(y_ready, L * 6 + 6)
                pe.wait_ge(acc_free, passed(L, 0, TURNS["cx_o"] + 1))
                for n in range(4):
                    pair = take(L, TURNS["co"] + n)
                    unit(L, 0, UNITS["co"] + n, pair, y)
                ffn(L, 1, 3, "f2in", "f2out")

            pe.wait_ge(acc_free, N_TURNS * DEPTH + 2)
            for c in range(3):
                if c == 2:
                    pe.wait_ge(rows_ready, 1)
                n = P if c < 2 else TS
                for k in range(KD):
                    ins = turn(M[0:n, 2 * (c % 2) + k // 4, (k % 4) * P:(k % 4 + 1) * P], x[:, k, c * P:c * P + n])
                ins.then_inc(start_turned, 1)


_OUTS = {
    "y_prompt": (1, SEQ, D_MODEL), "y_sample": (SAMPLES, NEW, D_MODEL),
    "p_att_k": (DEPTH, 1, SEQ, HEADS, DH), "p_att_v": (DEPTH, 1, SEQ, HEADS, DH),
    "p_mem_k": (DEPTH, 1, N_MEM, HEADS, MDH), "p_mem_v": (DEPTH, 1, N_MEM, HEADS, MDH),
    "p_pool": (DEPTH, 1, PBUF, POOL_W), "p_conv": (DEPTH, 1, CBUF, CONV_W),
    "s_att_k": (DEPTH, SAMPLES, NEW, HEADS, DH), "s_att_v": (DEPTH, SAMPLES, NEW, HEADS, DH),
    "s_pool": (DEPTH, SAMPLES, PBUF, POOL_W), "s_conv": (DEPTH, SAMPLES, CBUF, CONV_W),
}


def kernel(**inputs):
    import numpy as _np
    import concourse.bacc as _bacc
    from concourse import mybir as _mybir
    from concourse.bass_utils import run_bass_kernel_spmd as _run

    nc = _bacc.Bacc("TRN2", target_bir_lowering=False, num_devices=1)
    arrays = {f"in_{name}": _np.ascontiguousarray(a) for name, a in inputs.items()}
    arrays["in_shape_constants"] = shape_constants()
    ins = {key[3:]: nc.dram_tensor(key, a.shape, _mybir.dt.from_np(a.dtype), kind="ExternalInput").ap() for key, a in arrays.items()}
    outs = {name: nc.dram_tensor(f"out_{name}", shape, _mybir.dt.float32, kind="ExternalOutput").ap() for name, shape in _OUTS.items()}
    trunk_kernel(nc, ins, outs)
    r = _run(nc, [arrays], core_ids=[0])
    return tuple(r.results[0][f"out_{name}"] for name in _OUTS)
```

```python
from contextlib import ExitStack

import numpy as np

import concourse.bass as bass
from concourse import mybir

F32 = mybir.dt.float32
F32R = mybir.dt.float32r
I32 = mybir.dt.int32
ACT = mybir.ActivationFunctionType
ALU = mybir.AluOpType
AX = mybir.AxisListType

P = 128
D_MODEL, SEQ, DEPTH, SAMPLES, NEW, PAST, PAGE = 1024, 256, 2, 8, 4, 256, 128
TS = SAMPLES * NEW
T = SEQ + TS
KD = D_MODEL // P
D_FF = ((8 * D_MODEL // 3 + 127) // 128) * 128
KF = D_FF // P
POOL_W, CONV_W, HEADS, DH = 256, 256, 4, 128
ATT_W = HEADS * DH
WINDOWS = (2, 4, 8, 16)
PBUF, CONV_K = max(WINDOWS) - 1, 31
CBUF = CONV_K - 1
N_MEM, MDH = 256, 256
PAGES = PAST // PAGE
ROPE_DIM, THETA = DH // 4, 500000.0
EPS = 1e-6
MASKED = -1e30
PX = PBUF + SEQ + SAMPLES * (PBUF + NEW)
CX = CBUF + SEQ + SAMPLES * (CBUF + NEW)
ROWS = SAMPLES * HEADS * NEW

COLS = {}
_at = 0
for _name, _n in (("ident", P), ("causal", P), ("own", TS), ("pick", 2 * KD - 1), ("inv_win", 2), ("inv_first", 2 * max(WINDOWS)), ("cos", T), ("sin", T), ("swap", ROPE_DIM)):
    COLS[_name] = (_at, _at + _n)
    _at += _n
N_CONST = _at

PROWS = {}
_at = 0
for _name, _n in (("ln_ffn1", 8), ("ln_mix", 8), ("ln_cross", 8), ("ln_mem", 8), ("ln_ffn2", 8), ("pool_scale", 2),
                  ("conv_dw_b", 2), ("conv_ln_g", 2), ("conv_ln_b", 2), ("conv_pw_b", 2), ("att_q_norm", 1),
                  ("att_k_norm", 1), ("cq_norm", 2), ("conv_dw_w", 2 * CONV_K)):
    PROWS[_name] = (_at, _n)
    _at += _n
N_PROWS = _at

CX_ORDER = []
for _n in range(4):
    CX_ORDER += ["ckv"] + (["cq_stat"] + ["mem_k"] * 2 + ["cq_root"] * 2 + ["mem_k"] * 2 if _n == 0 else ["mem_k"] * 4)
CX_ORDER += ["ckv", "ckv", "mkt", "mkt", "ckv", "cx_s", "cx_s", "ckv", "cx_pt", "cx_pt", "cx_o", "cx_o", "cx_so"]
MIX_ORDER = (["state_in"] + ["win"] * 5 + ["qk_stat", "win"] + ["qk_root"] * 4 + ["win"] + ["rope"] * 4 + ["att_k"] * 2
             + ["win"] + ["att_k"] * 2 + ["win"] + ["att_k"] * 4 + ["tok"] * 3 + ["att_s"] * 2 + ["pool", "state_out"]
             + ["att_pt"] * 2 + ["att_o"] * 2 + ["pw", "att_so"])
WIN_COLUMNS = (3, 4, 5, 6, 1, 2, 0, 7, 8)
UNITS, TURNS = {}, {}
_u = _t = 0
for _name, _nu, _nt in (("f1in", KF, KF), ("f1out", 12, 4), ("win", 9, 0),
                        *((_n, 0, 1) for _n in MIX_ORDER), ("wout", 4, 4),
                        ("cq", 4, 4), ("ckv", 8, 0), *((_n, 0, 1) for _n in CX_ORDER), ("co", 4, 4), ("f2in", KF, KF),
                        ("f2out", 12, 4)):
    if _nu:
        UNITS[_name] = _u
    TURNS.setdefault(_name, []).extend(range(_t, _t + _nt))
    _u += _nu
    _t += _nt
N_UNITS = _u
RING_UNITS = N_UNITS + N_UNITS % 2
N_TURNS = _t
assert N_TURNS % 2 == 0
UNIT = 2048
OUT_PARTS = (8, 8, KF - 16)


def shape_constants():
    c = np.zeros((P, N_CONST), np.float32)

    def put(name, a):
        c[:a.shape[0], COLS[name][0]:COLS[name][0] + a.shape[1]] = a

    put("ident", np.eye(P, dtype=np.float32))
    put("causal", np.where(np.arange(P)[None, :] <= np.arange(P)[:, None], 0.0, MASKED).astype(np.float32))
    rb, rt = np.arange(ROWS) // (HEADS * NEW), np.arange(ROWS) % NEW
    cb, ct = np.arange(TS) // NEW, np.arange(TS) % NEW
    ok = (rb[:, None] == cb[None, :]) & (ct[None, :] <= rt[:, None])
    put("own", np.where(ok, 0.0, MASKED).astype(np.float32))
    pick = np.zeros((P, 2 * KD - 1), np.float32)
    pick[:, KD - 1] = 1.0
    put("pick", pick)
    inv, first = np.zeros((P, 2), np.float32), np.zeros((P, 2, max(WINDOWS)), np.float32)
    for g, win in enumerate(WINDOWS):
        rows = slice(64 * (g % 2), 64 * (g % 2) + 64)
        inv[rows, g // 2] = 1.0 / win
        first[rows, g // 2, :] = 1.0 / np.minimum(np.arange(max(WINDOWS)) + 1, win)
    put("inv_win", inv)
    put("inv_first", first.reshape(P, -1))
    half = ROPE_DIM // 2
    freq = np.power(np.float32(THETA), -np.arange(half, dtype=np.float32) / np.float32(half)).astype(np.float32)
    pos = np.concatenate([np.arange(SEQ), PAST + np.arange(TS) % NEW]).astype(np.float32)
    ang = (pos[None, :] * freq[:, None]).astype(np.float32)
    put("cos", np.concatenate([np.cos(ang), np.cos(ang)]).astype(np.float32))
    put("sin", np.concatenate([-np.sin(ang), np.sin(ang)]).astype(np.float32))
    put("swap", np.roll(np.eye(ROPE_DIM, dtype=np.float32), half, axis=0))
    return c


def trunk_kernel(nc, a, o):
    with ExitStack() as ctx:
        cursor = [nc.sbuf_base + (-nc.sbuf_base) % 64]

        def at(name, shape, dt, offset):
            return nc.alloc_sbuf_tensor_at(name, [P, *shape], dt, offset=offset)

        def region(n_elems):
            start = cursor[0]
            cursor[0] += 4 * n_elems
            cursor[0] += (-cursor[0]) % 32
            return start

        def sb(name, shape, dt=F32):
            return at(name, shape, dt, region(int(np.prod(shape))))

        raw = sb("raw_weights", [2, UNIT])
        w_hi = sb("w_hi", [2, UNIT], F32R)
        w_lo = sb("w_lo", [2, UNIT], F32R)
        x = sb("x_residual", [KD, T])
        const = sb("shape_consts", [N_CONST])
        prm_all = sb("params_all", [DEPTH, N_PROWS])
        prm = sb("params", [N_PROWS])
        ck_gain = sb("ck_gain", [MDH])
        pool_w = sb("pool_w_blocks", [2, P])
        pw_w = sb("conv_pw_w", [2, CONV_W])
        mem_t = sb("mem_normed", [KD, N_MEM])
        q_diag = sb("q_diag", [2, SAMPLES * HEADS, 32])
        p_diag = sb("p_diag", [2, SAMPLES, 32])
        ones = sb("ones", [P])
        small = sb("small", [96])
        pages = nc.alloc_sbuf_tensor_at("pages", [1, SAMPLES * PAGES], I32, offset=region(SAMPLES * PAGES))
        h_at = region(2 * KD * T)
        h_hi = at("h_hi", [KD, T], F32R, h_at)
        h_lo = at("h_lo", [KD, T], F32R, h_at + 4 * KD * T)
        hh0, hl0 = h_at, h_at + 4 * KD * T
        squares = at("squares", [KD, T], F32, hl0)
        cq_rms = at("cq_rms", [T], F32, hh0)
        conv_sq = at("conv_sq", [2, T], F32, hh0 + 16 * T)
        conv_act = at("conv_act", [2, T], F32, hh0 + 24 * T)
        probs = at("att_probs", [HEADS, 384], F32, hl0)
        sprobs = at("att_sample_probs", [PAST + TS], F32, hl0 + 6144)
        new_probs_t = at("att_new_probs_t", [ROWS], F32, hl0 + 6144 + 4 * (PAST + TS))
        cx_probs = at("cx_probs", [HEADS, 512], F32, hl0)
        cx_sprobs = at("cx_sample_probs", [N_MEM], F32, hh0)
        att_out_rows = at("att_out_rows", [ATT_W], F32, hh0)
        cx_out_rows = at("cx_out_rows", [2, 512], F32, hh0 + 4 * N_MEM)
        y_at = region(2 * KD * T)
        y_hi = at("y_hi", [KD, T], F32R, y_at)
        y_lo = at("y_lo", [KD, T], F32R, y_at + 4 * KD * T)
        norm_tmp = at("norm_tmp", [KD, T], F32, y_at + 4 * KD * T)
        qk_squares = at("qk_squares", [KD, T], F32, y_at)
        qk_rms = at("qk_rms", [T], F32, y_at + 4 * KD * T)
        rope_tmp = at("rope_tmp", [2, T], F32, y_at + 4 * KD * T + 4 * T)
        mix_tmp_at = region(2 * T)
        gate_up = at("gate_up", [2, T], F32, mix_tmp_at)
        mix_tmp = at("mix_tmp", [2, T], F32, mix_tmp_at)
        norm_r = sb("norm_r", [T])
        kv_at = region(2 * 2048)
        mem_kv = at("mem_kv", [2, 2, D_MODEL], F32, kv_at)
        att_kv = at("att_kv", [2, PAGES, ATT_W], F32, kv_at)
        rows_in = at("rows_in", [2, 2, D_MODEL], F32, kv_at)
        conv_a = at("conv_a", [2, T], F32, kv_at + 8192)
        conv_gate = at("conv_gate", [2, T], F32, kv_at + 8192 + 8 * T)
        conv_acc = at("conv_acc", [2, T], F32, kv_at + 8192 + 16 * T)
        kt_at = region(2 * 2048)
        x_squares = at("x_squares", [KD, T], F32, kt_at)
        mem_v2 = at("mem_v2", [2, 2, D_MODEL], F32, kt_at)
        att_v2 = at("att_v2", [2, PAGES, ATT_W], F32, kt_at)
        mem_kt = at("mem_kt", [2, KD, N_MEM], F32, kt_at)
        att_kt = at("att_kt", [2, HEADS, PAST], F32, kt_at)
        win_a = at("win_a", [PX], F32, kt_at + 8192)
        win_b = at("win_b", [PX], F32, kt_at + 8192 + 1696)
        win_c = at("win_c", [PX], F32, kt_at + 8192 + 2 * 1696)
        pool_rows = at("pool_rows", [POOL_W], F32, kt_at + 8192 + 3 * 1696)
        conv_rows = at("conv_rows", [2, CONV_W], F32, kt_at + 8192 + 3 * 1696 + 1024)
        param_rows = at("param_rows", [DEPTH, P], F32, kt_at)
        arena = region(2 * KF * T)
        g_hi = at("g_hi", [KF, T], F32R, arena)
        g_lo = at("g_lo", [KF, T], F32R, arena + 4 * KF * T)
        zpos = [arena]

        def az(name, shape):
            start = zpos[0]
            zpos[0] += (4 * int(np.prod(shape)) + 31) // 32 * 32
            assert zpos[0] <= arena + 8 * KF * T, name
            return at(name, shape, F32, start)

        z = az("z_qk", [KD, T])
        after_z = zpos[0]
        v_t = az("v_t", [HEADS, T])
        k_tok = az("k_tok", [3, ATT_W])
        v_tok = az("v_tok", [3, ATT_W])
        pxt = az("pool_ext", [2, PX])
        cxt = az("conv_ext", [2, CX])
        pool_d = az("pool_diff", [2, PX])
        fresh = az("fresh", [4, TS])
        probs_t = az("att_probs_t", [HEADS, 384])
        sstate = az("sample_state", [2 * POOL_W])
        pstate = az("prompt_state", [2, POOL_W])
        zpos[0] = after_z
        mk = az("mk", [2, D_MODEL])
        mv = az("mv", [2, D_MODEL])
        mkt = az("mk_t", [KD, N_MEM])
        cx_probs_t = az("cx_probs_t", [HEADS, 512])
        zpos[0] = arena
        y_rows = az("y_rows", [3, D_MODEL])
        assert cursor[0] <= nc.sbuf_usable_end, (cursor[0], nc.sbuf_usable_end)

        G = ctx.enter_context(nc.psum_tensor("pairs", [P, 2, 2, 512], F32))
        M = ctx.enter_context(nc.psum_tensor("fixed", [P, 4, 512], F32))
        SCORES, STAT, OUTS, NEWS = 0, 1, 2, 3

        def sem(name):
            return ctx.enter_context(nc.semaphore(name))

        raw_landed = [sem(f"raw_landed{i}") for i in range(2)]
        hi_ready, lo_ready, unit_used = sem("hi_ready"), sem("lo_ready"), sem("unit_used")
        acc_ready, acc_free = sem("acc_ready"), sem("acc_free")
        const_landed, rows_landed, pages_landed = sem("const_landed"), sem("rows_landed"), sem("pages_landed")
        mem_landed, x_landed = sem("mem_landed"), sem("x_landed")
        fills_done, start_turned, start_taken = sem("fills_done"), sem("start_turned"), sem("start_taken")
        mem_sq, mem_norm = sem("mem_squared"), sem("mem_normed_s")
        sq_ready, stat_ready, root_ready, h_ready = (sem(n) for n in ("sq_ready", "stat_ready", "root_ready", "h_ready"))
        gate_scaled, silu_ready, g_ready = sem("gate_scaled"), sem("silu_ready"), sem("g_ready")
        x_rounded, m_rounded = sem("x_rounded"), sem("m_rounded")
        gate_ready, zsq_ready, rq_ready, z_normed, z_done = (
            sem(n) for n in ("gate_ready", "zsq_ready", "rq_ready", "z_normed", "z_done"))
        mixer_idle, mixer_params, states_in = sem("mixer_idle"), sem("mixer_params"), sem("states_in")
        tiles_free, out_landed, carry_landed = sem("tiles_free"), sem("out_landed"), sem("carry_landed")
        pooled, fresh_ready = sem("pooled"), sem("fresh_ready")
        kv_landed = [sem(f"kv_landed{i}") for i in range(4)]
        s_rows_out = sem("s_rows_out")
        prm_ready, gate_in = sem("prm_ready"), sem("gate_in")
        r_ready, pool_in, y_rounded = sem("r_ready"), sem("pool_in"), sem("y_rounded")
        v_used, kt_half, score_done = sem("v_used"), sem("kt_half"), sem("score_done")
        q_diag_ready, news_done, s_bias, s_exp, s_probs, s_turned, s_probs_t = (
            sem(n) for n in ("q_diag_ready", "news_done", "s_bias", "s_exp", "s_probs", "s_turned", "s_probs_t"))
        p_bias, p_exp, p_probs = sem("p_bias"), sem("p_exp"), sem("p_probs")
        conv_done, ln_sum, ln_centred, ln_sq, ln_var, ln_root, ln_out, conv_silu = (
            sem(n) for n in ("conv_done", "ln_sum", "ln_centred", "ln_sq", "ln_var", "ln_root", "ln_out", "conv_silu"))
        y_ready, m_ready, mk_sq, mk_root, mk_ready = (
            sem(n) for n in ("y_ready", "m_ready", "mk_sq", "mk_root", "mk_ready"))
        rows_ready, final_landed = sem("rows_ready"), sem("final_landed")
        cx_bias = sem("cx_bias")
        sp_passed, pool_passed = sem("sp_passed"), sem("pool_passed")
        x_sample_rows = mem_kt[0:TS, 1, 0:4, :].rearrange("p k c -> p (k c)")

        def cc(name, parts=P):
            return const[0:parts, COLS[name][0]:COLS[name][1]]

        ident = cc("ident")

        def par(name, k=0):
            r = PROWS[name][0] + k
            return prm[:, r:r + 1]

        def ap(t, offset, dims, parts=P, part0=0):
            full = t[part0:part0 + parts]
            return bass.AP(tensor=full.tensor, offset=full.offset + offset, ap=[[full.ap[0][0], parts], *dims])

        def into_row(h):
            at_h = COLS["pick"][0] + KD - 1 - h
            return const[:, at_h:at_h + KD]

        def from_row(h):
            return ap(const, COLS["ident"][0] + h, [[0, P]], KD)

        def conv_new(c):
            return cxt[:, c, CBUF + SEQ:].rearrange("p (b r) -> p b r", b=SAMPLES)

        sm = lambda i, n=1: small[:, i:i + n]
        eps = sm(0)

        def pool_diff(c):
            return pool_d[:, c, :]

        def spread_q(dve, att):
            for d in range(1 if att else 2):
                for odd in range(2):
                    dst = ap(q_diag, d * SAMPLES * HEADS * 32 + odd * (HEADS * 32 + 16), [[256, 4], [36, HEADS], [1, NEW]])
                    src = ap(z, (0 if att else d * T) + SEQ + odd * NEW, [[2 * NEW, 4], [T if att else 2 * T, HEADS], [1, NEW]])
                    last = dve.tensor_copy(dst, src)
            last.then_inc(q_diag_ready, 1)

        def spread_p(dve):
            for c in range(2):
                dst = ap(p_diag, c * SAMPLES * 32, [[64, SAMPLES // 2], [48, 2], [1, HEADS * NEW]])
                ins = dve.tensor_copy(dst, M[:, SCORES, c * P:(c + 1) * P].rearrange("p (b o r) -> p b o r", b=SAMPLES // 2, o=2))
            return ins

        def normalise_probs(dve, L, exp_sem, exp_value, tile, parts, done):
            dve.wait_ge(exp_sem, exp_value)
            dve.reciprocal(sm(48, 8), sm(24, 8))
            dve.drain()
            for h in range(HEADS):
                for c, s in enumerate(parts):
                    dve.tensor_scalar(tile[:, h, s], tile[:, h, s], sm(48 + 2 * h + c), None, ALU.mult).then_inc(done, 1)

        def raw_value(L, i, u):
            per_layer = RING_UNITS // 2 - (u % 2) * (RING_UNITS - N_UNITS)
            return 32 * (L * per_layer + i + u // 2 + 1)

        def half_value(L, i, u, half):
            return L * (2 * RING_UNITS) + i * 4 + (2 * u + half + 1)

        def half_inc(u, half):
            return 1 + (2 * (RING_UNITS - N_UNITS) if (u == N_UNITS - 1 and half) else 0)

        def turn_value(L, i, t):
            return L * N_TURNS + i * 2 + (t + 1)

        def passed(L, i, t):
            return turn_value(L, i, t) + 2

        def release(u):
            prev = u - 2
            if prev < 0:
                return "turn", -1
            for name in UNITS:
                nu = {"f1out": 12, "f2out": 12}.get(name)
                if nu and UNITS[name] <= prev < UNITS[name] + nu:
                    m, q = divmod(prev - UNITS[name], 3)
                    if q < 2:
                        return "unit", 2 * m + q + (8 if name == "f2out" else 0)
                    return "turn", TURNS[name][m]
            name = [n for n in UNITS if UNITS[n] <= prev and (n.startswith("f") or n in ("win", "wout", "cq", "ckv", "co"))][-1]
            return "turn", TURNS[name][prev - UNITS[name]]

        def chunks_of(u):
            for f in ("f1out", "f2out"):
                if UNITS[f] <= u < UNITS[f] + 12:
                    return OUT_PARTS[(u - UNITS[f]) % 3]
            return 8

        def kv_slot(n):
            return n % 2 + (2 if n >= SAMPLES and n % 4 >= 2 else 0)

        def kv_value(L, mem, n):
            slot = kv_slot(n)
            items = [m for m in range(2 * SAMPLES) if kv_slot(m) == slot]
            done = items.index(n) + 1
            per_layer = 16 * len(items) * (PAGES + 1)
            return L * per_layer + 16 * (len(items) * PAGES + done if mem else done * PAGES)

        block = ctx.enter_context(nc.Block())

        @block.sync
        def _(sp):
            sp.dma_start(const[:, :], a["shape_constants"]).then_inc(const_landed, 16)
            sp.dma_start(pages[:, :], a["page_table"].rearrange("(o b) c -> o (b c)", o=1)).then_inc(pages_landed, 16)
            sp.dma_start(rows_in[:, 0, :, :], a["mem_prompt"].rearrange("o (c p) d -> p (o c) d", p=P)).then_inc(mem_landed, 16)
            sp.dma_start(rows_in[:, 1, :, :], a["x_prompt"].rearrange("o (c p) d -> p (o c) d", p=P)).then_inc(x_landed, 16)
            sp.dma_start(x_sample_rows, a["x_sample"].rearrange("b t d -> (b t) d")).then_inc(x_landed, 16)

            def load(L, i, u, src, nk=8, gates=False):
                sp.wait_ge(lo_ready, half_value(L, i, u, 1))
                sp.sem_inc(sp_passed, 1)
                dst = raw[:, u % 2, 0:nk * 256]
                if gates:
                    dst = dst.rearrange("p (k g c) -> p k g c", g=2, c=P)
                    for g in range(2):
                        sp.dma_start(dst[:, :, g, :], src[:, :, g, :]).then_inc(raw_landed[u % 2], 16)
                else:
                    sp.dma_start(dst.rearrange("p (k c) -> p k c", c=256), src).then_inc(raw_landed[u % 2], 32)

            def ffn_in(L, name, w):
                v = w.rearrange("l (k p) (g m c) -> l m p k g c", p=P, g=2, c=P)
                with sp.Fori(0, KF // 2) as i:
                    for j in range(2):
                        load(L, i, UNITS[name] + j, v[L, i * 2 + j], gates=True)

            def ffn_out(L, name, w):
                v = w.rearrange("l (k p) (m c) -> l m p k c", p=P, c=256)
                for m in range(4):
                    for n, nk in enumerate(OUT_PARTS):
                        load(L, 0, UNITS[name] + 3 * m + n, v[L, m, :, 8 * n:8 * n + nk, :], nk)

            def square(L, name, w, order):
                v = w.rearrange("l (k p) (m c) -> l m p k c", p=P, c=256)
                for n, m in enumerate(order):
                    load(L, 0, UNITS[name] + n, v[L, m])

            with sp.Fori(0, DEPTH) as L:
                ffn_in(L, "f1in", a["w_ffn1_in"])
                ffn_out(L, "f1out", a["w_ffn1_out"])
                square(L, "win", a["w_in"], WIN_COLUMNS)
                square(L, "wout", a["w_out"], range(4))
                square(L, "cq", a["w_cq"], range(4))
                square(L, "ckv", a["w_ckv"], range(8))
                square(L, "co", a["w_co"], range(4))
                ffn_in(L, "f2in", a["w_ffn2_in"])
                ffn_out(L, "f2out", a["w_ffn2_out"])
            sp.wait_ge(rows_ready, 3)
            sp.dma_start(o["y_prompt"].rearrange("o (c p) d -> p (o c) d", p=P), y_rows[:, 0:2, :]).then_inc(final_landed, 16)
            sp.dma_start(o["y_sample"].rearrange("b t d -> (b t) d"), y_rows[0:TS, 2, :]).then_inc(final_landed, 16)
            sp.wait_ge(final_landed, 32)

        @block.gpsimd
        def _(pool):
            pool.memset(ones[:, :], 1.0).then_inc(fills_done, 1)
            pool.memset(eps, EPS).then_inc(fills_done, 1)
            pool.memset(q_diag[:, :, :, :], 0.0).then_inc(fills_done, 1)
            pool.memset(p_diag[:, :, :, :], 0.0).then_inc(fills_done, 1)
            pool.memset(pool_w[:, :, :], 0.0).then_inc(fills_done, 1)
            for name, (r, n) in PROWS.items():
                src = a[name]
                if name == "conv_dw_w":
                    src = src.rearrange("l j (c p) -> (j c) l p", p=P)
                else:
                    src = src.rearrange("l (c p) -> c l p", p=P)
                pool.dma_start(param_rows[r:r + n, :, :], src).then_inc(rows_landed, 16)
            pool.dma_start(o["s_pool"][:, :, 0:PBUF - NEW, :], a["state_pool"][:, :, NEW:PBUF, :]).then_inc(carry_landed, 16)
            pool.dma_start(o["s_conv"][:, :, 0:CBUF - NEW, :], a["state_conv"][:, :, NEW:CBUF, :]).then_inc(carry_landed, 16)
            pool.wait_ge(pages_landed, 16)
            pool.wait_ge(fills_done, 5)
            pool.wait_ge(start_taken, 10)

            def page(L, n, cache, tile):
                for c in range(PAGES):
                    i = (n % SAMPLES) * PAGES + c
                    which = pool.value_load(pages[0:1, i:i + 1], min_val=0, max_val=cache.shape[1] - 1)
                    pool.dma_start(tile[:, c, :], cache[L, bass.ds(which, 1), :, :, :].rearrange("o p h d -> p (o h d)")
                                   ).then_inc(kv_landed[kv_slot(n)], 16)

            def memory(L, n, cache, tile):
                pool.dma_start(tile, cache[L, n % SAMPLES].rearrange("(c p) h d -> p c (h d)", p=P)).then_inc(kv_landed[kv_slot(n)], 16)

            def pooling(c):
                def add(out, a, b):
                    return pool.tensor_tensor(out, a, b, ALU.add)

                e = pxt[:, c, :]
                low, high = slice(0, 64), slice(64, P)
                inv = cc("inv_win")[:, c:c + 1]
                first = cc("inv_first").rearrange("p (c t) -> p c t", c=2)[:, c, :]
                w, w0 = slice(PBUF, PX), slice(PBUF, PBUF + max(WINDOWS))
                add(win_a[:, 1:], e[:, 1:], e[:, :-1])
                pool.drain()
                if c == 0:
                    sums = win_a, win_b
                    add(win_b[high, 3:], win_a[high, 3:], win_a[high, 1:-2])
                else:
                    sums = win_c, win_a
                    add(win_b[:, 3:], win_a[:, 3:], win_a[:, 1:-2])
                    pool.drain()
                    add(win_c[:, 7:], win_b[:, 7:], win_b[:, 3:-4])
                    pool.drain()
                    add(win_a[high, 15:], win_c[high, 15:], win_c[high, 7:-8])
                pool.drain()
                for g, s in zip(sums, (low, high)):
                    pool.tensor_scalar(pool_diff(c)[s, w], g[s, w], inv[s, :], None, ALU.mult)
                pool.drain()
                for g, s in zip(sums, (low, high)):
                    pool.tensor_tensor(pool_diff(c)[s, w0], g[s, w0], first[s, :], ALU.mult)
                pool.drain()
                ins = pool.tensor_tensor(pool_diff(c)[:, w], pool_diff(c)[:, w], e[:, w], ALU.subtract)
                pool.drain()
                return ins

            def samples(L, load, keys, values, key_turn, ring, ring2, scores0, used0, first_wait):
                for n in range(2 * SAMPLES):
                    b = n - SAMPLES
                    if first_wait and n < 2:
                        pool.wait_ge(v_used, L * (2 * SAMPLES) + SAMPLES)
                    elif 2 <= n < SAMPLES + 2:
                        pool.wait_ge(acc_ready, passed(L, 0, key_turn(n - 2)))
                    elif b in (2, 3):
                        pool.wait_ge(score_done, L * (2 * SAMPLES) + scores0 + SAMPLES)
                    elif b >= 4:
                        pool.wait_ge(v_used, L * (2 * SAMPLES) + used0 + b - 4 + 1)
                    if first_wait or n >= 2:
                        pool.sem_inc(pool_passed, 1)
                    if not first_wait and n in (8, 9):
                        if n == 8:
                            pool.wait_ge(pool_in, L + 1)
                            pool.sem_inc(pool_passed, 1)
                        pooling(n - 8)
                        if n == 9:
                            pool.sem_inc(pooled, 1)
                    tile = ring2[:, n % 2] if b % 4 >= 2 and b >= 0 else ring[:, n % 2]
                    load(L, n, keys if b < 0 else values, tile)

            with pool.Fori(0, DEPTH) as L:
                pool.wait_ge(mixer_idle, L + 1)
                for g in range(4):
                    s = slice(64 * (g % 2), 64 * (g % 2) + 64)
                    pool.dma_start(pool_w[s, g // 2, s], a["pool_w"][L, g]).then_inc(mixer_params, 16)
                pool.dma_start(pw_w[:, :, :], a["conv_pw_w"][L].rearrange("(k p) c -> p k c", p=P)).then_inc(mixer_params, 16)
                pool.dma_start(ck_gain[:, :], a["ck_norm"][L].partition_broadcast(P)).then_inc(mixer_params, 16)
                pool.dma_start(pool_rows[0:120, :], a["state_pool"][L].rearrange("b r c -> (b r) c")).then_inc(states_in, 16)
                pool.dma_start(conv_rows[0:120, :, :], a["state_conv"][L].rearrange("(n b) r c -> (b r) n c", n=2)).then_inc(states_in, 16)
                samples(L, page, a["cache_att_k"], a["cache_att_v"], lambda n: TURNS["att_k"][n], att_kv, att_v2, 0, 0, False)
                pool.wait_ge(acc_free, passed(L, 0, TURNS["tok"][2]))
                for name, tile in (("att_k", k_tok), ("att_v", v_tok)):
                    pool.dma_start(o["p_" + name][L].rearrange("o (c p) h d -> p (o c) (h d)", p=P), tile[:, 0:2, :]).then_inc(out_landed, 16)
                    pool.dma_start(o["s_" + name][L].rearrange("b t h d -> (b t) (h d)"), tile[0:TS, 2, :]).then_inc(out_landed, 16)
                pool.dma_start(o["s_pool"][L][:, PBUF - NEW:PBUF, :], sstate[0:TS, 0:POOL_W]).then_inc(out_landed, 16)
                pool.dma_start(o["s_conv"][L][:, CBUF - NEW:CBUF, :], sstate[0:TS, POOL_W:]).then_inc(out_landed, 16)
                pool.dma_start(o["p_pool"][L, 0], pstate[0:PBUF, 0, :]).then_inc(out_landed, 16)
                pool.dma_start(o["p_conv"][L, 0], pstate[0:CBUF, 1, :]).then_inc(out_landed, 16)
                pool.wait_ge(out_landed, L * 160 + 128)
                pool.sem_inc(tiles_free, 1)
                pool.wait_ge(conv_silu, L + 1)
                samples(L, memory, a["cache_mem_k"], a["cache_mem_v"], lambda n: TURNS["mem_k"][2 * n + 1], mem_kv, mem_v2, SAMPLES, SAMPLES, True)
                pool.wait_ge(mk_ready, L * 8 + 8)
                pool.wait_ge(acc_free, passed(L, 0, TURNS["ckv"][7]))
                pool.dma_start(o["p_mem_k"][L, 0].rearrange("(c p) h d -> p c (h d)", p=P), mk[:, :, :]).then_inc(out_landed, 16)
                pool.dma_start(o["p_mem_v"][L, 0].rearrange("(c p) h d -> p c (h d)", p=P), mv[:, :, :]).then_inc(out_landed, 16)
                pool.wait_ge(out_landed, L * 160 + 160)
                pool.sem_inc(tiles_free, 1)
            pool.wait_ge(carry_landed, 32)

        @block.scalar
        def _(act):
            def copy(out, in_):
                return act.activation(out, in_, ACT.Copy)

            def split(L, i, u, base=0):
                n = chunks_of(u) * 128
                act.wait_ge(raw_landed[u % 2], raw_value(L, i, u))
                kind, n_before = release(u)
                if kind == "turn":
                    act.wait_ge(acc_ready, passed(L, i, n_before))
                else:
                    act.wait_ge(unit_used, L * 16 + n_before + 1)
                for half in range(2):
                    s = slice(half * n, half * n + n)
                    copy(w_hi[:, u % 2, s], raw[:, u % 2, s]).then_inc(hi_ready, half_inc(u, half))

            NORMS = ("ln_ffn1", "ln_mix", "ln_cross", "ln_ffn2")

            def norm_in(L, n, m):
                if n == 0:
                    act.wait_ge(acc_free, passed(L, 0, -1))
                else:
                    act.wait_ge(acc_free, passed(L, 0, TURNS[("", "f1out", "wout", "co")[n]][m]))
                act.activation(x_squares[:, 2 * m:2 * m + 2, :], x[:, 2 * m:2 * m + 2, :], ACT.Square).then_inc(sq_ready, 1)
                for k in (2 * m, 2 * m + 1):
                    act.activation(h_hi[:, k, :], x[:, k, :], ACT.Copy, scale=par(NORMS[n], k)).then_inc(x_rounded, 1)

            def norm_root(L, n):
                act.wait_ge(stat_ready, L * 4 + n + 1)
                act.activation(norm_r[:, :], M[:, STAT, 0:T], ACT.Sqrt, bias=eps, scale=1.0 / D_MODEL).then_inc(root_ready, 1)

            def ffn(L, first, fin, fout):
                n0 = 0 if fin == "f1in" else KF
                u0, t0 = UNITS[fin], TURNS[fin][0]
                with act.Fori(0, KF // 2) as i:
                    for j in range(2):
                        split(L, i, u0 + j + 1)
                        act.wait_ge(gate_scaled, L * (2 * KF) + i * 2 + (first * KF + j + 1))
                        act.activation(gate_up[:, 0, :], gate_up[:, 0, :], ACT.Silu).then_inc(silu_ready, 1)
                u0 = UNITS[fout]
                for n in range(1, 12):
                    split(L, 0, u0 + n)
                    if fout == "f1out" and n in (4, 7, 10):
                        norm_in(L, 1, n // 3 - 1)
                if fout == "f1out":
                    split(L, 0, u0 + 12)
                    norm_in(L, 1, 3)

            act.wait_ge(fills_done, 5)
            act.wait_ge(mem_landed, 16)
            for c in range(2):
                act.activation(norm_tmp[:, 4 * c:4 * c + 4, 0:256], rows_in[:, 0, c, :], ACT.Square, accum_out=sm(1 + c))
            act.drain()
            act.activation(sm(3, 2), sm(1, 2), ACT.Sqrt, bias=eps, scale=1.0 / D_MODEL).then_inc(mem_sq, 1)

            act.wait_ge(start_taken, 10)
            with act.Fori(0, DEPTH) as L:
                split(L, 0, 0)
                act.wait_ge(prm_ready, L + 1)
                for m in range(4):
                    norm_in(L, 0, m)
                norm_root(L, 0)
                ffn(L, 0, "f1in", "f1out")
                norm_root(L, 1)
                def key_half(L, t, n, out):
                    act.wait_ge(acc_ready, passed(L, 0, t))
                    copy(out, G[:, t % 2, 0, :]).then_inc(kt_half, 1)

                def att_key_half(b):
                    if b >= 2:
                        act.wait_ge(score_done, L * 16 + b - 1)
                    key_half(L, TURNS["att_k"][b], b, att_kt[:, b % 2, 0:2, :].rearrange("p h c -> p (h c)"))

                for n in range(9):
                    split(L, 0, UNITS["win"] + n + 1)
                    if 1 <= n <= 4:
                        act.wait_ge(acc_free, passed(L, 0, TURNS["win"][n - 1]))
                        act.activation(qk_squares[:, 2 * n - 2:2 * n, :], z[:, 2 * n - 2:2 * n, :], ACT.Square).then_inc(zsq_ready, 1)
                    if n == 4:
                        t = TURNS["qk_stat"][0]
                        act.wait_ge(acc_ready, passed(L, 0, t))
                        act.activation(qk_rms[0:KD, :], G[0:KD, t % 2, 0, 0:T], ACT.Sqrt, bias=small[0:KD, 0:1], scale=1.0 / DH).then_inc(rq_ready, 1)
                    if n == 5:
                        act.wait_ge(gate_in, L + 1)
                        act.activation(conv_gate[:, :, :], conv_gate[:, :, :], ACT.Sigmoid).then_inc(gate_ready, 1)
                    if n >= 6:
                        for b in ((0, 1), (2, 3), (4, 5, 6, 7))[n - 6]:
                            att_key_half(b)
                for h in range(HEADS):
                    act.wait_ge(p_bias, L * 2 + 1)
                    for c, s in ((0, slice(0, 128)), (1, slice(128, 384))):
                        act.activation(probs[:, h, s], probs[:, h, s], ACT.Exp, bias=sm(16 + 2 * h + c), scale=DH ** -0.5,
                                       accum_out=sm(24 + 2 * h + c)).then_inc(p_exp, 1)
                act.wait_ge(s_bias, L * 2 + 1)
                act.activation(sprobs[:, :], sprobs[:, :], ACT.Exp, bias=sm(5), scale=DH ** -0.5, accum_out=sm(6)).then_inc(s_exp, 1)
                t = TURNS["pool"][0]
                act.wait_ge(acc_ready, passed(L, 0, t))
                for c in range(2):
                    act.activation(y_hi[:, c, :], G[:, t % 2, c, 0:T], ACT.Copy, scale=par("pool_scale", c)).then_inc(y_rounded, 1)
                act.wait_ge(ln_centred, L + 1)
                act.activation(conv_sq[:, :, :], conv_acc[:, :, :], ACT.Square).then_inc(ln_sq, 1)
                act.wait_ge(ln_var, L + 1)
                act.activation(norm_r[:, :], M[:, STAT, 0:T], ACT.Sqrt, bias=eps, scale=1.0 / CONV_W).then_inc(ln_root, 1)
                act.wait_ge(ln_out, L + 1)
                for c in range(2):
                    last = act.activation(conv_act[:, c, :], conv_acc[:, c, :], ACT.Silu, bias=par("conv_ln_b", c))
                last.then_inc(conv_silu, 1)
                t = TURNS["pw"][0]
                act.wait_ge(acc_ready, passed(L, 0, t))
                for c in range(2):
                    act.activation(y_hi[:, 2 + c, :], G[:, t % 2, c, 0:T], ACT.Identity, bias=par("conv_pw_b", c)).then_inc(y_rounded, 1)
                for n in range(4):
                    split(L, 0, UNITS["wout"] + n + 1)
                    if n > 0:
                        norm_in(L, 2, n - 1)
                norm_in(L, 2, 3)
                norm_root(L, 2)
                for n in range(4):
                    split(L, 0, UNITS["cq"] + n + 1)
                    for k in (range(0, 2), range(2, 5), range(5, 8), ())[n]:
                        act.activation(y_hi[:, k, 0:N_MEM], mem_t[:, k, :], ACT.Copy, scale=par("ln_mem", k)).then_inc(m_rounded, 1)
                act.wait_ge(acc_ready, passed(L, 0, TURNS["cq"][3]))
                for j in range(4):
                    act.wait_ge(acc_free, passed(L, 0, TURNS["cq"][j]))
                    act.activation(squares[:, 2 * j:2 * j + 2, :], z[:, 2 * j:2 * j + 2, :], ACT.Square).then_inc(zsq_ready, 1)
                for n in range(4):
                    t = TURNS["ckv"][n]
                    split(L, 0, UNITS["ckv"] + n + 1)
                    for c in range(2):
                        act.wait_ge(acc_ready, passed(L, 0, t))
                        act.activation(G[:, t % 2, c, 256:512], G[:, t % 2, c, 0:MDH], ACT.Square,
                                       accum_out=sm(32 + 4 * c + n)).then_inc(mk_sq, 1)
                    if n == 0:
                        t = TURNS["cq_stat"][0]
                        act.wait_ge(acc_ready, passed(L, 0, t))
                        act.activation(cq_rms[0:KD, :], G[0:KD, t % 2, 0, 0:T], ACT.Sqrt, bias=small[0:KD, 0:1], scale=1.0 / MDH).then_inc(rq_ready, 1)
                    for b in (2 * n, 2 * n + 1):
                        for half in range(2):
                            if b >= 2 and half == 0:
                                act.wait_ge(score_done, L * 16 + SAMPLES + b - 1)
                            key_half(L, TURNS["mem_k"][2 * b + half], b,
                                     mem_kt[:, b % 2, 4 * half:4 * half + 2, :].rearrange("p h c -> p (h c)"))
                act.activation(sm(40, 8), sm(32, 8), ACT.Sqrt, bias=eps, scale=1.0 / MDH).then_inc(mk_root, 1)
                split(L, 0, UNITS["ckv"] + 5)
                act.wait_ge(s_bias, L * 2 + 2)
                act.activation(cx_sprobs[:, :], M[:, SCORES, 0:N_MEM], ACT.Exp, bias=sm(5), scale=MDH ** -0.5, accum_out=sm(6)).then_inc(s_exp, 1)
                split(L, 0, UNITS["ckv"] + 6)
                split(L, 0, UNITS["ckv"] + 7)
                for j in range(2):
                    t = TURNS["cx_s"][j]
                    act.wait_ge(cx_bias, L * 2 + j + 1)
                    for e in range(2):
                        h = 2 * j + e
                        for c in range(2):
                            act.activation(cx_probs[:, h, 256 * c:256 * c + 256], G[:, t % 2, e, 256 * c:256 * c + 256], ACT.Exp,
                                           bias=sm(16 + 2 * h + c), scale=MDH ** -0.5, accum_out=sm(24 + 2 * h + c)).then_inc(p_exp, 1)
                split(L, 0, UNITS["co"])
                for n in range(4):
                    split(L, 0, UNITS["co"] + n + 1)
                    if n > 0:
                        norm_in(L, 3, n - 1)
                norm_in(L, 3, 3)
                norm_root(L, 3)
                ffn(L, 1, "f2in", "f2out")


        @block.vector
        def _(dve):
            def tt(out, in0, in1, op):
                return dve.tensor_tensor(out, in0, in1, op)

            def stt(out, in0, scalar, in1, op0, op1):
                return dve.scalar_tensor_tensor(out, in0, scalar, in1, op0, op1)

            def split(L, i, u):
                n = chunks_of(u) * 128
                for half in range(2):
                    s = slice(half * n, half * n + n)
                    dve.wait_ge(hi_ready, half_value(L, i, u, half))
                    tt(w_lo[:, u % 2, s], raw[:, u % 2, s], w_hi[:, u % 2, s].bitcast(F32), ALU.subtract
                       ).then_inc(lo_ready, half_inc(u, half))

            def hi_lo(items, done, first_step=None):
                n = len(items)
                for k in range(n + 2):
                    if k < n and items[k][0] is not None:
                        items[k][0]()
                    if 1 <= k <= n:
                        _, src, hi, lo = items[k - 1]
                        dve.tensor_copy(hi, src)
                    if k >= 2:
                        _, src, hi, lo = items[k - 2]
                        done(tt(lo, src, hi.bitcast(F32), ALU.subtract), k - 2)
                    if k < n + 1:
                        dve.drain()

            NORMS = ("ln_ffn1", "ln_mix", "ln_cross", "ln_ffn2")

            def norm_in(L, n, m):
                for k in (2 * m, 2 * m + 1):
                    dve.wait_ge(x_rounded, L * 32 + 8 * n + k + 1)
                    stt(h_lo[:, k, :], x[:, k, :], par(NORMS[n], k), h_hi[:, k, :].bitcast(F32), ALU.mult, ALU.subtract).then_inc(h_ready, 1)

            def norm_root(L, n):
                dve.wait_ge(root_ready, L * 4 + n + 1)
                dve.reciprocal(norm_r[:, :], norm_r[:, :])
                dve.drain()

            def scaled(out, in_):
                return tt(out, in_, ap(norm_r, 0, [[0, 2], [1, T]]), ALU.mult)

            def free(ins):
                return ins.then_inc(acc_free, 1)

            def acc(L, t, i=0):
                dve.wait_ge(acc_ready, passed(L, i, t))
                return G[:, t % 2, :, :]

            def residual(L, t, m, scale):
                pair = acc(L, t)
                free(stt(x[:, 2 * m:2 * m + 2, :], pair[:, :, 0:T], scale, x[:, 2 * m:2 * m + 2, :], ALU.mult, ALU.add))

            def ffn(L, which, fin, fout):
                u0, t0 = UNITS[fin], TURNS[fin][0]
                with dve.Fori(0, KF // 2) as i:
                    for j in range(2):
                        split(L, i, u0 + j + 1)
                        dve.drain()
                        pair = acc(L, t0 + j, i)
                        scaled(gate_up[:, :, :], pair[:, :, 0:T]).then_inc(gate_scaled, 1)
                        free(dve.drain())
                        dve.wait_ge(silu_ready, L * (2 * KF) + i * 2 + (which * KF + j + 1))
                        tt(gate_up[:, 1, :], gate_up[:, 0, :], gate_up[:, 1, :], ALU.mult)
                        dve.drain()
                        m = i * 2 + j
                        hi = g_hi[:, bass.ds(m, 1), :].rearrange("p o t -> p (o t)")
                        lo = g_lo[:, bass.ds(m, 1), :].rearrange("p o t -> p (o t)")
                        dve.tensor_copy(hi, gate_up[:, 1, :])
                        dve.drain()
                        tt(lo, gate_up[:, 1, :], hi.bitcast(F32), ALU.subtract).then_inc(g_ready, 1)
                for m in range(4):
                    for n in range(3 * m + 1, 3 * m + 4):
                        if n < 12 or fout == "f1out":
                            split(L, 0, UNITS[fout] + n)
                        if fout == "f1out" and m > 0 and n == 3 * m + 1:
                            norm_in(L, 1, m - 1)
                    residual(L, TURNS[fout][m], m, 0.5)
                if fout == "f1out":
                    norm_in(L, 1, 3)

            dve.sem_inc(acc_free, 2)
            dve.sem_inc(lo_ready, 4)
            dve.sem_inc(mixer_idle, 1)
            dve.wait_ge(mem_sq, 1)
            dve.reciprocal(sm(3, 2), sm(3, 2))
            dve.drain()
            for c in range(2):
                dve.tensor_scalar(rows_in[:, 0, c, :], rows_in[:, 0, c, :], sm(3 + c), None, ALU.mult).then_inc(mem_norm, 1)
            for n in range(10):
                dve.wait_ge(start_turned, n + 1)
                bank = M[:, n % 4, :]
                if n == 0:
                    ins = dve.tensor_copy(prm_all[:, :, :], bank[:, 0:2 * N_PROWS].rearrange("p (l r) -> p l r", l=2))
                elif n < 9:
                    k = 2 * ((n - 1) % 4)
                    dst = mem_t[:, k:k + 2, :] if n < 5 else x[:, k:k + 2, 0:SEQ]
                    ins = dve.tensor_copy(dst, bank.rearrange("p (k t) -> p k t", k=2))
                else:
                    ins = dve.tensor_copy(x[:, :, SEQ:T], bank[:, 0:KD * TS].rearrange("p (k t) -> p k t", k=KD))
                ins.then_inc(start_taken, 1)
            dve.drain()

            with dve.Fori(0, DEPTH) as L:
                dve.tensor_copy(prm[:, :], prm_all[:, bass.ds(L, 1), :].rearrange("p o r -> p (o r)")).then_inc(prm_ready, 1)
                dve.drain()
                split(L, 0, 0)
                for m in range(4):
                    norm_in(L, 0, m)
                norm_root(L, 0)
                ffn(L, 0, "f1in", "f1out")

                dve.memset(pxt[:, :, 0:PBUF], 0.0)
                dve.memset(cxt[:, :, 0:CBUF], 0.0)
                norm_root(L, 1)

                def pool_new(c):
                    return pxt[:, c, PBUF + SEQ:].rearrange("p (b r) -> p b r", b=SAMPLES)

                pair = acc(L, TURNS["state_in"][0])
                for c in range(2):
                    for half in range(2):
                        dve.tensor_copy(conv_new(c)[:, 4 * half:4 * half + 4, 0:CBUF],
                                        pair[:, 0, 240 * c + 120 * half:240 * c + 120 * half + 120].rearrange("p (b r) -> p b r", b=4))
                    last = dve.tensor_copy(pool_new(c)[:, :, 0:PBUF], pair[:, 1, 120 * c:120 * c + 120].rearrange("p (b r) -> p b r", b=SAMPLES))
                free(last)
                def taps(j0, j1):
                    for j in range(j0, j1):
                        w = PROWS["conv_dw_w"][0] + 2 * j
                        for c in range(2):
                            for out, src in ((conv_acc[:, c, 0:SEQ], cxt[:, c, j:j + SEQ]),
                                             (conv_acc[:, c, SEQ:T].rearrange("p (b t) -> p b t", b=SAMPLES), conv_new(c)[:, :, j:j + NEW])):
                                if j == 0:
                                    dve.tensor_scalar(out, src, prm[:, w + c:w + c + 1], par("conv_dw_b", c), ALU.mult, ALU.add)
                                else:
                                    stt(out, src, prm[:, w + c:w + c + 1], out, ALU.mult, ALU.add)
                        dve.drain()

                def att_keys(b):
                    pair = acc(L, TURNS["att_k"][b])
                    if b >= 2:
                        dve.wait_ge(score_done, L * 16 + b - 1)
                    dve.wait_ge(kt_half, L * 24 + b + 1)
                    free(dve.tensor_copy(att_kt[:, b % 2, 2:4, :].rearrange("p h c -> p (h c)"), pair[:, 1, :]))

                def win(n, j0=0, j1=0):
                    split(L, 0, UNITS["win"] + n + 1)
                    dve.drain()
                    taps(j0, j1)
                    return acc(L, TURNS["win"][n])

                for n in range(4):
                    free(scaled(z[:, 2 * n:2 * n + 2, :], win(n)[:, :, 0:T]))
                free(scaled(conv_a[:, :, :], win(4)[:, :, 0:T]))
                dve.wait_ge(rq_ready, L * 2 + 1)
                acc(L, TURNS["qk_stat"][0])
                dve.reciprocal(qk_rms[0:KD, :], qk_rms[0:KD, :]).then_inc(r_ready, 1)
                free(dve.drain())
                free(scaled(conv_gate[:, :, :], win(5)[:, :, 0:T]))
                dve.drain()
                dve.sem_inc(gate_in, 1)
                dve.wait_ge(gate_ready, L + 1)
                tt(cxt[:, :, CBUF:CBUF + SEQ], conv_a[:, :, 0:SEQ], conv_gate[:, :, 0:SEQ], ALU.mult)
                tt(fresh[:, 2:4, :], conv_a[:, :, SEQ:T], conv_gate[:, :, SEQ:T], ALU.mult)
                dve.drain()
                for c in range(2):
                    last = dve.tensor_copy(conv_new(c)[:, :, CBUF:], fresh[:, 2 + c, :].rearrange("p (b t) -> p b t", b=SAMPLES))
                last.then_inc(fresh_ready, 1)
                for j in range(4):
                    pair = acc(L, TURNS["qk_root"][j])
                    stt(z[:, 2 * j:2 * j + 2, :], z[:, 2 * j:2 * j + 2, :], par("att_q_norm" if j < 2 else "att_k_norm"), pair[:, :, 0:T],
                        ALU.mult, ALU.mult).then_inc(z_normed, 1)
                    free(dve.drain())
                pair = win(6, 0, 3)
                tt(pxt[:, :, PBUF:PBUF + SEQ], pair[:, :, 0:SEQ], ap(norm_r, 0, [[0, 2], [1, SEQ]]), ALU.mult)
                free(tt(fresh[:, 0:2, :], pair[:, :, SEQ:T], ap(norm_r, SEQ, [[0, 2], [1, TS]]), ALU.mult))
                dve.drain()
                for c in range(2):
                    dve.tensor_copy(pool_new(c)[:, :, PBUF:], fresh[:, c, :].rearrange("p (b t) -> p b t", b=SAMPLES))
                dve.drain()
                dve.sem_inc(pool_in, 1)
                for j in range(4):
                    pair = acc(L, TURNS["rope"][j])
                    turned = z[0:ROPE_DIM, 2 * j:2 * j + 2, :]
                    cos2 = ap(const, COLS["cos"][0], [[0, 2], [1, T]], ROPE_DIM)
                    sin2 = ap(const, COLS["sin"][0], [[0, 2], [1, T]], ROPE_DIM)
                    free(tt(rope_tmp[0:ROPE_DIM, :, :], pair[0:ROPE_DIM, :, 0:T], sin2, ALU.mult))
                    tt(turned, turned, cos2, ALU.mult)
                    dve.drain()
                    tt(turned, turned, rope_tmp[0:ROPE_DIM, :, :], ALU.add).then_inc(z_done, 1)
                    dve.drain()
                spread_q(dve, att=True)
                for b in (0, 1):
                    att_keys(b)
                free(scaled(v_t[:, 0:2, :], win(7, 3, 8)[:, :, 0:T]))
                for b in (2, 3):
                    att_keys(b)
                    taps(3 * b + 2, 3 * b + 5)
                free(scaled(v_t[:, 2:4, :], win(8)[:, :, 0:T]))
                for b in range(4, SAMPLES):
                    att_keys(b)
                    taps(3 * b + 2, 3 * b + 5)
                dve.drain()

                for c in range(3):
                    n = P if c < 2 else TS
                    pair = acc(L, TURNS["tok"][c])
                    dve.tensor_copy(k_tok[0:n, c, :], pair[0:n, 0, :])
                    last = dve.tensor_copy(v_tok[0:n, c, :], pair[0:n, 1, :])
                    free(last)

                for j in range(2):
                    pair = acc(L, TURNS["att_s"][j])
                    blocks = pair.rearrange("p e (n c) -> p e n c", n=2)[:, :, :, 0:P]
                    causal4 = ap(const, COLS["causal"][0], [[0, 2], [0, 2], [1, P]])
                    out = ap(probs, 2 * j * 384, [[384, 2], [256, 2], [1, P]])
                    tt(out, blocks, causal4, ALU.add)
                    free(dve.tensor_copy(probs[:, 2 * j:2 * j + 2, P:2 * P], pair[:, :, P:2 * P]))
                dve.drain()
                peak = small[:, 72:80].rearrange("p (h c) -> p h c", c=2)
                dve.tensor_reduce(peak[:, :, 0], probs[:, :, 0:P], AX.X, ALU.max, negate=True)
                dve.tensor_reduce(peak[:, :, 1], probs[:, :, P:384], AX.X, ALU.max, negate=True)
                dve.drain()
                dve.tensor_scalar(sm(16, 8), sm(72, 8), DH ** -0.5, None, ALU.mult).then_inc(p_bias, 2)

                dve.wait_ge(news_done, L + 1)
                dve.tensor_copy(sprobs[:, 0:PAST], M[:, SCORES, 0:PAST])
                tt(sprobs[:, PAST:], M[:, NEWS, 0:TS], cc("own"), ALU.add)
                dve.drain()
                dve.tensor_reduce(sm(64), sprobs[:, :], AX.X, ALU.max, negate=True)
                dve.drain()
                dve.tensor_scalar(sm(5), sm(64), DH ** -0.5, None, ALU.mult).then_inc(s_bias, 1)
                taps(26, CONV_K)
                dve.sem_inc(conv_done, 1)
                pair = acc(L, TURNS["pool"][0])
                dve.wait_ge(y_rounded, L * 4 + 2)
                for c in range(2):
                    last = stt(y_lo[:, c, :], pair[:, c, 0:T], par("pool_scale", c), y_hi[:, c, :].bitcast(F32), ALU.mult, ALU.subtract
                               ).then_inc(y_ready, 1)
                free(dve.drain())
                pair = acc(L, TURNS["state_out"][0])
                dve.tensor_copy(sstate[0:TS, :], pair[0:TS, 0, :])
                dve.tensor_copy(pstate[0:PBUF, 0, :], pair[0:PBUF, 1, 0:256])
                free(dve.tensor_copy(pstate[0:CBUF, 1, :], pair[0:CBUF, 1, 256:512]))
                normalise_probs(dve, L, p_exp, L * 16 + 8, probs, (slice(0, P), slice(P, 384)), p_probs)
                dve.wait_ge(s_exp, L * 2 + 1)
                dve.reciprocal(sm(7), sm(6))
                dve.drain()
                dve.tensor_scalar(sprobs[:, :], sprobs[:, :], sm(7), None, ALU.mult).then_inc(s_probs, 1)
                dve.wait_ge(ln_sum, L + 1)
                for c in range(2):
                    last = stt(conv_acc[:, c, :], M[:, STAT, 0:T], -1.0 / CONV_W, conv_acc[:, c, :], ALU.mult, ALU.add)
                last.then_inc(ln_centred, 1)
                for j in range(2):
                    pair = acc(L, TURNS["att_pt"][j])
                    free(dve.tensor_copy(probs_t[:, 2 * j:2 * j + 2, :], pair[:, :, 0:384]))
                dve.wait_ge(s_turned, L * 2 + 1)
                spread_p(dve)
                dve.tensor_copy(new_probs_t[0:TS, :], M[0:TS, SCORES, PAST:PAST + ROWS]).then_inc(s_probs_t, 1)
                for j in range(2):
                    pair = acc(L, TURNS["att_o"][j])
                    s = slice(4 + 2 * j, 6 + 2 * j)
                    dve.tensor_copy(y_hi[:, s, 0:SEQ], pair[:, :, 0:SEQ])
                    dve.drain()
                    free(tt(y_lo[:, s, 0:SEQ], pair[:, :, 0:SEQ], y_hi[:, s, 0:SEQ].bitcast(F32), ALU.subtract))
                dve.wait_ge(ln_root, L + 1)
                dve.reciprocal(norm_r[:, :], norm_r[:, :])
                dve.drain()
                for c in range(2):
                    last = stt(conv_acc[:, c, :], conv_acc[:, c, :], par("conv_ln_g", c), norm_r[:, :], ALU.mult, ALU.mult)
                last.then_inc(ln_out, 1)
                dve.wait_ge(v_used, L * 16 + 8)
                dve.tensor_copy(att_out_rows[:, :], M[:, OUTS, :]).then_inc(s_rows_out, 1)
                pair = acc(L, TURNS["pw"][0])
                dve.wait_ge(y_rounded, L * 4 + 4)
                for c in range(2):
                    stt(y_lo[:, 2 + c, :], pair[:, c, 0:T], par("conv_pw_b", c), y_hi[:, 2 + c, :].bitcast(F32), ALU.add, ALU.subtract
                        ).then_inc(y_ready, 1)
                free(dve.drain())
                acc(L, TURNS["att_so"][0])
                new = bass.AP(tensor=G, offset=(TURNS["att_so"][0] % 2) * 1024, ap=[[2048, P], [P + NEW, HEADS], [HEADS * NEW, SAMPLES], [1, NEW]])
                hi, lo = (y[:, 4:8, SEQ:T].rearrange("p k (b t) -> p k b t", b=SAMPLES) for y in (y_hi, y_lo))
                dve.tensor_copy(hi, new)
                dve.drain()
                tt(lo, new, hi.bitcast(F32), ALU.subtract).then_inc(y_ready, 1)
                free(dve.drain())
                for n in range(4):
                    split(L, 0, UNITS["wout"] + n + 1)
                    if n > 0:
                        norm_in(L, 2, n - 1)
                    residual(L, TURNS["wout"][n], n, 1.0)
                norm_in(L, 2, 3)

                norm_root(L, 2)
                for n in range(4):
                    split(L, 0, UNITS["cq"] + n + 1)
                    for k in (range(0, 2), range(2, 5), range(5, 8), ())[n]:
                        dve.wait_ge(m_rounded, L * 8 + k + 1)
                        stt(y_lo[:, k, 0:N_MEM], mem_t[:, k, :], par("ln_mem", k), y_hi[:, k, 0:N_MEM].bitcast(F32), ALU.mult, ALU.subtract
                            ).then_inc(m_ready, 1)
                    pair = acc(L, TURNS["cq"][n])
                    if n == 0:
                        dve.wait_ge(tiles_free, 2 * L + 1)
                    free(scaled(z[:, 2 * n:2 * n + 2, :], pair[:, :, 0:T]))
                def ckv_out(n):
                    pair = acc(L, TURNS["ckv"][n])
                    if n < HEADS:
                        dve.wait_ge(mk_sq, L * 8 + 2 * n + 2)
                        free(dve.tensor_copy(mk[:, :, n * MDH:(n + 1) * MDH], pair[:, :, 0:MDH]))
                    else:
                        free(dve.tensor_copy(mv[:, :, (n - HEADS) * MDH:(n - HEADS + 1) * MDH], pair[:, :, 0:MDH]))

                for n in range(4):
                    split(L, 0, UNITS["ckv"] + n + 1)
                    ckv_out(n)
                    if n == 0:
                        dve.wait_ge(rq_ready, L * 2 + 2)
                        acc(L, TURNS["cq_stat"][0])
                        dve.reciprocal(cq_rms[0:KD, :], cq_rms[0:KD, :]).then_inc(r_ready, 1)
                        free(dve.drain())
                    for b in (2 * n, 2 * n + 1):
                        if b == 1:
                            for j in range(2):
                                pair = acc(L, TURNS["cq_root"][j])
                                for e in range(2):
                                    for d in range(2):
                                        k = 4 * j + 2 * e + d
                                        last = stt(z[:, k, :], z[:, k, :], par("cq_norm", d), pair[:, e, 0:T], ALU.mult, ALU.mult)
                                free(last)
                            dve.drain()
                            dve.sem_inc(z_done, 1)
                            spread_q(dve, att=False)
                        for half in range(2):
                            pair = acc(L, TURNS["mem_k"][2 * b + half])
                            if b >= 2 and half == 0:
                                dve.wait_ge(score_done, L * 16 + SAMPLES + b - 1)
                            dve.wait_ge(kt_half, L * 24 + SAMPLES + 2 * b + half + 1)
                            free(dve.tensor_copy(mem_kt[:, b % 2, 4 * half + 2:4 * half + 4, :].rearrange("p h c -> p (h c)"), pair[:, 1, :]))
                split(L, 0, UNITS["ckv"] + 5)
                dve.wait_ge(mk_root, L + 1)
                dve.reciprocal(sm(56, 8), sm(40, 8))
                dve.drain()
                for c in range(2):
                    for h in range(HEADS):
                        s = slice(h * MDH, (h + 1) * MDH)
                        stt(mk[:, c, s], mk[:, c, s], sm(56 + 4 * c + h), ck_gain[:, :], ALU.mult, ALU.mult).then_inc(mk_ready, 1)
                ckv_out(4)
                dve.wait_ge(score_done, L * 16 + 2 * SAMPLES)
                dve.tensor_reduce(sm(64), M[:, SCORES, 0:N_MEM], AX.X, ALU.max, negate=True)
                dve.drain()
                dve.tensor_scalar(sm(5), sm(64), MDH ** -0.5, None, ALU.mult).then_inc(s_bias, 1)
                dve.wait_ge(s_exp, L * 2 + 2)
                dve.reciprocal(sm(7), sm(6))
                dve.drain()
                dve.tensor_scalar(cx_sprobs[:, :], cx_sprobs[:, :], sm(7), None, ALU.mult).then_inc(s_probs, 1)
                split(L, 0, UNITS["ckv"] + 6)
                ckv_out(5)
                for j in range(2):
                    pair = acc(L, TURNS["mkt"][j])
                    free(dve.tensor_copy(mkt[:, 4 * j:4 * j + 4, :].rearrange("p (e k) t -> p e k t", e=2),
                                         pair.rearrange("p e (k t) -> p e k t", k=2)))
                dve.wait_ge(s_turned, L * 2 + 2)
                spread_p(dve).then_inc(s_probs_t, 1)
                split(L, 0, UNITS["ckv"] + 7)
                ckv_out(6)
                for j in range(2):
                    pair = acc(L, TURNS["cx_s"][j])
                    dve.tensor_reduce(small[:, 72 + 4 * j:76 + 4 * j].rearrange("p (e c) -> p e c", e=2),
                                      pair.rearrange("p e (c t) -> p e c t", c=2), AX.X, ALU.max, negate=True)
                    dve.drain()
                    dve.tensor_scalar(sm(16 + 4 * j, 4), sm(72 + 4 * j, 4), MDH ** -0.5, None, ALU.mult).then_inc(cx_bias, 1)
                for j in range(2):
                    dve.wait_ge(p_exp, L * 16 + 8 + 4 * j + 4)
                    free(dve.reciprocal(sm(48 + 4 * j, 4), sm(24 + 4 * j, 4)))
                dve.drain()
                for h in range(HEADS):
                    for c in range(2):
                        s = slice(256 * c, 256 * c + 256)
                        dve.tensor_scalar(cx_probs[:, h, s], cx_probs[:, h, s], sm(48 + 2 * h + c), None, ALU.mult).then_inc(p_probs, 1)
                split(L, 0, UNITS["co"])
                ckv_out(7)
                for j in range(2):
                    pair = acc(L, TURNS["cx_pt"][j])
                    free(dve.tensor_copy(cx_probs_t[:, 2 * j:2 * j + 2, :], pair))
                dve.wait_ge(v_used, L * 16 + 16)
                dve.tensor_copy(cx_out_rows[:, :, :], M[:, OUTS:OUTS + 2, :]).then_inc(s_rows_out, 1)
                for j in range(2):
                    pair = acc(L, TURNS["cx_o"][j]).rearrange("p e (k t) -> p e k t", k=2)
                    hi = y_hi[:, 4 * j:4 * j + 4, 0:SEQ].rearrange("p (e k) t -> p e k t", e=2)
                    lo = y_lo[:, 4 * j:4 * j + 4, 0:SEQ].rearrange("p (e k) t -> p e k t", e=2)
                    dve.tensor_copy(hi, pair)
                    dve.drain()
                    free(tt(lo, pair, hi.bitcast(F32), ALU.subtract))
                acc(L, TURNS["cx_so"][0])
                parts = []
                for h in range(HEADS):
                    at_h = (TURNS["cx_so"][0] % 2) * 1024 + 2 * h * P + h * NEW
                    new = bass.AP(tensor=G, offset=at_h, ap=[[2048, P], [P, 2], [HEADS * NEW, SAMPLES], [1, NEW]])
                    hi, lo = (y[:, 2 * h:2 * h + 2, SEQ:T].rearrange("p k (b t) -> p k b t", b=SAMPLES) for y in (y_hi, y_lo))
                    dve.tensor_copy(hi, new)
                    parts.append((new, hi, lo))
                dve.drain()
                for new, hi, lo in parts:
                    last = tt(lo, new, hi.bitcast(F32), ALU.subtract)
                last.then_inc(y_ready, 1)
                free(dve.drain())
                for n in range(4):
                    split(L, 0, UNITS["co"] + n + 1)
                    if n > 0:
                        norm_in(L, 3, n - 1)
                    residual(L, TURNS["co"][n], n, 1.0)
                norm_in(L, 3, 3)
                dve.sem_inc(mixer_idle, 1)
                dve.wait_ge(tiles_free, 2 * L + 2)
                norm_root(L, 3)
                ffn(L, 1, "f2in", "f2out")

            for c in range(3):
                n = P if c < 2 else TS
                dve.wait_ge(start_turned, 10 + c + 1)
                dve.tensor_copy(y_rows[0:n, c, :].rearrange("p (b d) -> p b d", b=2), M[0:n, 2 * (c % 2):2 * (c % 2) + 2, :]
                                ).then_inc(rows_ready, 1)

        @block.tensor
        def _(pe):
            def mm(out, lhsT, rhs, start=True, stop=True, **kw):
                return pe.matmul(out, lhsT, rhs, start=start, stop=stop, **kw)

            def take(L, t, i=0):
                pe.wait_ge(acc_free, turn_value(L, i, t))
                return G[:, t % 2, :, :]

            def unit(L, i, u, pair, rhs, first=True, last=True, nk=8, k0=0, tokens=T, wait=None):
                for k in range(nk):
                    if k % (nk // 2) == 0:
                        pe.wait_ge(lo_ready, half_value(L, i, u, k // (nk // 2)) + 4)
                    if wait is not None:
                        wait(k0 + k)
                    r_hi, r_lo = rhs(k0 + k)
                    for m in range(2):
                        s = slice((2 * k + m) * P, (2 * k + m + 1) * P)
                        out = pair[:, m, 0:tokens]
                        mm(out, w_hi[:, u % 2, s], r_hi, first and k == 0, False)
                        mm(out, w_hi[:, u % 2, s], r_lo, False, False)
                        ins = mm(out, w_lo[:, u % 2, s], r_hi, False, last and k == nk - 1)
                return ins.then_inc(acc_ready if last else unit_used, 1)

            def norm(L, n):
                for k in range(KD):
                    if k % 2 == 0:
                        pe.wait_ge(sq_ready, L * 16 + 4 * n + k // 2 + 1)
                    ins = mm(M[:, STAT, 0:T], ones[:, :], x_squares[:, k, :], k == 0, k == KD - 1)
                ins.then_inc(stat_ready, 1)

            def h(k):
                return h_hi[:, k, :], h_lo[:, k, :]

            def h_wait(L, n):
                return lambda k: pe.wait_ge(h_ready, L * 32 + 8 * n + k + 1)

            def ffn(L, which, n, fin, fout):
                norm(L, n)
                with pe.Fori(0, KF // 2) as i:
                    for j in range(2):
                        pair = take(L, TURNS[fin][j], i)
                        unit(L, i, UNITS[fin] + j, pair, h, wait=h_wait(L, n))
                for m in range(4):
                    pair = take(L, TURNS[fout][m])
                    for q, nk in enumerate(OUT_PARTS):
                        unit(L, 0, UNITS[fout] + 3 * m + q, pair, lambda k: (g_hi[:, k, :], g_lo[:, k, :]),
                                   q == 0, q == 2, nk, 8 * q,
                                   wait=(lambda k: pe.wait_ge(g_ready, L * (2 * KF) + which * KF + k + 1)) if m == 0 else None)

            def turn(out, in_, n=P):
                return pe.transpose(out, in_, ident[0:n, 0:n])

            pe.sem_inc(acc_ready, 2)
            pe.wait_ge(const_landed, 16)
            pe.wait_ge(fills_done, 5)
            pe.wait_ge(rows_landed, 16 * len(PROWS))
            for layer in range(DEPTH):
                ins = turn(M[:, 0, layer * N_PROWS:(layer + 1) * N_PROWS], param_rows[0:N_PROWS, layer, :], N_PROWS)
            ins.then_inc(start_turned, 1)
            for n in range(1, 9):
                src = 0 if n < 5 else 1
                pe.wait_ge(mem_norm, 2) if n < 5 else pe.wait_ge(x_landed, 32)
                if n >= 4:
                    pe.wait_ge(start_taken, n - 3)
                for e in range(2):
                    k = 2 * ((n - 1) % 4) + e
                    for c in range(2):
                        ins = turn(M[:, n % 4, 256 * e + P * c:256 * e + P * c + P], rows_in[:, src, c, k * P:(k + 1) * P])
                ins.then_inc(start_turned, 1)
            pe.wait_ge(start_taken, 6)
            for k in range(KD):
                ins = turn(M[:, 1, k * TS:(k + 1) * TS], x_sample_rows[:, k * P:(k + 1) * P], TS)
            ins.then_inc(start_turned, 1)
            pe.wait_ge(start_taken, 10)

            with pe.Fori(0, DEPTH) as L:
                ffn(L, 0, 0, "f1in", "f1out")
                norm(L, 1)
                pair = take(L, TURNS["state_in"][0])
                pe.wait_ge(states_in, L * 32 + 32)
                for c in range(2):
                    for half in range(2):
                        turn(pair[:, 0, 240 * c + 120 * half:240 * c + 120 * half + 120], conv_rows[0:120, half, c * P:(c + 1) * P], 120)
                    ins = turn(pair[:, 1, 120 * c:120 * c + 120], pool_rows[0:120, c * P:(c + 1) * P], 120)
                ins.then_inc(acc_ready, 1)
                def win(n):
                    pair = take(L, TURNS["win"][n])
                    unit(L, 0, UNITS["win"] + n, pair, h, wait=h_wait(L, 1))

                def rows32(b):
                    return slice(32 * (b // 2), 32 * (b // 2) + 32)

                def att_scores(b):
                    pe.wait_ge(acc_free, passed(L, 0, TURNS["att_k"][b]))
                    for hd in range(HEADS):
                        ins = mm(M[rows32(b), SCORES, 0:PAST], q_diag[:, 0, b * HEADS + hd, :], att_kt[:, b % 2, hd, :],
                                 b % 2 == 0 and hd == 0, b % 2 == 1 and hd == HEADS - 1, skip_group_check=True)
                    ins.then_inc(score_done, 1)

                def att_keys(b):
                    pair = take(L, TURNS["att_k"][b])
                    pe.wait_ge(kv_landed[kv_slot(b)], kv_value(L, False, b))
                    for hd in range(HEADS):
                        for c in range(PAGES):
                            col = 256 * (hd % 2) + P * c
                            ins = turn(pair[:, hd // 2, col:col + P], att_kv[:, b % 2, c, hd * P:(hd + 1) * P])
                    ins.then_inc(acc_ready, 1)
                    if b == 1:
                        pe.wait_ge(q_diag_ready, L * 2 + 1)
                    if b > 0:
                        att_scores(b - 1)

                for n in range(5):
                    win(n)
                pair = take(L, TURNS["qk_stat"][0])
                for k in range(KD):
                    if k % 2 == 0:
                        pe.wait_ge(zsq_ready, L * 8 + k // 2 + 1)
                    ins = mm(pair[0:KD, 0, 0:T], into_row(k), qk_squares[:, k, :], k == 0, k == KD - 1)
                ins.then_inc(acc_ready, 1)
                win(5)
                pe.wait_ge(r_ready, L * 2 + 1)
                for j in range(4):
                    pair = take(L, TURNS["qk_root"][j])
                    for e in range(2):
                        ins = mm(pair[:, e, 0:T], from_row(2 * j + e), qk_rms[0:KD, :])
                    ins.then_inc(acc_ready, 1)
                win(6)
                for j in range(4):
                    pair = take(L, TURNS["rope"][j])
                    pe.wait_ge(z_normed, L * 4 + j + 1)
                    for e in range(2):
                        ins = mm(pair[0:ROPE_DIM, e, 0:T], cc("swap"), z[:, 2 * j + e, :])
                    ins.then_inc(acc_ready, 1)
                att_keys(0)
                att_keys(1)
                win(7)
                att_keys(2)
                att_keys(3)
                win(8)
                for b in range(4, SAMPLES):
                    att_keys(b)
                att_scores(SAMPLES - 1)
                pe.wait_ge(z_done, L * 5 + 4)
                for c in range(3):
                    pair = take(L, TURNS["tok"][c])
                    n = P if c < 2 else TS
                    for hd in range(HEADS):
                        turn(pair[0:n, 0, hd * P:(hd + 1) * P], z[:, HEADS + hd, c * P:c * P + n])
                        ins = turn(pair[0:n, 1, hd * P:(hd + 1) * P], v_t[:, hd, c * P:c * P + n])
                    ins.then_inc(acc_ready, 1)
                for b in range(SAMPLES):
                    for hd in range(HEADS):
                        ins = mm(M[rows32(b), NEWS, 0:TS], q_diag[:, 0, b * HEADS + hd, :], z[:, HEADS + hd, SEQ:T],
                                 b % 2 == 0 and hd == 0, b % 2 == 1 and hd == HEADS - 1, skip_group_check=True)
                ins.then_inc(news_done, 1)
                for j in range(2):
                    pair = take(L, TURNS["att_s"][j])
                    for e in range(2):
                        hd = 2 * j + e
                        mm(pair[:, e, 0:P], z[:, hd, 0:P], z[:, HEADS + hd, 0:P])
                        ins = mm(pair[:, e, P:384], z[:, hd, P:SEQ], z[:, HEADS + hd, 0:SEQ])
                    ins.then_inc(acc_ready, 1)
                pair = take(L, TURNS["pool"][0])
                pe.wait_ge(pooled, L + 1)
                pe.wait_ge(mixer_params, L * 96 + 96)
                for c in range(2):
                    d = pool_diff(c)
                    mm(pair[:, c, 0:SEQ], pool_w[:, c, :], d[:, PBUF:PBUF + SEQ])
                    new = d[:, PBUF + SEQ:].rearrange("p (b r) -> p b r", b=SAMPLES)[:, :, PBUF:]
                    ins = mm(pair[:, c, SEQ:T].rearrange("p (b t) -> p b t", b=SAMPLES), pool_w[:, c, :], new)
                ins.then_inc(acc_ready, 1)
                pair = take(L, TURNS["state_out"][0])
                pe.wait_ge(fresh_ready, L + 1)
                for k in range(4):
                    turn(pair[0:TS, 0, k * P:(k + 1) * P], fresh[:, k, :])
                for c in range(2):
                    turn(pair[0:PBUF, 1, c * P:(c + 1) * P], pxt[:, c, SEQ:SEQ + PBUF])
                    ins = turn(pair[0:CBUF, 1, 256 + c * P:256 + (c + 1) * P], cxt[:, c, SEQ:SEQ + CBUF])
                ins.then_inc(acc_ready, 1)
                pe.wait_ge(conv_done, L + 1)
                for c in range(2):
                    ins = mm(M[:, STAT, 0:T], ones[:, :], conv_acc[:, c, :], c == 0, c == 1)
                ins.then_inc(ln_sum, 1)
                for j in range(2):
                    pair = take(L, TURNS["att_pt"][j])
                    pe.wait_ge(p_probs, L * 16 + 4 * j + 4)
                    for e in range(2):
                        hd = 2 * j + e
                        turn(pair[:, e, 0:P], probs[:, hd, 0:P])
                        turn(pair[:, e, P:2 * P], probs[:, hd, P:2 * P])
                        ins = turn(pair[:, e, 2 * P:3 * P], probs[:, hd, 2 * P:3 * P])
                    ins.then_inc(acc_ready, 1)
                pe.wait_ge(s_probs, L * 2 + 1)
                for c in range(2):
                    turn(M[:, SCORES, c * P:(c + 1) * P], sprobs[:, c * P:(c + 1) * P])
                turn(M[0:TS, SCORES, 2 * P:3 * P], sprobs[:, 2 * P:]).then_inc(s_turned, 1)
                pe.wait_ge(ln_sq, L + 1)
                for c in range(2):
                    ins = mm(M[:, STAT, 0:T], ones[:, :], conv_sq[:, c, :], c == 0, c == 1)
                ins.then_inc(ln_var, 1)
                for j in range(2):
                    pair = take(L, TURNS["att_o"][j])
                    pe.wait_ge(acc_free, passed(L, 0, TURNS["att_pt"][j]))
                    for e in range(2):
                        hd = 2 * j + e
                        s = slice(hd * P, (hd + 1) * P)
                        mm(pair[:, e, 0:P], v_tok[:, 0, s], probs_t[:, hd, 0:P])
                        mm(pair[:, e, P:SEQ], v_tok[:, 0, s], probs_t[:, hd, P:SEQ], True, False)
                        ins = mm(pair[:, e, P:SEQ], v_tok[:, 1, s], probs_t[:, hd, SEQ:384], False, True)
                    ins.then_inc(acc_ready, 1)
                pe.wait_ge(s_probs_t, L * 2 + 1)
                mm(M[:, OUTS, :], new_probs_t[0:TS, :], v_tok[0:TS, 2, :], True, False, skip_group_check=True)

                def att_values(b):
                    n = SAMPLES + b
                    tile = att_v2 if b % 4 >= 2 else att_kv
                    pe.wait_ge(kv_landed[kv_slot(n)], kv_value(L, False, n))
                    for c in range(PAGES):
                        ins = mm(M[rows32(b), OUTS, :], p_diag[:, c, b, :], tile[:, b % 2, c, :], False, b % 2 == 1 and c == PAGES - 1,
                                 skip_group_check=True)
                    ins.then_inc(v_used, 1)

                for b in range(SAMPLES):
                    att_values(b)
                pair = take(L, TURNS["pw"][0])
                pe.wait_ge(conv_silu, L + 1)
                for m in range(2):
                    for k in range(2):
                        ins = mm(pair[:, m, 0:T], pw_w[:, k, m * P:(m + 1) * P], conv_act[:, k, :], k == 0, k == 1)
                ins.then_inc(acc_ready, 1)
                pair = take(L, TURNS["att_so"][0])
                pe.wait_ge(s_rows_out, L * 2 + 1)
                for hd in range(HEADS):
                    ins = turn(pair[:, 0, hd * P:(hd + 1) * P], att_out_rows[:, hd * P:(hd + 1) * P])
                ins.then_inc(acc_ready, 1)
                def y(k):
                    return y_hi[:, k, :], y_lo[:, k, :]

                pe.wait_ge(y_ready, L * 6 + 5)
                for n in range(4):
                    pair = take(L, TURNS["wout"][n])
                    unit(L, 0, UNITS["wout"] + n, pair, y)
                norm(L, 2)
                for n in range(4):
                    pair = take(L, TURNS["cq"][n])
                    unit(L, 0, UNITS["cq"] + n, pair, h, wait=h_wait(L, 2))
                def ckv(n):
                    u = UNITS["ckv"] + n
                    pair = take(L, TURNS["ckv"][n])
                    for k in range(KD):
                        if k % 4 == 0:
                            pe.wait_ge(lo_ready, half_value(L, 0, u, k // 4) + 4)
                        s = slice(k * 256, (k + 1) * 256)
                        for c in range(2):
                            tok = slice(c * P, (c + 1) * P)
                            out = pair[:, c, 0:256]
                            mm(out, y_hi[:, k, tok], w_hi[:, u % 2, s], k == 0, False)
                            mm(out, y_hi[:, k, tok], w_lo[:, u % 2, s], False, False)
                            ins = mm(out, y_lo[:, k, tok], w_hi[:, u % 2, s], False, k == KD - 1)
                    ins.then_inc(acc_ready, 1)

                def mem_keys(b):
                    pe.wait_ge(kv_landed[kv_slot(b)], kv_value(L, True, b))
                    for half in range(2):
                        pair = take(L, TURNS["mem_k"][2 * b + half])
                        for q in range(4):
                            for c in range(2):
                                hd = 4 * half + q
                                col = 256 * (q % 2) + P * c
                                ins = turn(pair[:, q // 2, col:col + P], mem_kv[:, b % 2, c, hd * P:(hd + 1) * P])
                        ins.then_inc(acc_ready, 1)

                def mem_scores(b):
                    pe.wait_ge(acc_free, passed(L, 0, TURNS["mem_k"][2 * b + 1]))
                    for hd in range(KD):
                        ins = mm(M[rows32(b), SCORES, 0:N_MEM], q_diag[:, hd % 2, b * HEADS + hd // 2, :], mem_kt[:, b % 2, hd, :],
                                 b % 2 == 0 and hd == 0, b % 2 == 1 and hd == KD - 1, skip_group_check=True)
                    ins.then_inc(score_done, 1)

                def mem_values(b):
                    n = SAMPLES + b
                    tile = mem_v2 if b % 4 >= 2 else mem_kv
                    pe.wait_ge(kv_landed[kv_slot(n)], kv_value(L, True, n))
                    for half in range(2):
                        for c in range(2):
                            ins = mm(M[rows32(b), OUTS + half, :], p_diag[:, c, b, :], tile[:, b % 2, c, half * 512:(half + 1) * 512],
                                     b % 2 == 0 and c == 0, b % 2 == 1 and c == 1, skip_group_check=True)
                    ins.then_inc(v_used, 1)

                pe.wait_ge(m_ready, L * 8 + 8)
                for n in range(4):
                    ckv(n)
                    if n == 0:
                        pair = take(L, TURNS["cq_stat"][0])
                        for k in range(KD):
                            if k % 2 == 0:
                                pe.wait_ge(zsq_ready, L * 8 + 4 + k // 2 + 1)
                            ins = mm(pair[0:KD, 0, 0:T], into_row(k // 2), squares[:, k, :], k == 0, k == KD - 1)
                        ins.then_inc(acc_ready, 1)
                    for b in (2 * n, 2 * n + 1):
                        if b == 1:
                            pe.wait_ge(r_ready, L * 2 + 2)
                            for j in range(2):
                                pair = take(L, TURNS["cq_root"][j])
                                for e in range(2):
                                    ins = mm(pair[:, e, 0:T], from_row(2 * j + e), cq_rms[0:KD, :])
                                ins.then_inc(acc_ready, 1)
                        mem_keys(b)
                        if b == 1:
                            pe.wait_ge(q_diag_ready, L * 2 + 2)
                        if b > 0:
                            mem_scores(b - 1)
                mem_scores(SAMPLES - 1)
                ckv(4)
                ckv(5)
                pe.wait_ge(mk_ready, L * 8 + 8)
                for j in range(2):
                    pair = take(L, TURNS["mkt"][j])
                    for q in range(4):
                        for c in range(2):
                            hd = 4 * j + q
                            col = 256 * (q % 2) + P * c
                            ins = turn(pair[:, q // 2, col:col + P], mk[:, c, hd * P:(hd + 1) * P])
                    ins.then_inc(acc_ready, 1)
                pe.wait_ge(s_probs, L * 2 + 2)
                for c in range(2):
                    ins = turn(M[:, SCORES, c * P:(c + 1) * P], cx_sprobs[:, c * P:(c + 1) * P])
                ins.then_inc(s_turned, 1)
                ckv(6)
                pe.wait_ge(z_done, L * 5 + 5)
                pe.wait_ge(acc_free, passed(L, 0, TURNS["mkt"][1]))
                for j in range(2):
                    pair = take(L, TURNS["cx_s"][j])
                    for e in range(2):
                        for c in range(2):
                            for d in range(2):
                                hd = 2 * (2 * j + e) + d
                                ins = mm(pair[:, e, 256 * c:256 * c + 256], z[:, hd, c * P:(c + 1) * P], mkt[:, hd, :], d == 0, d == 1)
                    ins.then_inc(acc_ready, 1)
                pe.wait_ge(s_probs_t, L * 2 + 2)
                for b in range(0, 3):
                    mem_values(b)
                ckv(7)
                for b in range(3, 5):
                    mem_values(b)
                for j in range(2):
                    pair = take(L, TURNS["cx_pt"][j])
                    pe.wait_ge(p_probs, L * 16 + 8 + 4 * j + 4)
                    for e in range(2):
                        for c in range(2):
                            for m in range(2):
                                ins = turn(pair[:, e, 256 * m + P * c:256 * m + P * c + P],
                                           cx_probs[:, 2 * j + e, 256 * c + P * m:256 * c + P * m + P])
                    ins.then_inc(acc_ready, 1)
                for b in range(5, SAMPLES):
                    mem_values(b)
                for j in range(2):
                    pair = take(L, TURNS["cx_o"][j])
                    pe.wait_ge(acc_free, passed(L, 0, TURNS["cx_pt"][j]))
                    for e in range(2):
                        hh = 2 * j + e
                        for d in range(2):
                            s = slice((2 * hh + d) * P, (2 * hh + d + 1) * P)
                            for m in range(2):
                                ins = mm(pair[:, e, 256 * d:256 * d + 256], mv[:, m, s], cx_probs_t[:, hh, 256 * m:256 * m + 256], m == 0, m == 1)
                    ins.then_inc(acc_ready, 1)
                pair = take(L, TURNS["cx_so"][0])
                pe.wait_ge(s_rows_out, L * 2 + 2)
                for k in range(KD):
                    ins = turn(pair[:, k // 4, (k % 4) * P:(k % 4 + 1) * P], cx_out_rows[:, k // 4, (k % 4) * P:(k % 4 + 1) * P])
                ins.then_inc(acc_ready, 1)
                pe.wait_ge(y_ready, L * 6 + 6)
                pe.wait_ge(acc_free, passed(L, 0, TURNS["cx_o"][1]))
                for n in range(4):
                    pair = take(L, TURNS["co"][n])
                    unit(L, 0, UNITS["co"] + n, pair, y)
                ffn(L, 1, 3, "f2in", "f2out")

            pe.wait_ge(acc_free, N_TURNS * DEPTH + 2)
            for c in range(3):
                if c == 2:
                    pe.wait_ge(rows_ready, 1)
                n = P if c < 2 else TS
                for k in range(KD):
                    ins = turn(M[0:n, 2 * (c % 2) + k // 4, (k % 4) * P:(k % 4 + 1) * P], x[:, k, c * P:c * P + n])
                ins.then_inc(start_turned, 1)


_OUTS = {
    "y_prompt": (1, SEQ, D_MODEL), "y_sample": (SAMPLES, NEW, D_MODEL),
    "p_att_k": (DEPTH, 1, SEQ, HEADS, DH), "p_att_v": (DEPTH, 1, SEQ, HEADS, DH),
    "p_mem_k": (DEPTH, 1, N_MEM, HEADS, MDH), "p_mem_v": (DEPTH, 1, N_MEM, HEADS, MDH),
    "p_pool": (DEPTH, 1, PBUF, POOL_W), "p_conv": (DEPTH, 1, CBUF, CONV_W),
    "s_att_k": (DEPTH, SAMPLES, NEW, HEADS, DH), "s_att_v": (DEPTH, SAMPLES, NEW, HEADS, DH),
    "s_pool": (DEPTH, SAMPLES, PBUF, POOL_W), "s_conv": (DEPTH, SAMPLES, CBUF, CONV_W),
}


def kernel(**inputs):
    import numpy as _np
    import concourse.bacc as _bacc
    from concourse import mybir as _mybir
    from concourse.bass_utils import run_bass_kernel_spmd as _run

    nc = _bacc.Bacc("TRN2", target_bir_lowering=False, num_devices=1)
    arrays = {f"in_{name}": _np.ascontiguousarray(a) for name, a in inputs.items()}
    arrays["in_shape_constants"] = shape_constants()
    ins = {key[3:]: nc.dram_tensor(key, a.shape, _mybir.dt.from_np(a.dtype), kind="ExternalInput").ap() for key, a in arrays.items()}
    outs = {name: nc.dram_tensor(f"out_{name}", shape, _mybir.dt.float32, kind="ExternalOutput").ap() for name, shape in _OUTS.items()}
    trunk_kernel(nc, ins, outs)
    r = _run(nc, [arrays], core_ids=[0])
    return tuple(r.results[0][f"out_{name}"] for name in _OUTS)
```

```python
from contextlib import ExitStack

import numpy as np

import concourse.bass as bass
from concourse import mybir

F32 = mybir.dt.float32
F32R = mybir.dt.float32r
I32 = mybir.dt.int32
ACT = mybir.ActivationFunctionType
ALU = mybir.AluOpType
AX = mybir.AxisListType

P = 128
D_MODEL, SEQ, DEPTH, SAMPLES, NEW, PAST, PAGE = 1024, 256, 2, 8, 4, 256, 128
TS = SAMPLES * NEW
T = SEQ + TS
KD = D_MODEL // P
D_FF = ((8 * D_MODEL // 3 + 127) // 128) * 128
KF = D_FF // P
POOL_W, CONV_W, HEADS, DH = 256, 256, 4, 128
ATT_W = HEADS * DH
WINDOWS = (2, 4, 8, 16)
PBUF, CONV_K = max(WINDOWS) - 1, 31
CBUF = CONV_K - 1
N_MEM, MDH = 256, 256
PAGES = PAST // PAGE
ROPE_DIM, THETA = DH // 4, 500000.0
EPS = 1e-6
MASKED = -1e30
PX = PBUF + SEQ + SAMPLES * (PBUF + NEW)
CX = CBUF + SEQ + SAMPLES * (CBUF + NEW)
ROWS = SAMPLES * HEADS * NEW

COLS = {}
_at = 0
for _name, _n in (("ident", P), ("causal", P), ("own", TS), ("pick", 2 * KD - 1), ("inv_win", 2), ("inv_first", 2 * max(WINDOWS)), ("cos", T), ("sin", T), ("swap", ROPE_DIM)):
    COLS[_name] = (_at, _at + _n)
    _at += _n
N_CONST = _at

PROWS = {}
_at = 0
for _name, _n in (("ln_ffn1", 8), ("ln_mix", 8), ("ln_cross", 8), ("ln_mem", 8), ("ln_ffn2", 8), ("pool_scale", 2),
                  ("conv_dw_b", 2), ("conv_ln_g", 2), ("conv_ln_b", 2), ("conv_pw_b", 2), ("att_q_norm", 1),
                  ("att_k_norm", 1), ("cq_norm", 2), ("conv_dw_w", 2 * CONV_K)):
    PROWS[_name] = (_at, _n)
    _at += _n
N_PROWS = _at
PARAMS_BY_POOL = ("conv_dw_w", "conv_dw_b", "conv_ln_g", "conv_ln_b", "conv_pw_b")
PARAMS_BY_ACT = tuple(_n for _n in PROWS if _n not in PARAMS_BY_POOL)

CX_ORDER = []
for _n in range(4):
    CX_ORDER += ["ckv"] + (["cq_stat"] + ["mem_k"] * 2 + ["cq_root"] * 2 + ["mem_k"] * 2 if _n == 0 else ["mem_k"] * 4)
CX_ORDER += ["ckv", "ckv", "mkt", "mkt", "ckv", "cx_s", "cx_s", "ckv", "cx_pt", "cx_pt", "cx_o", "cx_o", "cx_so"]
MIX_ORDER = (["state_in"] + ["win"] * 6 + ["qk_stat", "win"] + ["qk_root"] * 4 + ["win"] + ["rope"] * 2 + ["att_k"] + ["rope"] * 2 + ["att_s", "att_k", "att_s"]
             + ["att_k"] * 2 + ["win"] + ["att_k"] * 2 + ["att_pt"] * 2 + ["att_k"] * 2 + ["tok"] * 3 + ["pool", "state_out"]
             + ["att_o"] * 2 + ["pw", "att_so"])
WIN_COLUMNS = (1, 2, 3, 4, 5, 6, 0, 7, 8)
UNITS, TURNS = {}, {}
_u = _t = 0
for _name, _nu, _nt in (("f1in", KF, KF), ("f1out", 12, 4), ("win", 9, 0),
                        *((_n, 0, 1) for _n in MIX_ORDER), ("wout", 4, 4),
                        ("cq", 4, 4), ("ckv", 8, 0), *((_n, 0, 1) for _n in CX_ORDER), ("co", 4, 4), ("f2in", KF, KF),
                        ("f2out", 12, 4)):
    if _nu:
        UNITS[_name] = _u
    TURNS.setdefault(_name, []).extend(range(_t, _t + _nt))
    _u += _nu
    _t += _nt
N_UNITS = _u
RING_UNITS = N_UNITS + N_UNITS % 2
N_TURNS = _t
assert N_TURNS % 2 == 0
ROPE_ORDER = (0, 2, 1, 3)
FIRST = 0
UNIT = 2048
OUT_PARTS = (8, 8, KF - 16)


def shape_constants():
    c = np.zeros((P, N_CONST), np.float32)

    def put(name, a):
        c[:a.shape[0], COLS[name][0]:COLS[name][0] + a.shape[1]] = a

    put("ident", np.eye(P, dtype=np.float32))
    put("causal", np.where(np.arange(P)[None, :] <= np.arange(P)[:, None], 0.0, MASKED).astype(np.float32))
    rb, rt = np.arange(ROWS) // (HEADS * NEW), np.arange(ROWS) % NEW
    cb, ct = np.arange(TS) // NEW, np.arange(TS) % NEW
    ok = (rb[:, None] == cb[None, :]) & (ct[None, :] <= rt[:, None])
    put("own", np.where(ok, 0.0, MASKED).astype(np.float32))
    pick = np.zeros((P, 2 * KD - 1), np.float32)
    pick[:, KD - 1] = 1.0
    put("pick", pick)
    inv, first = np.zeros((P, 2), np.float32), np.zeros((P, 2, max(WINDOWS)), np.float32)
    for g, win in enumerate(WINDOWS):
        rows = slice(64 * (g % 2), 64 * (g % 2) + 64)
        inv[rows, g // 2] = 1.0 / win
        first[rows, g // 2, :] = 1.0 / np.minimum(np.arange(max(WINDOWS)) + 1, win)
    put("inv_win", inv)
    put("inv_first", first.reshape(P, -1))
    half = ROPE_DIM // 2
    freq = np.power(np.float32(THETA), -np.arange(half, dtype=np.float32) / np.float32(half)).astype(np.float32)
    pos = np.concatenate([np.arange(SEQ), PAST + np.arange(TS) % NEW]).astype(np.float32)
    ang = (pos[None, :] * freq[:, None]).astype(np.float32)
    put("cos", np.concatenate([np.cos(ang), np.cos(ang)]).astype(np.float32))
    put("sin", np.concatenate([-np.sin(ang), np.sin(ang)]).astype(np.float32))
    put("swap", np.roll(np.eye(ROPE_DIM, dtype=np.float32), half, axis=0))
    return c


def trunk_kernel(nc, a, o):
    with ExitStack() as ctx:
        cursor = [nc.sbuf_base + (-nc.sbuf_base) % 64]

        def at(name, shape, dt, offset):
            return nc.alloc_sbuf_tensor_at(name, [P, *shape], dt, offset=offset)

        def region(n_elems):
            start = cursor[0]
            cursor[0] += 4 * n_elems
            cursor[0] += (-cursor[0]) % 32
            return start

        def sb(name, shape, dt=F32):
            return at(name, shape, dt, region(int(np.prod(shape))))

        raw = sb("raw_weights", [2, UNIT])
        w_hi = sb("w_hi", [2, UNIT], F32R)
        w_lo = sb("w_lo", [2, UNIT], F32R)
        x = sb("x_residual", [KD, T])
        const = sb("shape_consts", [N_CONST])
        prm_all = sb("params_all", [DEPTH, N_PROWS])
        prm = sb("params", [N_PROWS])
        ck_gain = sb("ck_gain", [MDH])
        pool_w = sb("pool_w_blocks", [2, P])
        pw_w = sb("conv_pw_w", [2, CONV_W])
        mem_t = sb("mem_normed", [KD, N_MEM])
        q_diag = sb("q_diag", [2, SAMPLES * HEADS, 32])
        p_diag = sb("p_diag", [2, SAMPLES, 32])
        ones = sb("ones", [P])
        small = sb("small", [96])
        pages = nc.alloc_sbuf_tensor_at("pages", [1, SAMPLES * PAGES], I32, offset=region(SAMPLES * PAGES))
        h_at = region(2 * KD * T)
        h_hi = at("h_hi", [KD, T], F32R, h_at)
        h_lo = at("h_lo", [KD, T], F32R, h_at + 4 * KD * T)
        hh0, hl0 = h_at, h_at + 4 * KD * T
        squares = at("squares", [KD, T], F32, hl0)
        cq_rms = at("cq_rms", [T], F32, hh0)
        conv_sq = at("conv_sq", [2, T], F32, hh0 + 16 * T)
        conv_act = at("conv_act", [2, T], F32, hh0 + 24 * T)
        sprobs = at("att_sample_probs", [PAST + TS], F32, hl0 + 6144)
        new_probs_t = at("att_new_probs_t", [ROWS], F32, hl0 + 6144 + 4 * (PAST + TS))
        cx_probs = at("cx_probs", [HEADS, 512], F32, hl0)
        cx_sprobs = at("cx_sample_probs", [N_MEM], F32, hh0)
        att_out_rows = at("att_out_rows", [ATT_W], F32, hh0)
        cx_out_rows = at("cx_out_rows", [2, 512], F32, hh0 + 4 * N_MEM)
        y_at = region(2 * KD * T)
        y_hi = at("y_hi", [KD, T], F32R, y_at)
        y_lo = at("y_lo", [KD, T], F32R, y_at + 4 * KD * T)
        norm_tmp = at("norm_tmp", [KD, T], F32, y_at + 4 * KD * T)
        qk_squares = at("qk_squares", [KD, T], F32, y_at)
        probs = at("att_probs", [HEADS, 384], F32, y_at)
        qk_rms = at("qk_rms", [T], F32, y_at + 4 * KD * T)
        rope_tmp = at("rope_tmp", [2, T], F32, y_at + 4 * KD * T + 4 * T)
        mix_tmp_at = region(2 * T)
        gate_up = at("gate_up", [2, T], F32, mix_tmp_at)
        mix_tmp = at("mix_tmp", [2, T], F32, mix_tmp_at)
        norm_r = sb("norm_r", [T])
        kv_at = region(2 * 2048)
        mem_kv = at("mem_kv", [2, 2, D_MODEL], F32, kv_at)
        att_kv = at("att_kv", [2, PAGES, ATT_W], F32, kv_at)
        rows_in = at("rows_in", [2, 2, D_MODEL], F32, kv_at)
        conv_a = at("conv_a", [2, T], F32, kv_at + 8192)
        conv_gate = at("conv_gate", [2, T], F32, kv_at + 8192 + 8 * T)
        conv_acc = at("conv_acc", [2, T], F32, kv_at + 8192 + 16 * T)
        kt_at = region(2 * 2048)
        x_squares = at("x_squares", [KD, T], F32, kt_at)
        mem_v2 = at("mem_v2", [2, 2, D_MODEL], F32, kt_at)
        att_v2 = at("att_v2", [2, PAGES, ATT_W], F32, kt_at)
        mem_kt = at("mem_kt", [2, KD, N_MEM], F32, kt_at)
        att_kt = at("att_kt", [2, HEADS, PAST], F32, kt_at)
        win_a = at("win_a", [PX], F32, kt_at + 8192)
        win_b = at("win_b", [PX], F32, kt_at + 8192 + 1696)
        win_c = at("win_c", [PX], F32, kt_at + 8192 + 2 * 1696)
        tap_products = at("tap_products", [TS, CONV_K], F32, kt_at + 8192)
        pool_rows = at("pool_rows", [POOL_W], F32, kt_at + 8192 + 3 * 1696)
        conv_rows = at("conv_rows", [2, CONV_W], F32, kt_at + 8192 + 3 * 1696 + 1024)
        param_rows = at("param_rows", [DEPTH, P], F32, kt_at)
        arena = region(2 * KF * T)
        g_hi = at("g_hi", [KF, T], F32R, arena)
        g_lo = at("g_lo", [KF, T], F32R, arena + 4 * KF * T)
        zpos = [arena]

        def az(name, shape):
            start = zpos[0]
            zpos[0] += (4 * int(np.prod(shape)) + 31) // 32 * 32
            assert zpos[0] <= arena + 8 * KF * T, name
            return at(name, shape, F32, start)

        z = az("z_qk", [KD, T])
        after_z = zpos[0]
        v_t = az("v_t", [HEADS, T])
        k_tok = az("k_tok", [3, ATT_W])
        v_tok = az("v_tok", [3, ATT_W])
        pxt = az("pool_ext", [2, PX])
        cxt = az("conv_ext", [2, CX])
        pool_d = az("pool_diff", [2, PX])
        fresh = az("fresh", [4, TS])
        probs_t = az("att_probs_t", [HEADS, 384])
        sstate = az("sample_state", [2 * POOL_W])
        pstate = az("prompt_state", [2, POOL_W])
        zpos[0] = after_z
        mk = az("mk", [2, D_MODEL])
        mv = az("mv", [2, D_MODEL])
        mkt = az("mk_t", [KD, N_MEM])
        cx_probs_t = az("cx_probs_t", [HEADS, 512])
        zpos[0] = arena
        y_rows = az("y_rows", [3, D_MODEL])
        assert cursor[0] <= nc.sbuf_usable_end, (cursor[0], nc.sbuf_usable_end)

        G = ctx.enter_context(nc.psum_tensor("pairs", [P, 2, 2, 512], F32))
        M = ctx.enter_context(nc.psum_tensor("fixed", [P, 4, 512], F32))
        SCORES, STAT, OUTS, NEWS = 0, 1, 2, 3

        def sem(name):
            return ctx.enter_context(nc.semaphore(name))

        raw_landed = [sem(f"raw_landed{i}") for i in range(2)]
        hi_ready, lo_ready, unit_used = sem("hi_ready"), sem("lo_ready"), sem("unit_used")
        acc_ready, acc_free = sem("acc_ready"), sem("acc_free")
        const_landed, rows_landed, pages_landed = sem("const_landed"), sem("rows_landed"), sem("pages_landed")
        act_rows_landed = sem("act_rows_landed")
        mem_landed, x_landed = sem("mem_landed"), sem("x_landed")
        fills_done, start_turned, start_taken = sem("fills_done"), sem("start_turned"), sem("start_taken")
        mem_sq, mem_norm = sem("mem_squared"), sem("mem_normed_s")
        sq_ready, stat_ready, root_ready, h_ready = (sem(n) for n in ("sq_ready", "stat_ready", "root_ready", "h_ready"))
        gate_scaled, silu_ready, g_ready = sem("gate_scaled"), sem("silu_ready"), sem("g_ready")
        x_rounded, m_rounded = sem("x_rounded"), sem("m_rounded")
        gate_ready, zsq_ready, rq_ready, z_normed, z_done = (
            sem(n) for n in ("gate_ready", "zsq_ready", "rq_ready", "z_normed", "z_done"))
        mixer_idle, mixer_params, states_in = sem("mixer_idle"), sem("mixer_params"), sem("states_in")
        tiles_free, out_landed, carry_landed = sem("tiles_free"), sem("out_landed"), sem("carry_landed")
        pooled, fresh_ready = sem("pooled"), sem("fresh_ready")
        kv_landed = [sem(f"kv_landed{i}") for i in range(4)]
        conv_new_done = sem("conv_new_done")
        act_landed = [sem(f"act_landed{i}") for i in range(2)]
        s_rows_out = sem("s_rows_out")
        kt_whole, act_passed, dve_passed = sem("kt_whole"), sem("act_passed"), sem("dve_passed")
        prm_ready, gate_in = sem("prm_ready"), sem("gate_in")
        r_ready, pool_in, y_rounded = sem("r_ready"), sem("pool_in"), sem("y_rounded")
        v_used, kt_half, score_done = sem("v_used"), sem("kt_half"), sem("score_done")
        q_diag_ready, news_done, s_bias, s_exp, s_probs, s_turned, s_probs_t = (
            sem(n) for n in ("q_diag_ready", "news_done", "s_bias", "s_exp", "s_probs", "s_turned", "s_probs_t"))
        p_bias, p_exp, p_probs = sem("p_bias"), sem("p_exp"), sem("p_probs")
        conv_done, ln_sum, ln_centred, ln_sq, ln_var, ln_root, ln_out, conv_silu = (
            sem(n) for n in ("conv_done", "ln_sum", "ln_centred", "ln_sq", "ln_var", "ln_root", "ln_out", "conv_silu"))
        y_ready, m_ready, mk_sq, mk_root, mk_ready = (
            sem(n) for n in ("y_ready", "m_ready", "mk_sq", "mk_root", "mk_ready"))
        rows_ready, final_landed = sem("rows_ready"), sem("final_landed")
        cx_hi, cx_rows_out = sem("cx_hi"), sem("cx_rows_out")
        cx_bias, sq_summed = sem("cx_bias"), sem("sq_summed")
        sp_passed, pool_passed = sem("sp_passed"), sem("pool_passed")
        x_sample_rows = mem_kt[0:TS, 1, 0:4, :].rearrange("p k c -> p (k c)")

        def cc(name, parts=P):
            return const[0:parts, COLS[name][0]:COLS[name][1]]

        ident = cc("ident")

        def par(name, k=0):
            r = PROWS[name][0] + k
            return prm[:, r:r + 1]

        def ap(t, offset, dims, parts=P, part0=0):
            full = t[part0:part0 + parts]
            return bass.AP(tensor=full.tensor, offset=full.offset + offset, ap=[[full.ap[0][0], parts], *dims])

        def into_row(h):
            at_h = COLS["pick"][0] + KD - 1 - h
            return const[:, at_h:at_h + KD]

        def from_row(h):
            return ap(const, COLS["ident"][0] + h, [[0, P]], KD)

        def conv_new(c):
            return cxt[:, c, CBUF + SEQ:].rearrange("p (b r) -> p b r", b=SAMPLES)

        sm = lambda i, n=1: small[:, i:i + n]
        eps = sm(0)

        def pool_diff(c):
            return pool_d[:, c, :]

        def spread_q(dve, att):
            for d in range(1 if att else 2):
                for odd in range(2):
                    dst = ap(q_diag, d * SAMPLES * HEADS * 32 + odd * (HEADS * 32 + 16), [[256, 4], [36, HEADS], [1, NEW]])
                    src = ap(z, (0 if att else d * T) + SEQ + odd * NEW, [[2 * NEW, 4], [T if att else 2 * T, HEADS], [1, NEW]])
                    last = dve.tensor_copy(dst, src)
            last.then_inc(q_diag_ready, 1)

        def spread_p(dve):
            for c in range(2):
                dst = ap(p_diag, c * SAMPLES * 32, [[64, SAMPLES // 2], [48, 2], [1, HEADS * NEW]])
                ins = dve.tensor_copy(dst, M[:, SCORES, c * P:(c + 1) * P].rearrange("p (b o r) -> p b o r", b=SAMPLES // 2, o=2))
            return ins

        def normalise_probs(dve, L, exp_sem, exp_value, tile, parts, done):
            dve.wait_ge(exp_sem, exp_value)
            dve.reciprocal(sm(48, 8), sm(24, 8))
            dve.drain()
            for h in range(HEADS):
                for c, s in enumerate(parts):
                    dve.tensor_scalar(tile[:, h, s], tile[:, h, s], sm(48 + 2 * h + c), None, ALU.mult).then_inc(done, 1)

        def raw_value(L, i, u):
            per_layer = RING_UNITS // 2 - (u % 2) * (RING_UNITS - N_UNITS)
            return 32 * (L * per_layer + i + u // 2 + 1)

        def half_value(L, i, u, half):
            return L * (2 * RING_UNITS) + i * 4 + (2 * u + half + 1)

        def half_inc(u, half):
            return 1 + (2 * (RING_UNITS - N_UNITS) if (u == N_UNITS - 1 and half) else 0)

        def turn_value(L, i, t):
            return L * N_TURNS + i * 2 + (t + 1)

        def passed(L, i, t):
            return turn_value(L, i, t) + 2

        def release(u):
            prev = u - 2
            if prev < 0:
                return "turn", -1
            for name in UNITS:
                nu = {"f1out": 12, "f2out": 12}.get(name)
                if nu and UNITS[name] <= prev < UNITS[name] + nu:
                    m, q = divmod(prev - UNITS[name], 3)
                    if q < 2:
                        return "unit", 2 * m + q + (8 if name == "f2out" else 0)
                    return "turn", TURNS[name][m]
            name = [n for n in UNITS if UNITS[n] <= prev and (n.startswith("f") or n in ("win", "wout", "cq", "ckv", "co"))][-1]
            return "turn", TURNS[name][prev - UNITS[name]]

        def chunks_of(u):
            for f in ("f1out", "f2out"):
                if UNITS[f] <= u < UNITS[f] + 12:
                    return OUT_PARTS[(u - UNITS[f]) % 3]
            return 8

        def kv_slot(n):
            return n % 2 + (2 if n >= SAMPLES and n % 4 >= 2 else 0)

        def by_act(mem, n):
            return not mem and (2 <= n < SAMPLES + 2 or n in (SAMPLES + 4, SAMPLES + 5))

        def kv_sem(mem, n):
            return act_landed[n % 2] if by_act(mem, n) else kv_landed[kv_slot(n)]

        def kv_value(L, mem, n):
            sizes = [(m, i, PAGES - (PAGES - 1) * m) for m in (False, True) for i in range(2 * SAMPLES) if kv_sem(m, i) is kv_sem(mem, n)]
            done = sum(size for m, i, size in sizes if (m, i) <= (mem, n))
            return L * (16 * sum(size for *_, size in sizes)) + 16 * done

        def page_numbers(eng, n):
            return [eng.value_load(pages[0:1, i:i + 1], min_val=0, max_val=a["cache_att_k"].shape[1] - 1)
                    for i in range((n % SAMPLES) * PAGES, (n % SAMPLES + 1) * PAGES)]

        def load_pages(eng, L, n, numbers):
            cache = a["cache_att_k"] if n < SAMPLES else a["cache_att_v"]
            tile = (att_v2 if kv_slot(n) >= 2 else att_kv)[:, n % 2]
            for c, which in enumerate(numbers):
                eng.dma_start(tile[:, c, :], cache[L, bass.ds(which, 1), :, :, :].rearrange("o p h d -> p (o h d)")
                              ).then_inc(kv_sem(False, n), 16)

        def load_params(eng, names, landed):
            for name in names:
                r, n = PROWS[name]
                src = a[name]
                if name == "conv_dw_w":
                    src = src.rearrange("l j (c p) -> (j c) l p", p=P)
                else:
                    src = src.rearrange("l (c p) -> c l p", p=P)
                eng.dma_start(param_rows[r:r + n, :, :], src).then_inc(landed, 16)

        block = ctx.enter_context(nc.Block())

        @block.sync
        def _(sp):
            sp.dma_start(const[:, :], a["shape_constants"]).then_inc(const_landed, 16)
            sp.dma_start(rows_in[:, 1, :, :], a["x_prompt"].rearrange("o (c p) d -> p (o c) d", p=P)).then_inc(x_landed, 16)
            sp.dma_start(x_sample_rows, a["x_sample"].rearrange("b t d -> (b t) d")).then_inc(x_landed, 16)
            sp.dma_start(rows_in[:, 0, :, :], a["mem_prompt"].rearrange("o (c p) d -> p (o c) d", p=P)).then_inc(mem_landed, 16)
            sp.dma_start(pages[:, :], a["page_table"].rearrange("(o b) c -> o (b c)", o=1)).then_inc(pages_landed, 16)

            def load(L, i, u, src, nk=8, gates=False):
                sp.wait_ge(lo_ready, half_value(L, i, u, 1))
                sp.sem_inc(sp_passed, 1)
                dst = raw[:, u % 2, 0:nk * 256]
                if gates:
                    dst = dst.rearrange("p (k g c) -> p k g c", g=2, c=P)
                    for g in range(2):
                        sp.dma_start(dst[:, :, g, :], src[:, :, g, :]).then_inc(raw_landed[u % 2], 16)
                else:
                    sp.dma_start(dst.rearrange("p (k c) -> p k c", c=256), src).then_inc(raw_landed[u % 2], 32)

            def ffn_in(L, name, w):
                v = w.rearrange("l (k p) (g m c) -> l m p k g c", p=P, g=2, c=P)
                with sp.Fori(0, KF // 2) as i:
                    for j in range(2):
                        load(L, i, UNITS[name] + j, v[L, i * 2 + j], gates=True)

            def ffn_out(L, name, w):
                v = w.rearrange("l (k p) (m c) -> l m p k c", p=P, c=256)
                for m in range(4):
                    for n, nk in enumerate(OUT_PARTS):
                        load(L, 0, UNITS[name] + 3 * m + n, v[L, m, :, 8 * n:8 * n + nk, :], nk)

            def square(L, name, w, order):
                v = w.rearrange("l (k p) (m c) -> l m p k c", p=P, c=256)
                for n, m in enumerate(order):
                    load(L, 0, UNITS[name] + n, v[L, m])

            with sp.Fori(0, DEPTH) as L:
                ffn_in(L, "f1in", a["w_ffn1_in"])
                ffn_out(L, "f1out", a["w_ffn1_out"])
                square(L, "win", a["w_in"], WIN_COLUMNS)
                square(L, "wout", a["w_out"], range(4))
                square(L, "cq", a["w_cq"], range(4))
                square(L, "ckv", a["w_ckv"], range(8))
                square(L, "co", a["w_co"], range(4))
                ffn_in(L, "f2in", a["w_ffn2_in"])
                ffn_out(L, "f2out", a["w_ffn2_out"])
            sp.wait_ge(rows_ready, 3)
            sp.dma_start(o["y_prompt"].rearrange("o (c p) d -> p (o c) d", p=P), y_rows[:, 0:2, :]).then_inc(final_landed, 16)
            sp.dma_start(o["y_sample"].rearrange("b t d -> (b t) d"), y_rows[0:TS, 2, :]).then_inc(final_landed, 16)
            sp.wait_ge(final_landed, 32)

        @block.gpsimd
        def _(pool):
            pool.memset(ones[:, :], 1.0).then_inc(fills_done, 1)
            pool.memset(eps, EPS).then_inc(fills_done, 1)
            pool.memset(q_diag[:, :, :, :], 0.0).then_inc(fills_done, 1)
            pool.memset(p_diag[:, :, :, :], 0.0).then_inc(fills_done, 1)
            pool.memset(pool_w[:, :, :], 0.0).then_inc(fills_done, 1)
            load_params(pool, PARAMS_BY_POOL, rows_landed)
            pool.dma_start(o["s_pool"][:, :, 0:PBUF - NEW, :], a["state_pool"][:, :, NEW:PBUF, :]).then_inc(carry_landed, 16)
            pool.dma_start(o["s_conv"][:, :, 0:CBUF - NEW, :], a["state_conv"][:, :, NEW:CBUF, :]).then_inc(carry_landed, 16)
            pool.wait_ge(pages_landed, 16)
            pool.wait_ge(fills_done, 5)
            pool.wait_ge(start_taken, 10)

            def pooling(c):
                def add(out, a, b):
                    return pool.tensor_tensor(out, a, b, ALU.add)

                e = pxt[:, c, :]
                low, high = slice(0, 64), slice(64, P)
                inv = cc("inv_win")[:, c:c + 1]
                first = cc("inv_first").rearrange("p (c t) -> p c t", c=2)[:, c, :]
                w, w0 = slice(PBUF, PX), slice(PBUF, PBUF + max(WINDOWS))
                add(win_a[:, 1:], e[:, 1:], e[:, :-1])
                pool.drain()
                if c == 0:
                    sums = win_a, win_b
                    add(win_b[high, 3:], win_a[high, 3:], win_a[high, 1:-2])
                else:
                    sums = win_c, win_a
                    add(win_b[:, 3:], win_a[:, 3:], win_a[:, 1:-2])
                    pool.drain()
                    add(win_c[:, 7:], win_b[:, 7:], win_b[:, 3:-4])
                    pool.drain()
                    add(win_a[high, 15:], win_c[high, 15:], win_c[high, 7:-8])
                pool.drain()
                for g, s in zip(sums, (low, high)):
                    pool.tensor_scalar(pool_diff(c)[s, w], g[s, w], inv[s, :], None, ALU.mult)
                pool.drain()
                for g, s in zip(sums, (low, high)):
                    pool.tensor_tensor(pool_diff(c)[s, w0], g[s, w0], first[s, :], ALU.mult)
                pool.drain()
                ins = pool.tensor_tensor(pool_diff(c)[:, w], pool_diff(c)[:, w], e[:, w], ALU.subtract)
                pool.drain()
                return ins

            with pool.Fori(0, DEPTH) as L:
                pool.wait_ge(mixer_idle, L + 1)
                for g in range(4):
                    s = slice(64 * (g % 2), 64 * (g % 2) + 64)
                    pool.dma_start(pool_w[s, g // 2, s], a["pool_w"][L, g]).then_inc(mixer_params, 16)
                pool.dma_start(pw_w[:, :, :], a["conv_pw_w"][L].rearrange("(k p) c -> p k c", p=P)).then_inc(mixer_params, 16)
                pool.dma_start(ck_gain[:, :], a["ck_norm"][L].partition_broadcast(P)).then_inc(mixer_params, 16)
                pool.dma_start(pool_rows[0:120, :], a["state_pool"][L].rearrange("b r c -> (b r) c")).then_inc(states_in, 16)
                pool.dma_start(conv_rows[0:120, :, :], a["state_conv"][L].rearrange("(n b) r c -> (b r) n c", n=2)).then_inc(states_in, 16)
                for n in range(2):
                    load_pages(pool, L, n, page_numbers(pool, n))
                pool.wait_ge(pool_in, L + 1)
                pool.sem_inc(pool_passed, 1)
                for c in range(2):
                    pooling(c)
                pool.sem_inc(pooled, 1)
                for c in range(2):
                    windows = ap(cxt, c * CX + CBUF + SEQ, [[CBUF + NEW, SAMPLES], [1, NEW], [1, CONV_K]])
                    taps = ap(prm, PROWS["conv_dw_w"][0] + c, [[0, SAMPLES], [0, NEW], [2, CONV_K]])
                    products = ap(tap_products, 0, [[NEW * CONV_K, SAMPLES], [CONV_K, NEW], [1, CONV_K]])
                    pool.tensor_tensor(products, windows, taps, ALU.mult)
                    pool.drain()
                    left = CONV_K
                    while left > 1:
                        half = (left + 1) // 2
                        first = ap(tap_products, 0, [[CONV_K, TS], [1, left - half]])
                        pool.tensor_tensor(first, first, ap(tap_products, half, [[CONV_K, TS], [1, left - half]]), ALU.add)
                        pool.drain()
                        left = half
                    pool.tensor_scalar(conv_acc[:, c, SEQ:T], ap(tap_products, 0, [[CONV_K, TS]]), par("conv_dw_b", c), None, ALU.add)
                    pool.drain()
                pool.sem_inc(conv_new_done, 1)
                for b in (2, 3, 6, 7):
                    numbers = page_numbers(pool, b)
                    if b < 4:
                        pool.wait_ge(score_done, L * (2 * SAMPLES) + SAMPLES)
                    else:
                        pool.wait_ge(v_used, L * (2 * SAMPLES) + b - 4 + 1)
                    pool.sem_inc(pool_passed, 1)
                    load_pages(pool, L, SAMPLES + b, numbers)
                pool.wait_ge(acc_free, passed(L, 0, TURNS["state_out"][0]))
                for name, tile in (("att_k", k_tok), ("att_v", v_tok)):
                    pool.dma_start(o["p_" + name][L].rearrange("o (c p) h d -> p (o c) (h d)", p=P), tile[:, 0:2, :]).then_inc(out_landed, 16)
                    pool.dma_start(o["s_" + name][L].rearrange("b t h d -> (b t) (h d)"), tile[0:TS, 2, :]).then_inc(out_landed, 16)
                pool.dma_start(o["s_pool"][L][:, PBUF - NEW:PBUF, :], sstate[0:TS, 0:POOL_W]).then_inc(out_landed, 16)
                pool.dma_start(o["s_conv"][L][:, CBUF - NEW:CBUF, :], sstate[0:TS, POOL_W:]).then_inc(out_landed, 16)
                pool.dma_start(o["p_pool"][L, 0], pstate[0:PBUF, 0, :]).then_inc(out_landed, 16)
                pool.dma_start(o["p_conv"][L, 0], pstate[0:CBUF, 1, :]).then_inc(out_landed, 16)
                pool.wait_ge(out_landed, L * 160 + 128)
                pool.sem_inc(tiles_free, 1)
                pool.wait_ge(conv_silu, L + 1)
                for n in range(2 * SAMPLES):
                    b = n - SAMPLES
                    if n < 2:
                        pool.wait_ge(v_used, L * (2 * SAMPLES) + SAMPLES)
                    elif b < 2:
                        pool.wait_ge(acc_ready, passed(L, 0, TURNS["mem_k"][2 * (n - 2) + 1]))
                    elif b < 4:
                        pool.wait_ge(score_done, L * (2 * SAMPLES) + 2 * SAMPLES)
                    else:
                        pool.wait_ge(v_used, L * (2 * SAMPLES) + SAMPLES + b - 4 + 1)
                    pool.sem_inc(pool_passed, 1)
                    cache = a["cache_mem_k"] if b < 0 else a["cache_mem_v"]
                    tile = (mem_v2 if kv_slot(n) >= 2 else mem_kv)[:, n % 2]
                    pool.dma_start(tile, cache[L, n % SAMPLES].rearrange("(c p) h d -> p c (h d)", p=P)).then_inc(kv_landed[kv_slot(n)], 16)
                pool.wait_ge(mk_ready, L * 8 + 8)
                pool.wait_ge(acc_free, passed(L, 0, TURNS["ckv"][7]))
                pool.dma_start(o["p_mem_k"][L, 0].rearrange("(c p) h d -> p c (h d)", p=P), mk[:, :, :]).then_inc(out_landed, 16)
                pool.dma_start(o["p_mem_v"][L, 0].rearrange("(c p) h d -> p c (h d)", p=P), mv[:, :, :]).then_inc(out_landed, 16)
                pool.wait_ge(out_landed, L * 160 + 160)
                pool.sem_inc(tiles_free, 1)
            pool.wait_ge(carry_landed, 32)

        @block.scalar
        def _(act):
            def copy(out, in_):
                return act.activation(out, in_, ACT.Copy)

            def split(L, i, u, base=0):
                n = chunks_of(u) * 128
                act.wait_ge(raw_landed[u % 2], raw_value(L, i, u))
                kind, n_before = release(u)
                if kind == "turn":
                    act.wait_ge(acc_ready, passed(L, i, n_before))
                else:
                    act.wait_ge(unit_used, L * 16 + n_before + 1)
                for half in range(2):
                    s = slice(half * n, half * n + n)
                    copy(w_hi[:, u % 2, s], raw[:, u % 2, s]).then_inc(hi_ready, half_inc(u, half))

            NORMS = ("ln_ffn1", "ln_mix", "ln_cross", "ln_ffn2")

            def norm_in(L, n, m):
                if n == 0:
                    act.wait_ge(acc_free, passed(L, 0, -1))
                else:
                    act.wait_ge(acc_free, passed(L, 0, TURNS[("", "f1out", "wout", "co")[n]][m]))
                for k in (2 * m, 2 * m + 1):
                    act.activation(h_hi[:, k, :], x[:, k, :], ACT.Copy, scale=par(NORMS[n], k)).then_inc(x_rounded, 1)
                act.activation(x_squares[:, 2 * m:2 * m + 2, :], x[:, 2 * m:2 * m + 2, :], ACT.Square).then_inc(sq_ready, 1)

            def norm_root(L, n):
                act.wait_ge(stat_ready, L * 4 + n + 1)
                act.activation(norm_r[:, :], M[:, STAT, 0:T], ACT.Sqrt, bias=eps, scale=1.0 / D_MODEL).then_inc(root_ready, 1)

            def ffn(L, first, fin, fout):
                u0 = UNITS[fin]

                def pair_in(i):
                    for j in range(2):
                        split(L, i, u0 + j + 1)
                        if i is FIRST and j == 0:
                            norm_root(L, 3 * first)
                        act.wait_ge(gate_scaled, L * (2 * KF) + i * 2 + (first * KF + j + 1))
                        act.activation(gate_up[:, 0, :], gate_up[:, 0, :], ACT.Silu).then_inc(silu_ready, 1)

                pair_in(FIRST)
                with act.Fori(1, KF // 2) as i:
                    pair_in(i)
                u0 = UNITS[fout]
                for n in range(1, 12):
                    split(L, 0, u0 + n)
                    if fout == "f1out" and n in (4, 7, 10):
                        norm_in(L, 1, n // 3 - 1)
                if fout == "f1out":
                    split(L, 0, u0 + 12)
                    norm_in(L, 1, 3)

            load_params(act, PARAMS_BY_ACT, act_rows_landed)
            act.wait_ge(fills_done, 5)
            act.wait_ge(mem_landed, 16)
            for c in range(2):
                act.activation(norm_tmp[:, 4 * c:4 * c + 4, 0:256], rows_in[:, 0, c, :], ACT.Square, accum_out=sm(1 + c))
            act.drain()
            act.activation(sm(3, 2), sm(1, 2), ACT.Sqrt, bias=eps, scale=1.0 / D_MODEL).then_inc(mem_sq, 1)

            act.wait_ge(pages_landed, 16)
            act.wait_ge(start_taken, 6)
            with act.Fori(0, DEPTH) as L:
                split(L, 0, 0)
                act.wait_ge(prm_ready, L + 1)
                for m in range(4):
                    norm_in(L, 0, m)
                ffn(L, 0, "f1in", "f1out")
                def key_half(L, t, n, out):
                    act.wait_ge(acc_ready, passed(L, 0, t))
                    copy(out, G[:, t % 2, 0, :]).then_inc(kt_half, 1)

                def att_keys(b):
                    t = TURNS["att_k"][b]
                    numbers = page_numbers(act, b + 2)
                    if b >= 2:
                        act.wait_ge(score_done, L * 16 + b - 1)
                        act.sem_inc(act_passed, 1)
                    act.wait_ge(acc_ready, passed(L, 0, t))
                    act.sem_inc(act_passed, 1)
                    copy(att_kt[:, b % 2, :, :].rearrange("p h c -> p (h c)"), G[:, t % 2, :, :].rearrange("p e c -> p (e c)")).then_inc(kt_whole, 1)
                    load_pages(act, L, b + 2, numbers)
                    act.drain()
                    act.wait_ge(acc_free, passed(L, 0, t - 1))
                    act.sem_inc(acc_free, 1)

                def prompt_exp(h):
                    act.wait_ge(p_bias, L * 2 + 1)
                    for c, s in ((0, slice(0, 128)), (1, slice(128, 384))):
                        act.activation(probs[:, h, s], probs[:, h, s], ACT.Exp, bias=sm(16 + 2 * h + c), scale=DH ** -0.5,
                                       accum_out=sm(24 + 2 * h + c)).then_inc(p_exp, 1)

                for n in range(9):
                    split(L, 0, UNITS["win"] + n + 1)
                    if n == 0:
                        norm_root(L, 1)
                    if n == 2:
                        act.wait_ge(gate_in, L + 1)
                        act.activation(conv_gate[:, :, :], conv_gate[:, :, :], ACT.Sigmoid).then_inc(gate_ready, 1)
                    if 3 <= n <= 6:
                        act.wait_ge(acc_free, passed(L, 0, TURNS["win"][n - 1]))
                        act.activation(qk_squares[:, 2 * n - 6:2 * n - 4, :], z[:, 2 * n - 6:2 * n - 4, :], ACT.Square).then_inc(zsq_ready, 1)
                    if n == 6:
                        t = TURNS["qk_stat"][0]
                        act.wait_ge(acc_ready, passed(L, 0, t))
                        act.activation(qk_rms[0:KD, :], G[0:KD, t % 2, 0, 0:T], ACT.Sqrt, bias=small[0:KD, 0:1], scale=1.0 / DH).then_inc(rq_ready, 1)
                    if n == 7:
                        for b in range(4):
                            att_keys(b)
                            if b == 2:
                                prompt_exp(0)
                                prompt_exp(1)
                    if n == 8:
                        prompt_exp(2)
                        prompt_exp(3)
                        for b in range(4, SAMPLES):
                            att_keys(b)
                act.wait_ge(s_bias, L * 2 + 1)
                act.activation(sprobs[:, :], sprobs[:, :], ACT.Exp, bias=sm(5), scale=DH ** -0.5, accum_out=sm(6)).then_inc(s_exp, 1)
                act.wait_ge(ln_centred, L + 1)
                act.activation(conv_sq[:, :, :], conv_acc[:, :, :], ACT.Square).then_inc(ln_sq, 1)
                t = TURNS["pool"][0]
                act.wait_ge(acc_ready, passed(L, 0, t))
                for c in range(2):
                    act.activation(y_hi[:, c, :], G[:, t % 2, c, 0:T], ACT.Copy, scale=par("pool_scale", c)).then_inc(y_rounded, 1)
                act.wait_ge(ln_var, L + 1)
                act.activation(norm_r[:, :], M[:, STAT, 0:T], ACT.Sqrt, bias=eps, scale=1.0 / CONV_W).then_inc(ln_root, 1)
                for b in (4, 5):
                    numbers = page_numbers(act, b)
                    act.wait_ge(v_used, L * (2 * SAMPLES) + b - 4 + 1)
                    act.sem_inc(act_passed, 1)
                    load_pages(act, L, SAMPLES + b, numbers)
                act.wait_ge(ln_out, L + 1)
                for c in range(2):
                    last = act.activation(conv_act[:, c, :], conv_acc[:, c, :], ACT.Silu, bias=par("conv_ln_b", c))
                last.then_inc(conv_silu, 1)
                t = TURNS["pw"][0]
                act.wait_ge(acc_ready, passed(L, 0, t))
                for c in range(2):
                    act.activation(y_hi[:, 2 + c, :], G[:, t % 2, c, 0:T], ACT.Identity, bias=par("conv_pw_b", c)).then_inc(y_rounded, 1)
                for n in range(4):
                    split(L, 0, UNITS["wout"] + n + 1)
                    if n > 0:
                        norm_in(L, 2, n - 1)
                norm_in(L, 2, 3)
                for n in range(4):
                    split(L, 0, UNITS["cq"] + n + 1)
                    if n == 0:
                        norm_root(L, 2)
                    for k in (range(0, 2), range(2, 5), range(5, 8), ())[n]:
                        act.activation(y_hi[:, k, 0:N_MEM], mem_t[:, k, :], ACT.Copy, scale=par("ln_mem", k)).then_inc(m_rounded, 1)
                act.wait_ge(acc_ready, passed(L, 0, TURNS["cq"][3]))
                for j in range(4):
                    act.wait_ge(acc_free, passed(L, 0, TURNS["cq"][j]))
                    act.activation(squares[:, 2 * j:2 * j + 2, :], z[:, 2 * j:2 * j + 2, :], ACT.Square).then_inc(zsq_ready, 1)
                for n in range(4):
                    t = TURNS["ckv"][n]
                    split(L, 0, UNITS["ckv"] + n + 1)
                    for c in range(2):
                        act.wait_ge(acc_ready, passed(L, 0, t))
                        act.activation(G[:, t % 2, c, 256:512], G[:, t % 2, c, 0:MDH], ACT.Square,
                                       accum_out=sm(32 + 4 * c + n)).then_inc(mk_sq, 1)
                    if n == 0:
                        t = TURNS["cq_stat"][0]
                        act.wait_ge(acc_ready, passed(L, 0, t))
                        act.activation(cq_rms[0:KD, :], G[0:KD, t % 2, 0, 0:T], ACT.Sqrt, bias=small[0:KD, 0:1], scale=1.0 / MDH).then_inc(rq_ready, 1)
                    for b in (2 * n, 2 * n + 1):
                        for half in range(2):
                            if b >= 2 and half == 0:
                                act.wait_ge(score_done, L * 16 + SAMPLES + b - 1)
                            key_half(L, TURNS["mem_k"][2 * b + half], b,
                                     mem_kt[:, b % 2, 4 * half:4 * half + 2, :].rearrange("p h c -> p (h c)"))
                act.activation(sm(40, 8), sm(32, 8), ACT.Sqrt, bias=eps, scale=1.0 / MDH).then_inc(mk_root, 1)
                split(L, 0, UNITS["ckv"] + 5)
                act.wait_ge(s_bias, L * 2 + 2)
                act.activation(cx_sprobs[:, :], M[:, SCORES, 0:N_MEM], ACT.Exp, bias=sm(5), scale=MDH ** -0.5, accum_out=sm(6)).then_inc(s_exp, 1)
                split(L, 0, UNITS["ckv"] + 6)
                split(L, 0, UNITS["ckv"] + 7)
                for j in range(2):
                    t = TURNS["cx_s"][j]
                    act.wait_ge(cx_bias, L * 2 + j + 1)
                    for e in range(2):
                        h = 2 * j + e
                        for c in range(2):
                            act.activation(cx_probs[:, h, 256 * c:256 * c + 256], G[:, t % 2, e, 256 * c:256 * c + 256], ACT.Exp,
                                           bias=sm(16 + 2 * h + c), scale=MDH ** -0.5, accum_out=sm(24 + 2 * h + c)).then_inc(p_exp, 1)
                split(L, 0, UNITS["co"])
                for j in range(2):
                    if j == 1:
                        act.wait_ge(v_used, L * 16 + 16)
                        copy(cx_out_rows[:, :, :], M[:, OUTS:OUTS + 2, :]).then_inc(cx_rows_out, 1)
                    t = TURNS["cx_o"][j]
                    act.wait_ge(acc_ready, passed(L, 0, t))
                    copy(y_hi[:, 4 * j:4 * j + 4, 0:SEQ].rearrange("p (e k) t -> p e k t", e=2),
                         G[:, t % 2, :, :].rearrange("p e (k t) -> p e k t", k=2)).then_inc(cx_hi, 1)
                for n in range(4):
                    split(L, 0, UNITS["co"] + n + 1)
                    if n > 0:
                        norm_in(L, 3, n - 1)
                norm_in(L, 3, 3)
                ffn(L, 1, "f2in", "f2out")


        @block.vector
        def _(dve):
            def tt(out, in0, in1, op):
                return dve.tensor_tensor(out, in0, in1, op)

            def stt(out, in0, scalar, in1, op0, op1):
                return dve.scalar_tensor_tensor(out, in0, scalar, in1, op0, op1)

            def split(L, i, u):
                n = chunks_of(u) * 128
                for half in range(2):
                    s = slice(half * n, half * n + n)
                    dve.wait_ge(hi_ready, half_value(L, i, u, half))
                    tt(w_lo[:, u % 2, s], raw[:, u % 2, s], w_hi[:, u % 2, s].bitcast(F32), ALU.subtract
                       ).then_inc(lo_ready, half_inc(u, half))

            def hi_lo(items, done, first_step=None):
                n = len(items)
                for k in range(n + 2):
                    if k < n and items[k][0] is not None:
                        items[k][0]()
                    if 1 <= k <= n:
                        _, src, hi, lo = items[k - 1]
                        dve.tensor_copy(hi, src)
                    if k >= 2:
                        _, src, hi, lo = items[k - 2]
                        done(tt(lo, src, hi.bitcast(F32), ALU.subtract), k - 2)
                    if k < n + 1:
                        dve.drain()

            NORMS = ("ln_ffn1", "ln_mix", "ln_cross", "ln_ffn2")

            def norm_in(L, n, m):
                for k in (2 * m, 2 * m + 1):
                    dve.wait_ge(x_rounded, L * 32 + 8 * n + k + 1)
                    stt(h_lo[:, k, :], x[:, k, :], par(NORMS[n], k), h_hi[:, k, :].bitcast(F32), ALU.mult, ALU.subtract).then_inc(h_ready, 1)
                if m > 0:
                    dve.wait_ge(sq_ready, L * 16 + 4 * n + m + 1)
                    ins = tt(x_squares[:, 0:2, :], x_squares[:, 0:2, :], x_squares[:, 2 * m:2 * m + 2, :], ALU.add)
                    if m == 3:
                        ins.then_inc(sq_summed, 1)
                    else:
                        dve.drain()

            def norm_root(L, n):
                dve.wait_ge(root_ready, L * 4 + n + 1)
                dve.reciprocal(norm_r[:, :], norm_r[:, :])
                dve.drain()

            def scaled(out, in_):
                return tt(out, in_, ap(norm_r, 0, [[0, 2], [1, T]]), ALU.mult)

            def free(ins):
                return ins.then_inc(acc_free, 1)

            def acc(L, t, i=0):
                dve.wait_ge(acc_ready, passed(L, i, t))
                return G[:, t % 2, :, :]

            def residual(L, t, m, scale):
                pair = acc(L, t)
                free(stt(x[:, 2 * m:2 * m + 2, :], pair[:, :, 0:T], scale, x[:, 2 * m:2 * m + 2, :], ALU.mult, ALU.add))

            def ffn(L, which, fin, fout):
                u0, t0 = UNITS[fin], TURNS[fin][0]

                def pair_in(i):
                    for j in range(2):
                        split(L, i, u0 + j + 1)
                        if i is FIRST and j == 0:
                            norm_root(L, 3 * which)
                        dve.drain()
                        pair = acc(L, t0 + j, i)
                        scaled(gate_up[:, :, :], pair[:, :, 0:T]).then_inc(gate_scaled, 1)
                        free(dve.drain())
                        dve.wait_ge(silu_ready, L * (2 * KF) + i * 2 + (which * KF + j + 1))
                        tt(gate_up[:, 1, :], gate_up[:, 0, :], gate_up[:, 1, :], ALU.mult)
                        dve.drain()
                        m = i * 2 + j
                        hi, lo = (g[:, m, :] if i is FIRST else g[:, bass.ds(m, 1), :].rearrange("p o t -> p (o t)") for g in (g_hi, g_lo))
                        dve.tensor_copy(hi, gate_up[:, 1, :])
                        dve.drain()
                        tt(lo, gate_up[:, 1, :], hi.bitcast(F32), ALU.subtract).then_inc(g_ready, 1)

                pair_in(FIRST)
                with dve.Fori(1, KF // 2) as i:
                    pair_in(i)
                for m in range(4):
                    for n in range(3 * m + 1, 3 * m + 4):
                        if n < 12 or fout == "f1out":
                            split(L, 0, UNITS[fout] + n)
                        if fout == "f1out" and m > 0 and n == 3 * m + 1:
                            norm_in(L, 1, m - 1)
                    residual(L, TURNS[fout][m], m, 0.5)
                if fout == "f1out":
                    norm_in(L, 1, 3)

            dve.sem_inc(acc_free, 2)
            dve.sem_inc(lo_ready, 4)
            dve.sem_inc(mixer_idle, 1)
            for n in range(10):
                if n == 6:
                    dve.wait_ge(mem_sq, 1)
                    dve.reciprocal(sm(3, 2), sm(3, 2))
                    dve.drain()
                    for c in range(2):
                        dve.tensor_scalar(rows_in[:, 0, c, :], rows_in[:, 0, c, :], sm(3 + c), None, ALU.mult).then_inc(mem_norm, 1)
                dve.wait_ge(start_turned, n + 1)
                bank = M[:, n % 4, :]
                if n == 4:
                    ins = dve.tensor_copy(x[:, :, SEQ:T], bank[:, 0:KD * TS].rearrange("p (k t) -> p k t", k=KD))
                elif n == 5:
                    ins = dve.tensor_copy(prm_all[:, :, :], bank[:, 0:2 * N_PROWS].rearrange("p (l r) -> p l r", l=2))
                else:
                    k = 2 * (n % 6)
                    dst = mem_t[:, k:k + 2, :] if n >= 6 else x[:, k:k + 2, 0:SEQ]
                    ins = dve.tensor_copy(dst, bank.rearrange("p (k t) -> p k t", k=2))
                ins.then_inc(start_taken, 1)
            dve.drain()

            with dve.Fori(0, DEPTH) as L:
                dve.tensor_copy(prm[:, :], prm_all[:, bass.ds(L, 1), :].rearrange("p o r -> p (o r)")).then_inc(prm_ready, 1)
                dve.drain()
                split(L, 0, 0)
                for m in range(4):
                    norm_in(L, 0, m)
                ffn(L, 0, "f1in", "f1out")

                dve.memset(pxt[:, :, 0:PBUF], 0.0)
                dve.memset(cxt[:, :, 0:CBUF], 0.0)

                def pool_new(c):
                    return pxt[:, c, PBUF + SEQ:].rearrange("p (b r) -> p b r", b=SAMPLES)

                pair = acc(L, TURNS["state_in"][0])
                for c in range(2):
                    for half in range(2):
                        dve.tensor_copy(conv_new(c)[:, 4 * half:4 * half + 4, 0:CBUF],
                                        pair[:, 0, 240 * c + 120 * half:240 * c + 120 * half + 120].rearrange("p (b r) -> p b r", b=4))
                    last = dve.tensor_copy(pool_new(c)[:, :, 0:PBUF], pair[:, 1, 120 * c:120 * c + 120].rearrange("p (b r) -> p b r", b=SAMPLES))
                free(last)
                def taps(j0, j1):
                    for j in range(j0, j1):
                        w = PROWS["conv_dw_w"][0] + 2 * j
                        for c in range(2):
                            out, src = conv_acc[:, c, 0:SEQ], cxt[:, c, j:j + SEQ]
                            if j == 0:
                                dve.tensor_scalar(out, src, prm[:, w + c:w + c + 1], par("conv_dw_b", c), ALU.mult, ALU.add)
                            else:
                                stt(out, src, prm[:, w + c:w + c + 1], out, ALU.mult, ALU.add)
                        dve.drain()

                def win(n, j0=0, j1=0):
                    split(L, 0, UNITS["win"] + n + 1)
                    if n == 0:
                        norm_root(L, 1)
                    dve.drain()
                    taps(j0, j1)
                    if n == 8:
                        dve.wait_ge(acc_free, passed(L, 0, TURNS["win"][n] - 1))
                    return acc(L, TURNS["win"][n])

                free(scaled(conv_a[:, :, :], win(0)[:, :, 0:T]))
                free(scaled(conv_gate[:, :, :], win(1)[:, :, 0:T]))
                dve.drain()
                dve.sem_inc(gate_in, 1)
                free(scaled(z[:, 0:2, :], win(2)[:, :, 0:T]))
                dve.wait_ge(gate_ready, L + 1)
                tt(cxt[:, :, CBUF:CBUF + SEQ], conv_a[:, :, 0:SEQ], conv_gate[:, :, 0:SEQ], ALU.mult)
                tt(fresh[:, 2:4, :], conv_a[:, :, SEQ:T], conv_gate[:, :, SEQ:T], ALU.mult)
                dve.drain()
                for c in range(2):
                    last = dve.tensor_copy(conv_new(c)[:, :, CBUF:], fresh[:, 2 + c, :].rearrange("p (b t) -> p b t", b=SAMPLES))
                last.then_inc(fresh_ready, 1)
                for n in range(3, 6):
                    free(scaled(z[:, 2 * n - 4:2 * n - 2, :], win(n, 3 * n - 9, 3 * n - 6)[:, :, 0:T]))
                taps(9, 12)
                dve.wait_ge(rq_ready, L * 2 + 1)
                acc(L, TURNS["qk_stat"][0])
                dve.reciprocal(qk_rms[0:KD, :], qk_rms[0:KD, :]).then_inc(r_ready, 1)
                free(dve.drain())
                pair = win(6)
                tt(pxt[:, :, PBUF:PBUF + SEQ], pair[:, :, 0:SEQ], ap(norm_r, 0, [[0, 2], [1, SEQ]]), ALU.mult)
                free(tt(fresh[:, 0:2, :], pair[:, :, SEQ:T], ap(norm_r, SEQ, [[0, 2], [1, TS]]), ALU.mult))
                dve.drain()
                for c in range(2):
                    dve.tensor_copy(pool_new(c)[:, :, PBUF:], fresh[:, c, :].rearrange("p (b t) -> p b t", b=SAMPLES))
                dve.drain()
                dve.sem_inc(pool_in, 1)
                for j in range(4):
                    pair = acc(L, TURNS["qk_root"][j])
                    stt(z[:, 2 * j:2 * j + 2, :], z[:, 2 * j:2 * j + 2, :], par("att_q_norm" if j < 2 else "att_k_norm"), pair[:, :, 0:T],
                        ALU.mult, ALU.mult).then_inc(z_normed, 1)
                    free(dve.drain())
                    if j < 3:
                        taps(12 + j, 13 + j)
                free(scaled(v_t[:, 0:2, :], win(7, 15, 19)[:, :, 0:T]))
                for place, j in enumerate(ROPE_ORDER):
                    if place == 2:
                        dve.wait_ge(acc_free, passed(L, 0, TURNS["att_k"][0]))
                        dve.sem_inc(dve_passed, 1)
                    pair = acc(L, TURNS["rope"][place])
                    turned = z[0:ROPE_DIM, 2 * j:2 * j + 2, :]
                    cos2 = ap(const, COLS["cos"][0], [[0, 2], [1, T]], ROPE_DIM)
                    sin2 = ap(const, COLS["sin"][0], [[0, 2], [1, T]], ROPE_DIM)
                    free(tt(rope_tmp[0:ROPE_DIM, :, :], pair[0:ROPE_DIM, :, 0:T], sin2, ALU.mult))
                    tt(turned, turned, cos2, ALU.mult)
                    dve.drain()
                    tt(turned, turned, rope_tmp[0:ROPE_DIM, :, :], ALU.add).then_inc(z_done, 1)
                    dve.drain()
                spread_q(dve, att=True)
                for j in range(2):
                    if j == 1:
                        dve.wait_ge(acc_free, passed(L, 0, TURNS["att_k"][1]))
                        dve.sem_inc(dve_passed, 1)
                    pair = acc(L, TURNS["att_s"][j])
                    blocks = pair.rearrange("p e (n c) -> p e n c", n=2)[:, :, :, 0:P]
                    causal4 = ap(const, COLS["causal"][0], [[0, 2], [0, 2], [1, P]])
                    out = ap(probs, 2 * j * 384, [[384, 2], [256, 2], [1, P]])
                    tt(out, blocks, causal4, ALU.add)
                    free(dve.tensor_copy(probs[:, 2 * j:2 * j + 2, P:2 * P], pair[:, :, P:2 * P]))
                dve.drain()
                peak = small[:, 72:80].rearrange("p (h c) -> p h c", c=2)
                dve.tensor_reduce(peak[:, :, 0], probs[:, :, 0:P], AX.X, ALU.max, negate=True)
                dve.tensor_reduce(peak[:, :, 1], probs[:, :, P:384], AX.X, ALU.max, negate=True)
                dve.drain()
                dve.tensor_scalar(sm(16, 8), sm(72, 8), DH ** -0.5, None, ALU.mult).then_inc(p_bias, 2)

                taps(19, 27)
                free(scaled(v_t[:, 2:4, :], win(8)[:, :, 0:T]))
                normalise_probs(dve, L, p_exp, L * 16 + 8, probs, (slice(0, P), slice(P, 384)), p_probs)
                dve.wait_ge(acc_free, passed(L, 0, TURNS["att_k"][5]))
                dve.sem_inc(dve_passed, 1)
                for j in range(2):
                    pair = acc(L, TURNS["att_pt"][j])
                    free(dve.tensor_copy(probs_t[:, 2 * j:2 * j + 2, :], pair[:, :, 0:384]))
                taps(27, CONV_K)
                dve.sem_inc(conv_done, 1)

                dve.wait_ge(news_done, L + 1)
                dve.wait_ge(score_done, L * (2 * SAMPLES) + SAMPLES)
                dve.tensor_copy(sprobs[:, 0:PAST], M[:, SCORES, 0:PAST])
                tt(sprobs[:, PAST:], M[:, NEWS, 0:TS], cc("own"), ALU.add)
                dve.drain()
                dve.tensor_reduce(sm(64), sprobs[:, :], AX.X, ALU.max, negate=True)
                dve.drain()
                dve.tensor_scalar(sm(5), sm(64), DH ** -0.5, None, ALU.mult).then_inc(s_bias, 1)
                dve.wait_ge(acc_free, passed(L, 0, TURNS["att_k"][SAMPLES - 1]))
                dve.sem_inc(dve_passed, 1)
                for c in range(3):
                    n = P if c < 2 else TS
                    pair = acc(L, TURNS["tok"][c])
                    dve.tensor_copy(k_tok[0:n, c, :], pair[0:n, 0, :])
                    last = dve.tensor_copy(v_tok[0:n, c, :], pair[0:n, 1, :])
                    free(last)
                    if c == 0:
                        dve.wait_ge(s_exp, L * 2 + 1)
                        dve.reciprocal(sm(7), sm(6))
                        dve.drain()
                        dve.tensor_scalar(sprobs[:, :], sprobs[:, :], sm(7), None, ALU.mult).then_inc(s_probs, 1)

                dve.wait_ge(ln_sum, L + 1)
                for c in range(2):
                    last = stt(conv_acc[:, c, :], M[:, STAT, 0:T], -1.0 / CONV_W, conv_acc[:, c, :], ALU.mult, ALU.add)
                last.then_inc(ln_centred, 1)
                dve.wait_ge(s_turned, L * 2 + 1)
                spread_p(dve)
                dve.tensor_copy(new_probs_t[0:TS, :], M[0:TS, SCORES, PAST:PAST + ROWS]).then_inc(s_probs_t, 1)
                pair = acc(L, TURNS["pool"][0])
                dve.wait_ge(y_rounded, L * 4 + 2)
                for c in range(2):
                    last = stt(y_lo[:, c, :], pair[:, c, 0:T], par("pool_scale", c), y_hi[:, c, :].bitcast(F32), ALU.mult, ALU.subtract
                               ).then_inc(y_ready, 1)
                free(dve.drain())
                pair = acc(L, TURNS["state_out"][0])
                dve.tensor_copy(sstate[0:TS, :], pair[0:TS, 0, :])
                dve.tensor_copy(pstate[0:PBUF, 0, :], pair[0:PBUF, 1, 0:256])
                free(dve.tensor_copy(pstate[0:CBUF, 1, :], pair[0:CBUF, 1, 256:512]))
                dve.wait_ge(ln_root, L + 1)
                dve.reciprocal(norm_r[:, :], norm_r[:, :])
                dve.drain()
                for c in range(2):
                    last = stt(conv_acc[:, c, :], conv_acc[:, c, :], par("conv_ln_g", c), norm_r[:, :], ALU.mult, ALU.mult)
                last.then_inc(ln_out, 1)
                for j in range(2):
                    pair = acc(L, TURNS["att_o"][j])
                    s = slice(4 + 2 * j, 6 + 2 * j)
                    dve.tensor_copy(y_hi[:, s, 0:SEQ], pair[:, :, 0:SEQ])
                    dve.drain()
                    free(tt(y_lo[:, s, 0:SEQ], pair[:, :, 0:SEQ], y_hi[:, s, 0:SEQ].bitcast(F32), ALU.subtract))
                pair = acc(L, TURNS["pw"][0])
                dve.wait_ge(y_rounded, L * 4 + 4)
                for c in range(2):
                    stt(y_lo[:, 2 + c, :], pair[:, c, 0:T], par("conv_pw_b", c), y_hi[:, 2 + c, :].bitcast(F32), ALU.add, ALU.subtract
                        ).then_inc(y_ready, 1)
                free(dve.drain())
                dve.wait_ge(v_used, L * 16 + 8)
                dve.tensor_copy(att_out_rows[:, :], M[:, OUTS, :]).then_inc(s_rows_out, 1)
                acc(L, TURNS["att_so"][0])
                new = bass.AP(tensor=G, offset=(TURNS["att_so"][0] % 2) * 1024, ap=[[2048, P], [P + NEW, HEADS], [HEADS * NEW, SAMPLES], [1, NEW]])
                hi, lo = (y[:, 4:8, SEQ:T].rearrange("p k (b t) -> p k b t", b=SAMPLES) for y in (y_hi, y_lo))
                dve.tensor_copy(hi, new)
                dve.drain()
                tt(lo, new, hi.bitcast(F32), ALU.subtract).then_inc(y_ready, 1)
                free(dve.drain())
                for n in range(4):
                    split(L, 0, UNITS["wout"] + n + 1)
                    if n > 0:
                        norm_in(L, 2, n - 1)
                    residual(L, TURNS["wout"][n], n, 1.0)
                norm_in(L, 2, 3)

                for n in range(4):
                    split(L, 0, UNITS["cq"] + n + 1)
                    if n == 0:
                        norm_root(L, 2)
                    for k in (range(0, 2), range(2, 5), range(5, 8), ())[n]:
                        dve.wait_ge(m_rounded, L * 8 + k + 1)
                        stt(y_lo[:, k, 0:N_MEM], mem_t[:, k, :], par("ln_mem", k), y_hi[:, k, 0:N_MEM].bitcast(F32), ALU.mult, ALU.subtract
                            ).then_inc(m_ready, 1)
                    pair = acc(L, TURNS["cq"][n])
                    if n == 0:
                        dve.wait_ge(tiles_free, 2 * L + 1)
                    free(scaled(z[:, 2 * n:2 * n + 2, :], pair[:, :, 0:T]))
                def ckv_out(n):
                    pair = acc(L, TURNS["ckv"][n])
                    if n < HEADS:
                        dve.wait_ge(mk_sq, L * 8 + 2 * n + 2)
                        free(dve.tensor_copy(mk[:, :, n * MDH:(n + 1) * MDH], pair[:, :, 0:MDH]))
                    else:
                        free(dve.tensor_copy(mv[:, :, (n - HEADS) * MDH:(n - HEADS + 1) * MDH], pair[:, :, 0:MDH]))

                for n in range(4):
                    split(L, 0, UNITS["ckv"] + n + 1)
                    ckv_out(n)
                    if n == 0:
                        dve.wait_ge(rq_ready, L * 2 + 2)
                        acc(L, TURNS["cq_stat"][0])
                        dve.reciprocal(cq_rms[0:KD, :], cq_rms[0:KD, :]).then_inc(r_ready, 1)
                        free(dve.drain())
                    for b in (2 * n, 2 * n + 1):
                        if b == 1:
                            for j in range(2):
                                pair = acc(L, TURNS["cq_root"][j])
                                for e in range(2):
                                    for d in range(2):
                                        k = 4 * j + 2 * e + d
                                        last = stt(z[:, k, :], z[:, k, :], par("cq_norm", d), pair[:, e, 0:T], ALU.mult, ALU.mult)
                                free(last)
                            dve.drain()
                            dve.sem_inc(z_done, 1)
                            spread_q(dve, att=False)
                        for half in range(2):
                            pair = acc(L, TURNS["mem_k"][2 * b + half])
                            if b >= 2 and half == 0:
                                dve.wait_ge(score_done, L * 16 + SAMPLES + b - 1)
                            dve.wait_ge(kt_half, L * 16 + 2 * b + half + 1)
                            free(dve.tensor_copy(mem_kt[:, b % 2, 4 * half + 2:4 * half + 4, :].rearrange("p h c -> p (h c)"), pair[:, 1, :]))
                split(L, 0, UNITS["ckv"] + 5)
                dve.wait_ge(mk_root, L + 1)
                dve.reciprocal(sm(56, 8), sm(40, 8))
                dve.drain()
                for c in range(2):
                    for h in range(HEADS):
                        s = slice(h * MDH, (h + 1) * MDH)
                        stt(mk[:, c, s], mk[:, c, s], sm(56 + 4 * c + h), ck_gain[:, :], ALU.mult, ALU.mult).then_inc(mk_ready, 1)
                ckv_out(4)
                dve.wait_ge(score_done, L * 16 + 2 * SAMPLES)
                dve.tensor_reduce(sm(64), M[:, SCORES, 0:N_MEM], AX.X, ALU.max, negate=True)
                dve.drain()
                dve.tensor_scalar(sm(5), sm(64), MDH ** -0.5, None, ALU.mult).then_inc(s_bias, 1)
                dve.wait_ge(s_exp, L * 2 + 2)
                dve.reciprocal(sm(7), sm(6))
                dve.drain()
                dve.tensor_scalar(cx_sprobs[:, :], cx_sprobs[:, :], sm(7), None, ALU.mult).then_inc(s_probs, 1)
                split(L, 0, UNITS["ckv"] + 6)
                ckv_out(5)
                for j in range(2):
                    pair = acc(L, TURNS["mkt"][j])
                    free(dve.tensor_copy(mkt[:, 4 * j:4 * j + 4, :].rearrange("p (e k) t -> p e k t", e=2),
                                         pair.rearrange("p e (k t) -> p e k t", k=2)))
                dve.wait_ge(s_turned, L * 2 + 2)
                spread_p(dve).then_inc(s_probs_t, 1)
                split(L, 0, UNITS["ckv"] + 7)
                ckv_out(6)
                for j in range(2):
                    pair = acc(L, TURNS["cx_s"][j])
                    dve.tensor_reduce(small[:, 72 + 4 * j:76 + 4 * j].rearrange("p (e c) -> p e c", e=2),
                                      pair.rearrange("p e (c t) -> p e c t", c=2), AX.X, ALU.max, negate=True)
                    dve.drain()
                    dve.tensor_scalar(sm(16 + 4 * j, 4), sm(72 + 4 * j, 4), MDH ** -0.5, None, ALU.mult).then_inc(cx_bias, 1)
                for j in range(2):
                    dve.wait_ge(p_exp, L * 16 + 8 + 4 * j + 4)
                    free(dve.reciprocal(sm(48 + 4 * j, 4), sm(24 + 4 * j, 4)))
                dve.drain()
                for h in range(HEADS):
                    for c in range(2):
                        s = slice(256 * c, 256 * c + 256)
                        dve.tensor_scalar(cx_probs[:, h, s], cx_probs[:, h, s], sm(48 + 2 * h + c), None, ALU.mult).then_inc(p_probs, 1)
                split(L, 0, UNITS["co"])
                ckv_out(7)
                for j in range(2):
                    pair = acc(L, TURNS["cx_pt"][j])
                    free(dve.tensor_copy(cx_probs_t[:, 2 * j:2 * j + 2, :], pair))
                for j in range(2):
                    pair = acc(L, TURNS["cx_o"][j]).rearrange("p e (k t) -> p e k t", k=2)
                    hi = y_hi[:, 4 * j:4 * j + 4, 0:SEQ].rearrange("p (e k) t -> p e k t", e=2)
                    lo = y_lo[:, 4 * j:4 * j + 4, 0:SEQ].rearrange("p (e k) t -> p e k t", e=2)
                    dve.wait_ge(cx_hi, L * 2 + j + 1)
                    free(tt(lo, pair, hi.bitcast(F32), ALU.subtract))
                acc(L, TURNS["cx_so"][0])
                parts = []
                for h in range(HEADS):
                    at_h = (TURNS["cx_so"][0] % 2) * 1024 + 2 * h * P + h * NEW
                    new = bass.AP(tensor=G, offset=at_h, ap=[[2048, P], [P, 2], [HEADS * NEW, SAMPLES], [1, NEW]])
                    hi, lo = (y[:, 2 * h:2 * h + 2, SEQ:T].rearrange("p k (b t) -> p k b t", b=SAMPLES) for y in (y_hi, y_lo))
                    dve.tensor_copy(hi, new)
                    parts.append((new, hi, lo))
                dve.drain()
                for new, hi, lo in parts:
                    last = tt(lo, new, hi.bitcast(F32), ALU.subtract)
                last.then_inc(y_ready, 1)
                free(dve.drain())
                for n in range(4):
                    split(L, 0, UNITS["co"] + n + 1)
                    if n > 0:
                        norm_in(L, 3, n - 1)
                    residual(L, TURNS["co"][n], n, 1.0)
                norm_in(L, 3, 3)
                dve.sem_inc(mixer_idle, 1)
                dve.wait_ge(tiles_free, 2 * L + 2)
                ffn(L, 1, "f2in", "f2out")

            for c in range(3):
                n = P if c < 2 else TS
                dve.wait_ge(start_turned, 10 + c + 1)
                dve.tensor_copy(y_rows[0:n, c, :].rearrange("p (b d) -> p b d", b=2), M[0:n, 2 * (c % 2):2 * (c % 2) + 2, :]
                                ).then_inc(rows_ready, 1)

        @block.tensor
        def _(pe):
            def mm(out, lhsT, rhs, start=True, stop=True, **kw):
                return pe.matmul(out, lhsT, rhs, start=start, stop=stop, **kw)

            def take(L, t, i=0):
                pe.wait_ge(acc_free, turn_value(L, i, t))
                return G[:, t % 2, :, :]

            def unit(L, i, u, pair, rhs, first=True, last=True, nk=8, k0=0, tokens=T, wait=None):
                for k in range(nk):
                    if k % (nk // 2) == 0:
                        pe.wait_ge(lo_ready, half_value(L, i, u, k // (nk // 2)) + 4)
                    if wait is not None:
                        wait(k0 + k)
                    r_hi, r_lo = rhs(k0 + k)
                    for m in range(2):
                        s = slice((2 * k + m) * P, (2 * k + m + 1) * P)
                        out = pair[:, m, 0:tokens]
                        mm(out, w_hi[:, u % 2, s], r_hi, first and k == 0, False)
                        mm(out, w_hi[:, u % 2, s], r_lo, False, False)
                        ins = mm(out, w_lo[:, u % 2, s], r_hi, False, last and k == nk - 1)
                return ins.then_inc(acc_ready if last else unit_used, 1)

            def norm(L, n):
                pe.wait_ge(sq_summed, L * 4 + n + 1)
                for k in range(2):
                    ins = mm(M[:, STAT, 0:T], ones[:, :], x_squares[:, k, :], k == 0, k == 1)
                ins.then_inc(stat_ready, 1)

            def h(k):
                return h_hi[:, k, :], h_lo[:, k, :]

            def h_wait(L, n):
                return lambda k: pe.wait_ge(h_ready, L * 32 + 8 * n + k + 1)

            def ffn(L, which, n, fin, fout):
                def pair_in(i):
                    for j in range(2):
                        pair = take(L, TURNS[fin][j], i)
                        unit(L, i, UNITS[fin] + j, pair, h, wait=h_wait(L, n))
                        if i is FIRST and j == 0:
                            norm(L, n)

                pair_in(FIRST)
                with pe.Fori(1, KF // 2) as i:
                    pair_in(i)
                for m in range(4):
                    pair = take(L, TURNS[fout][m])
                    for q, nk in enumerate(OUT_PARTS):
                        unit(L, 0, UNITS[fout] + 3 * m + q, pair, lambda k: (g_hi[:, k, :], g_lo[:, k, :]),
                                   q == 0, q == 2, nk, 8 * q,
                                   wait=(lambda k: pe.wait_ge(g_ready, L * (2 * KF) + which * KF + k + 1)) if m == 0 else None)

            def turn(out, in_, n=P):
                return pe.transpose(out, in_, ident[0:n, 0:n])

            pe.sem_inc(acc_ready, 2)
            pe.wait_ge(const_landed, 16)
            pe.wait_ge(x_landed, 32)
            for n in range(10):
                if n >= 4:
                    pe.wait_ge(start_taken, n - 3)
                if n == 4:
                    for k in range(KD):
                        ins = turn(M[:, n % 4, k * TS:(k + 1) * TS], x_sample_rows[:, k * P:(k + 1) * P], TS)
                elif n == 5:
                    pe.wait_ge(rows_landed, 16 * len(PARAMS_BY_POOL))
                    pe.wait_ge(act_rows_landed, 16 * len(PARAMS_BY_ACT))
                    for layer in range(DEPTH):
                        ins = turn(M[:, n % 4, layer * N_PROWS:(layer + 1) * N_PROWS], param_rows[0:N_PROWS, layer, :], N_PROWS)
                else:
                    if n == 6:
                        pe.wait_ge(mem_norm, 2)
                    for e in range(2):
                        k = 2 * (n % 6) + e
                        for c in range(2):
                            ins = turn(M[:, n % 4, 256 * e + P * c:256 * e + P * c + P], rows_in[:, 0 if n >= 6 else 1, c, k * P:(k + 1) * P])
                ins.then_inc(start_turned, 1)
            pe.wait_ge(fills_done, 5)
            pe.wait_ge(start_taken, 10)

            with pe.Fori(0, DEPTH) as L:
                ffn(L, 0, 0, "f1in", "f1out")
                pair = take(L, TURNS["state_in"][0])
                pe.wait_ge(states_in, L * 32 + 32)
                for c in range(2):
                    for half in range(2):
                        turn(pair[:, 0, 240 * c + 120 * half:240 * c + 120 * half + 120], conv_rows[0:120, half, c * P:(c + 1) * P], 120)
                    ins = turn(pair[:, 1, 120 * c:120 * c + 120], pool_rows[0:120, c * P:(c + 1) * P], 120)
                ins.then_inc(acc_ready, 1)
                def win(n):
                    pair = take(L, TURNS["win"][n])
                    unit(L, 0, UNITS["win"] + n, pair, h, wait=h_wait(L, 1))
                    if n == 0:
                        norm(L, 1)

                def rows32(b):
                    return slice(32 * (b // 2), 32 * (b // 2) + 32)

                def att_scores(b):
                    pe.wait_ge(kt_whole, L * SAMPLES + b + 1)
                    for hd in range(HEADS):
                        ins = mm(M[rows32(b), SCORES, 0:PAST], q_diag[:, 0, b * HEADS + hd, :], att_kt[:, b % 2, hd, :],
                                 b % 2 == 0 and hd == 0, b % 2 == 1 and hd == HEADS - 1, skip_group_check=True)
                    ins.then_inc(score_done, 1)

                def att_turned(b):
                    pair = take(L, TURNS["att_k"][b])
                    pe.wait_ge(kv_sem(False, b), kv_value(L, False, b))
                    for hd in range(HEADS):
                        for c in range(PAGES):
                            col = 256 * (hd % 2) + P * c
                            ins = turn(pair[:, hd // 2, col:col + P], att_kv[:, b % 2, c, hd * P:(hd + 1) * P])
                    ins.then_inc(acc_ready, 1)

                def att_keys(b):
                    att_scores(b)
                    att_turned(b + 2)

                for n in range(6):
                    win(n)
                pair = take(L, TURNS["qk_stat"][0])
                for k in range(KD):
                    if k % 2 == 0:
                        pe.wait_ge(zsq_ready, L * 8 + k // 2 + 1)
                    ins = mm(pair[0:KD, 0, 0:T], into_row(k), qk_squares[:, k, :], k == 0, k == KD - 1)
                ins.then_inc(acc_ready, 1)
                win(6)
                pe.wait_ge(r_ready, L * 2 + 1)
                for j in range(4):
                    pair = take(L, TURNS["qk_root"][j])
                    for e in range(2):
                        ins = mm(pair[:, e, 0:T], from_row(2 * j + e), qk_rms[0:KD, :])
                    ins.then_inc(acc_ready, 1)
                win(7)
                for place, j in enumerate(ROPE_ORDER):
                    pair = take(L, TURNS["rope"][place])
                    pe.wait_ge(z_normed, L * 4 + j + 1)
                    for e in range(2):
                        ins = mm(pair[0:ROPE_DIM, e, 0:T], cc("swap"), z[:, 2 * j + e, :])
                    ins.then_inc(acc_ready, 1)
                    if place == 1:
                        att_turned(0)
                for j in range(2):
                    if j == 1:
                        att_turned(1)
                    pair = take(L, TURNS["att_s"][j])
                    pe.wait_ge(z_done, L * 5 + 2 * j + 2)
                    for e in range(2):
                        hd = 2 * j + e
                        mm(pair[:, e, 0:P], z[:, hd, 0:P], z[:, HEADS + hd, 0:P])
                        ins = mm(pair[:, e, P:384], z[:, hd, P:SEQ], z[:, HEADS + hd, 0:SEQ])
                    ins.then_inc(acc_ready, 1)
                pe.wait_ge(q_diag_ready, L * 2 + 1)
                att_keys(0)
                att_keys(1)
                win(8)
                att_keys(2)
                att_keys(3)
                for j in range(2):
                    pair = take(L, TURNS["att_pt"][j])
                    pe.wait_ge(p_probs, L * 16 + 4 * j + 4)
                    for e in range(2):
                        hd = 2 * j + e
                        turn(pair[:, e, 0:P], probs[:, hd, 0:P])
                        turn(pair[:, e, P:2 * P], probs[:, hd, P:2 * P])
                        ins = turn(pair[:, e, 2 * P:3 * P], probs[:, hd, 2 * P:3 * P])
                    ins.then_inc(acc_ready, 1)
                att_keys(4)
                att_keys(5)
                for b in range(SAMPLES):
                    for hd in range(HEADS):
                        ins = mm(M[rows32(b), NEWS, 0:TS], q_diag[:, 0, b * HEADS + hd, :], z[:, HEADS + hd, SEQ:T],
                                 b % 2 == 0 and hd == 0, b % 2 == 1 and hd == HEADS - 1, skip_group_check=True)
                ins.then_inc(news_done, 1)
                att_scores(SAMPLES - 2)
                att_scores(SAMPLES - 1)
                pe.wait_ge(z_done, L * 5 + 4)
                for c in range(3):
                    pair = take(L, TURNS["tok"][c])
                    n = P if c < 2 else TS
                    for hd in range(HEADS):
                        turn(pair[0:n, 0, hd * P:(hd + 1) * P], z[:, HEADS + hd, c * P:c * P + n])
                        ins = turn(pair[0:n, 1, hd * P:(hd + 1) * P], v_t[:, hd, c * P:c * P + n])
                    ins.then_inc(acc_ready, 1)
                pe.wait_ge(conv_done, L + 1)
                pe.wait_ge(conv_new_done, L + 1)
                for c in range(2):
                    ins = mm(M[:, STAT, 0:T], ones[:, :], conv_acc[:, c, :], c == 0, c == 1)
                ins.then_inc(ln_sum, 1)
                pe.wait_ge(s_probs, L * 2 + 1)
                for c in range(2):
                    turn(M[:, SCORES, c * P:(c + 1) * P], sprobs[:, c * P:(c + 1) * P])
                turn(M[0:TS, SCORES, 2 * P:3 * P], sprobs[:, 2 * P:]).then_inc(s_turned, 1)
                pair = take(L, TURNS["pool"][0])
                pe.wait_ge(pooled, L + 1)
                pe.wait_ge(mixer_params, L * 96 + 96)
                for c in range(2):
                    d = pool_diff(c)
                    mm(pair[:, c, 0:SEQ], pool_w[:, c, :], d[:, PBUF:PBUF + SEQ])
                    new = d[:, PBUF + SEQ:].rearrange("p (b r) -> p b r", b=SAMPLES)[:, :, PBUF:]
                    ins = mm(pair[:, c, SEQ:T].rearrange("p (b t) -> p b t", b=SAMPLES), pool_w[:, c, :], new)
                ins.then_inc(acc_ready, 1)
                pair = take(L, TURNS["state_out"][0])
                pe.wait_ge(fresh_ready, L + 1)
                for k in range(4):
                    turn(pair[0:TS, 0, k * P:(k + 1) * P], fresh[:, k, :])
                for c in range(2):
                    turn(pair[0:PBUF, 1, c * P:(c + 1) * P], pxt[:, c, SEQ:SEQ + PBUF])
                    ins = turn(pair[0:CBUF, 1, 256 + c * P:256 + (c + 1) * P], cxt[:, c, SEQ:SEQ + CBUF])
                ins.then_inc(acc_ready, 1)
                pe.wait_ge(ln_sq, L + 1)
                for c in range(2):
                    ins = mm(M[:, STAT, 0:T], ones[:, :], conv_sq[:, c, :], c == 0, c == 1)
                ins.then_inc(ln_var, 1)
                pe.wait_ge(s_probs_t, L * 2 + 1)
                mm(M[:, OUTS, :], new_probs_t[0:TS, :], v_tok[0:TS, 2, :], True, False, skip_group_check=True)

                def att_values(b):
                    n = SAMPLES + b
                    tile = att_v2 if b % 4 >= 2 else att_kv
                    pe.wait_ge(kv_sem(False, n), kv_value(L, False, n))
                    for c in range(PAGES):
                        ins = mm(M[rows32(b), OUTS, :], p_diag[:, c, b, :], tile[:, b % 2, c, :], False, b % 2 == 1 and c == PAGES - 1,
                                 skip_group_check=True)
                    ins.then_inc(v_used, 1)

                for b in range(4):
                    att_values(b)
                for j in range(2):
                    pair = take(L, TURNS["att_o"][j])
                    pe.wait_ge(acc_free, passed(L, 0, TURNS["att_pt"][j]))
                    for e in range(2):
                        hd = 2 * j + e
                        s = slice(hd * P, (hd + 1) * P)
                        mm(pair[:, e, 0:P], v_tok[:, 0, s], probs_t[:, hd, 0:P])
                        mm(pair[:, e, P:SEQ], v_tok[:, 0, s], probs_t[:, hd, P:SEQ], True, False)
                        ins = mm(pair[:, e, P:SEQ], v_tok[:, 1, s], probs_t[:, hd, SEQ:384], False, True)
                    ins.then_inc(acc_ready, 1)
                pair = take(L, TURNS["pw"][0])
                pe.wait_ge(conv_silu, L + 1)
                for m in range(2):
                    for k in range(2):
                        ins = mm(pair[:, m, 0:T], pw_w[:, k, m * P:(m + 1) * P], conv_act[:, k, :], k == 0, k == 1)
                ins.then_inc(acc_ready, 1)
                for b in range(4, SAMPLES):
                    att_values(b)
                pair = take(L, TURNS["att_so"][0])
                pe.wait_ge(s_rows_out, L + 1)
                for hd in range(HEADS):
                    ins = turn(pair[:, 0, hd * P:(hd + 1) * P], att_out_rows[:, hd * P:(hd + 1) * P])
                ins.then_inc(acc_ready, 1)
                def y(k):
                    return y_hi[:, k, :], y_lo[:, k, :]

                pe.wait_ge(y_ready, L * 6 + 5)
                for n in range(4):
                    pair = take(L, TURNS["wout"][n])
                    unit(L, 0, UNITS["wout"] + n, pair, y)
                for n in range(4):
                    pair = take(L, TURNS["cq"][n])
                    unit(L, 0, UNITS["cq"] + n, pair, h, wait=h_wait(L, 2))
                    if n == 0:
                        norm(L, 2)
                def ckv(n):
                    u = UNITS["ckv"] + n
                    pair = take(L, TURNS["ckv"][n])
                    for k in range(KD):
                        if k % 4 == 0:
                            pe.wait_ge(lo_ready, half_value(L, 0, u, k // 4) + 4)
                        s = slice(k * 256, (k + 1) * 256)
                        for c in range(2):
                            tok = slice(c * P, (c + 1) * P)
                            out = pair[:, c, 0:256]
                            mm(out, y_hi[:, k, tok], w_hi[:, u % 2, s], k == 0, False)
                            mm(out, y_hi[:, k, tok], w_lo[:, u % 2, s], False, False)
                            ins = mm(out, y_lo[:, k, tok], w_hi[:, u % 2, s], False, k == KD - 1)
                    ins.then_inc(acc_ready, 1)

                def mem_keys(b):
                    pe.wait_ge(kv_sem(True, b), kv_value(L, True, b))
                    for half in range(2):
                        pair = take(L, TURNS["mem_k"][2 * b + half])
                        for q in range(4):
                            for c in range(2):
                                hd = 4 * half + q
                                col = 256 * (q % 2) + P * c
                                ins = turn(pair[:, q // 2, col:col + P], mem_kv[:, b % 2, c, hd * P:(hd + 1) * P])
                        ins.then_inc(acc_ready, 1)

                def mem_scores(b):
                    pe.wait_ge(acc_free, passed(L, 0, TURNS["mem_k"][2 * b + 1]))
                    for hd in range(KD):
                        ins = mm(M[rows32(b), SCORES, 0:N_MEM], q_diag[:, hd % 2, b * HEADS + hd // 2, :], mem_kt[:, b % 2, hd, :],
                                 b % 2 == 0 and hd == 0, b % 2 == 1 and hd == KD - 1, skip_group_check=True)
                    ins.then_inc(score_done, 1)

                def mem_values(b):
                    n = SAMPLES + b
                    tile = mem_v2 if b % 4 >= 2 else mem_kv
                    pe.wait_ge(kv_sem(True, n), kv_value(L, True, n))
                    for half in range(2):
                        for c in range(2):
                            ins = mm(M[rows32(b), OUTS + half, :], p_diag[:, c, b, :], tile[:, b % 2, c, half * 512:(half + 1) * 512],
                                     b % 2 == 0 and c == 0, b % 2 == 1 and c == 1, skip_group_check=True)
                    ins.then_inc(v_used, 1)

                pe.wait_ge(m_ready, L * 8 + 8)
                for n in range(4):
                    ckv(n)
                    if n == 0:
                        pair = take(L, TURNS["cq_stat"][0])
                        for k in range(KD):
                            if k % 2 == 0:
                                pe.wait_ge(zsq_ready, L * 8 + 4 + k // 2 + 1)
                            ins = mm(pair[0:KD, 0, 0:T], into_row(k // 2), squares[:, k, :], k == 0, k == KD - 1)
                        ins.then_inc(acc_ready, 1)
                    for b in (2 * n, 2 * n + 1):
                        if b == 1:
                            pe.wait_ge(r_ready, L * 2 + 2)
                            for j in range(2):
                                pair = take(L, TURNS["cq_root"][j])
                                for e in range(2):
                                    ins = mm(pair[:, e, 0:T], from_row(2 * j + e), cq_rms[0:KD, :])
                                ins.then_inc(acc_ready, 1)
                        mem_keys(b)
                        if b == 1:
                            pe.wait_ge(q_diag_ready, L * 2 + 2)
                        if b > 0:
                            mem_scores(b - 1)
                mem_scores(SAMPLES - 1)
                ckv(4)
                ckv(5)
                pe.wait_ge(mk_ready, L * 8 + 8)
                for j in range(2):
                    pair = take(L, TURNS["mkt"][j])
                    for q in range(4):
                        for c in range(2):
                            hd = 4 * j + q
                            col = 256 * (q % 2) + P * c
                            ins = turn(pair[:, q // 2, col:col + P], mk[:, c, hd * P:(hd + 1) * P])
                    ins.then_inc(acc_ready, 1)
                pe.wait_ge(s_probs, L * 2 + 2)
                for c in range(2):
                    ins = turn(M[:, SCORES, c * P:(c + 1) * P], cx_sprobs[:, c * P:(c + 1) * P])
                ins.then_inc(s_turned, 1)
                ckv(6)
                pe.wait_ge(z_done, L * 5 + 5)
                pe.wait_ge(acc_free, passed(L, 0, TURNS["mkt"][1]))
                for j in range(2):
                    pair = take(L, TURNS["cx_s"][j])
                    for e in range(2):
                        for c in range(2):
                            for d in range(2):
                                hd = 2 * (2 * j + e) + d
                                ins = mm(pair[:, e, 256 * c:256 * c + 256], z[:, hd, c * P:(c + 1) * P], mkt[:, hd, :], d == 0, d == 1)
                    ins.then_inc(acc_ready, 1)
                pe.wait_ge(s_probs_t, L * 2 + 2)
                for b in range(0, 3):
                    mem_values(b)
                ckv(7)
                for b in range(3, 5):
                    mem_values(b)
                for j in range(2):
                    pair = take(L, TURNS["cx_pt"][j])
                    pe.wait_ge(p_probs, L * 16 + 8 + 4 * j + 4)
                    for e in range(2):
                        for c in range(2):
                            for m in range(2):
                                ins = turn(pair[:, e, 256 * m + P * c:256 * m + P * c + P],
                                           cx_probs[:, 2 * j + e, 256 * c + P * m:256 * c + P * m + P])
                    ins.then_inc(acc_ready, 1)
                for j in range(2):
                    if j == 1:
                        for b in range(5, SAMPLES):
                            mem_values(b)
                    pair = take(L, TURNS["cx_o"][j])
                    pe.wait_ge(acc_free, passed(L, 0, TURNS["cx_pt"][j]))
                    for e in range(2):
                        hh = 2 * j + e
                        for d in range(2):
                            s = slice((2 * hh + d) * P, (2 * hh + d + 1) * P)
                            for m in range(2):
                                ins = mm(pair[:, e, 256 * d:256 * d + 256], mv[:, m, s], cx_probs_t[:, hh, 256 * m:256 * m + 256], m == 0, m == 1)
                    ins.then_inc(acc_ready, 1)
                pair = take(L, TURNS["cx_so"][0])
                pe.wait_ge(cx_rows_out, L + 1)
                for k in range(KD):
                    ins = turn(pair[:, k // 4, (k % 4) * P:(k % 4 + 1) * P], cx_out_rows[:, k // 4, (k % 4) * P:(k % 4 + 1) * P])
                ins.then_inc(acc_ready, 1)
                pe.wait_ge(y_ready, L * 6 + 6)
                pe.wait_ge(acc_free, passed(L, 0, TURNS["cx_o"][1]))
                for n in range(4):
                    pair = take(L, TURNS["co"][n])
                    unit(L, 0, UNITS["co"] + n, pair, y)
                ffn(L, 1, 3, "f2in", "f2out")

            pe.wait_ge(acc_free, N_TURNS * DEPTH + 2)
            for c in range(3):
                if c == 2:
                    pe.wait_ge(rows_ready, 1)
                n = P if c < 2 else TS
                for k in range(KD):
                    ins = turn(M[0:n, 2 * (c % 2) + k // 4, (k % 4) * P:(k % 4 + 1) * P], x[:, k, c * P:c * P + n])
                ins.then_inc(start_turned, 1)


_OUTS = {
    "y_prompt": (1, SEQ, D_MODEL), "y_sample": (SAMPLES, NEW, D_MODEL),
    "p_att_k": (DEPTH, 1, SEQ, HEADS, DH), "p_att_v": (DEPTH, 1, SEQ, HEADS, DH),
    "p_mem_k": (DEPTH, 1, N_MEM, HEADS, MDH), "p_mem_v": (DEPTH, 1, N_MEM, HEADS, MDH),
    "p_pool": (DEPTH, 1, PBUF, POOL_W), "p_conv": (DEPTH, 1, CBUF, CONV_W),
    "s_att_k": (DEPTH, SAMPLES, NEW, HEADS, DH), "s_att_v": (DEPTH, SAMPLES, NEW, HEADS, DH),
    "s_pool": (DEPTH, SAMPLES, PBUF, POOL_W), "s_conv": (DEPTH, SAMPLES, CBUF, CONV_W),
}


def kernel(**inputs):
    import numpy as _np
    import concourse.bacc as _bacc
    from concourse import mybir as _mybir
    from concourse.bass_utils import run_bass_kernel_spmd as _run

    nc = _bacc.Bacc("TRN2", target_bir_lowering=False, num_devices=1)
    arrays = {f"in_{name}": _np.ascontiguousarray(a) for name, a in inputs.items()}
    arrays["in_shape_constants"] = shape_constants()
    ins = {key[3:]: nc.dram_tensor(key, a.shape, _mybir.dt.from_np(a.dtype), kind="ExternalInput").ap() for key, a in arrays.items()}
    outs = {name: nc.dram_tensor(f"out_{name}", shape, _mybir.dt.float32, kind="ExternalOutput").ap() for name, shape in _OUTS.items()}
    trunk_kernel(nc, ins, outs)
    r = _run(nc, [arrays], core_ids=[0])
    return tuple(r.results[0][f"out_{name}"] for name in _OUTS)
```
